# Optimizing a Trainium2 kernel written in Bass

```python
import jax
import jax.numpy as jnp
from jax import lax
import numpy as np
import jax, jax.numpy as jnp

D_MODEL = 1024
BATCH = 1
SEQ = 512
DEPTH = 1

HEAD_DIM = 64
N_FOX_HEADS = 8
N_SB_HEADS = 8
FOX_WIDTH = N_FOX_HEADS * HEAD_DIM
SB_WIDTH = N_SB_HEADS * HEAD_DIM
N_GROUPS = 4
EXPERTS_PER_GROUP = 4
N_EXPERTS = N_GROUPS * EXPERTS_PER_GROUP
TOP_K_EXPERTS = 2
D_FF_EXPERT = D_MODEL // 2
Q_BLOCK = 128
RMS_EPS = 1e-6
N_MOD = 6
IN_SPLITS = (
    FOX_WIDTH, 2 * FOX_WIDTH, 3 * FOX_WIDTH,
    3 * FOX_WIDTH + N_FOX_HEADS,
    3 * FOX_WIDTH + N_FOX_HEADS + SB_WIDTH,
    3 * FOX_WIDTH + N_FOX_HEADS + 2 * SB_WIDTH,
    3 * FOX_WIDTH + N_FOX_HEADS + 3 * SB_WIDTH,
    3 * FOX_WIDTH + N_FOX_HEADS + 3 * SB_WIDTH + D_MODEL,
)
N_IN = 3 * FOX_WIDTH + N_FOX_HEADS + 3 * SB_WIDTH + 2 * D_MODEL


def rmsnorm(x, g):
    xf = x.astype(jnp.float32)
    xf = xf * lax.rsqrt(jnp.mean(xf * xf, axis=-1, keepdims=True) + RMS_EPS)
    return xf.astype(x.dtype) * g

def to_heads(t, n_heads):
    b, s, _ = t.shape
    return t.reshape(b, s, n_heads, HEAD_DIM).transpose(0, 2, 1, 3)

def from_heads(t):
    b, h, s, d = t.shape
    return t.transpose(0, 2, 1, 3).reshape(b, s, h * d)

def sweep_query_blocks(block_fn, seq):
    n_blocks = seq // Q_BLOCK
    out = lax.map(block_fn, jnp.arange(n_blocks))
    nb, b, h, qb, d = out.shape
    return out.transpose(1, 2, 0, 3, 4).reshape(b, h, nb * qb, d)

def forgetting_attention(q, k, v, log_f):
    seq = q.shape[2]
    scale = HEAD_DIM ** -0.5
    F = jnp.cumsum(log_f, axis=-1)
    kpos = jnp.arange(seq)

    def block(i):
        start = i * Q_BLOCK
        qs = lax.dynamic_slice_in_dim(q, start, Q_BLOCK, axis=2)
        Fq = lax.dynamic_slice_in_dim(F, start, Q_BLOCK, axis=2)
        logits = jnp.einsum("bhqd,bhkd->bhqk", qs, k).astype(jnp.float32) * scale
        logits = logits + Fq[..., :, None] - F[..., None, :]
        qpos = start + jnp.arange(Q_BLOCK)
        mask = kpos[None, :] <= qpos[:, None]
        logits = jnp.where(mask, logits, -jnp.inf)
        p = jax.nn.softmax(logits, axis=-1)
        return jnp.einsum("bhqk,bhkd->bhqd", p.astype(v.dtype), v)

    return sweep_query_blocks(block, seq)

def stick_breaking_attention(q, k, v):
    seq = q.shape[2]
    scale = HEAD_DIM ** -0.5
    kpos = jnp.arange(seq)

    def block(i):
        start = i * Q_BLOCK
        qs = lax.dynamic_slice_in_dim(q, start, Q_BLOCK, axis=2)
        z = jnp.einsum("bhqd,bhkd->bhqk", qs, k).astype(jnp.float32) * scale
        qpos = start + jnp.arange(Q_BLOCK)
        mask = kpos[None, :] < qpos[:, None]
        log_beta = jax.nn.log_sigmoid(z)
        log_one_minus = jnp.where(mask, jax.nn.log_sigmoid(-z), 0.0)
        suffix = lax.cumsum(log_one_minus, axis=3, reverse=True) - log_one_minus
        A = jnp.where(mask, jnp.exp(log_beta + suffix), 0.0)
        return jnp.einsum("bhqk,bhkd->bhqd", A.astype(v.dtype), v)

    return sweep_query_blocks(block, seq)

def hierarchical_moe(h, rg_w, rg_b, re_w, re_b, w_gate, w_up, w_down):
    b, s, d = h.shape
    hf = h.reshape(b * s, d)
    g_prob = jax.nn.softmax((hf @ rg_w + rg_b).astype(jnp.float32), axis=-1)
    g_top_p, g_idx = lax.top_k(g_prob, 1)
    e_logits = (hf @ re_w + re_b).astype(jnp.float32).reshape(b * s, N_GROUPS, EXPERTS_PER_GROUP)
    e_sel = jnp.take_along_axis(e_logits, g_idx[:, :, None], axis=1)[:, 0, :]
    e_prob = jax.nn.softmax(e_sel, axis=-1)
    e_top_p, e_idx = lax.top_k(e_prob, TOP_K_EXPERTS)
    e_top_p = e_top_p / jnp.sum(e_top_p, axis=-1, keepdims=True)
    within = jnp.sum(jax.nn.one_hot(e_idx, EXPERTS_PER_GROUP, dtype=jnp.float32)
                     * e_top_p[..., None], axis=1)
    combine = (jax.nn.one_hot(g_idx[:, 0], N_GROUPS, dtype=jnp.float32)[:, :, None]
               * within[:, None, :] * g_top_p[:, :, None])
    combine = combine.reshape(b * s, N_EXPERTS).astype(h.dtype)
    out = jnp.zeros_like(hf)
    for e in range(N_EXPERTS):
        act = jax.nn.silu(hf @ w_gate[e]) * (hf @ w_up[e])
        out = out + combine[:, e:e + 1] * (act @ w_down[e])
    return out.reshape(b, s, d)

def first_inputs(seed: int = 0) -> dict:
    key = jax.random.key(seed)
    ks = jax.random.split(key, 20)
    D, L = D_MODEL, DEPTH

    def nrm(k, shape, scale):
        return jax.random.normal(k, shape, jnp.float32) * scale

    return {
        "x": nrm(ks[0], (BATCH, SEQ, D), 1.0),
        "c": nrm(ks[1], (BATCH, D), 1.0),
        "ada_w": nrm(ks[2], (L, D, N_MOD * D), 0.5 * D ** -0.5),
        "ada_b": nrm(ks[3], (L, N_MOD * D), 0.02),
        "norm1_g": 1.0 + nrm(ks[4], (L, D), 0.02),
        "w_in": nrm(ks[5], (L, D, N_IN), D ** -0.5),
        "b_forget": 2.0 + nrm(ks[6], (L, N_FOX_HEADS), 0.1),
        "w_branch_fox": nrm(ks[7], (L, FOX_WIDTH, D), FOX_WIDTH ** -0.5),
        "w_branch_sb": nrm(ks[8], (L, SB_WIDTH, D), SB_WIDTH ** -0.5),
        "w_out": nrm(ks[9], (L, D, D), D ** -0.5),
        "norm2_g": 1.0 + nrm(ks[10], (L, D), 0.02),
        "router_group_w": nrm(ks[11], (L, D, N_GROUPS), D ** -0.5),
        "router_group_b": nrm(ks[12], (L, N_GROUPS), 0.01),
        "router_expert_w": nrm(ks[13], (L, D, N_EXPERTS), D ** -0.5),
        "router_expert_b": nrm(ks[14], (L, N_EXPERTS), 0.01),
        "expert_w_gate": nrm(ks[15], (L, N_EXPERTS, D, D_FF_EXPERT), D ** -0.5),
        "expert_w_up": nrm(ks[16], (L, N_EXPERTS, D, D_FF_EXPERT), D ** -0.5),
        "expert_w_down": nrm(ks[17], (L, N_EXPERTS, D_FF_EXPERT, D), D_FF_EXPERT ** -0.5),
        "final_g": 1.0 + nrm(ks[18], (D,), 0.02),
    }

def first_block(x, c, ada_w, ada_b, norm1_g, w_in, b_forget, w_branch_fox, w_branch_sb, w_out,
              norm2_g, router_group_w, router_group_b, router_expert_w, router_expert_b,
              expert_w_gate, expert_w_up, expert_w_down, final_g):
    c_act = jax.nn.silu(c)
    for l in range(DEPTH):
        mod = c_act @ ada_w[l] + ada_b[l]
        shift1, scale1, gate1, shift2, scale2, gate2 = [m[:, None, :] for m in jnp.split(mod, N_MOD, axis=-1)]

        h = rmsnorm(x, norm1_g[l]) * (1.0 + scale1) + shift1
        proj = h @ w_in[l]
        qa, ka, va, fa, qb, kb, vb, ga, gb = jnp.split(proj, IN_SPLITS, axis=-1)
        log_f = jax.nn.log_sigmoid((fa + b_forget[l]).astype(jnp.float32)).transpose(0, 2, 1)
        o_fox = forgetting_attention(to_heads(qa, N_FOX_HEADS), to_heads(ka, N_FOX_HEADS),
                                     to_heads(va, N_FOX_HEADS), log_f)
        o_sb = stick_breaking_attention(to_heads(qb, N_SB_HEADS), to_heads(kb, N_SB_HEADS),
                                        to_heads(vb, N_SB_HEADS))
        merged = (jax.nn.sigmoid(ga) * (from_heads(o_fox) @ w_branch_fox[l])
                  + jax.nn.sigmoid(gb) * (from_heads(o_sb) @ w_branch_sb[l]))
        x = x + gate1 * (merged @ w_out[l])

        h2 = rmsnorm(x, norm2_g[l]) * (1.0 + scale2) + shift2
        y = hierarchical_moe(h2, router_group_w[l], router_group_b[l], router_expert_w[l],
                             router_expert_b[l], expert_w_gate[l], expert_w_up[l], expert_w_down[l])
        x = x + gate2 * y
    return rmsnorm(x, final_g)


DEPTH_2 = 2

N_A_LAYERS = (DEPTH_2 + 1) // 2
N_C_LAYERS = DEPTH_2 // 2
D_FF = 4 * D_MODEL
EPS = 1e-6
NEG = -1e30

CONV_WIDTH = D_MODEL // 2
CONV_GROUPS = 8
CONV_K = 3
MLA_HEADS = 8
MLA_NOPE = 64
MLA_ROPE = 32
MLA_V = 64
MLA_KV_RANK = 256
MLA_Q_RANK = 3 * MLA_KV_RANK
ROPE_THETA = 10000.0
MLA_Q_BLOCK = 128
A_IN = 3 * CONV_WIDTH + MLA_Q_RANK + MLA_KV_RANK + MLA_ROPE
A_MIX = CONV_WIDTH + MLA_HEADS * MLA_V
NSA_HEADS = 16
NSA_GROUPS = 4
NSA_REP = NSA_HEADS // NSA_GROUPS
NSA_DH = 64
CMP_LEN = 32
CMP_STRIDE = 16
SLC_LEN = 64
N_SEL = 16
WINDOW = 512
NSA_Q_BLOCK = 32
FORCE_BONUS = 1e4
KV_W = NSA_GROUPS * NSA_DH
C_MIX = NSA_HEADS * NSA_DH
C_IN = C_MIX + 6 * KV_W + 3 * NSA_HEADS


def rms_norm(x, g):
    xf = x.astype(jnp.float32)
    y = xf * lax.rsqrt(jnp.mean(xf * xf, axis=-1, keepdims=True) + EPS)
    return (y * g.astype(jnp.float32)).astype(x.dtype)

def alibi_slopes(n):
    return jnp.asarray(2.0 ** (-8.0 * np.arange(1, n + 1) / n), jnp.float32)

def rope(x, pos):
    half = x.shape[-1] // 2
    inv = ROPE_THETA ** (-jnp.arange(half, dtype=jnp.float32) / half)
    ang = pos.astype(jnp.float32)[:, None] * inv[None, :]
    cos, sin = jnp.cos(ang)[:, None, :], jnp.sin(ang)[:, None, :]
    x1 = x[..., :half].astype(jnp.float32)
    x2 = x[..., half:].astype(jnp.float32)
    return jnp.concatenate([x1 * cos - x2 * sin, x2 * cos + x1 * sin], axis=-1).astype(x.dtype)

def short_conv(u, w):
    c = u.shape[-1]
    return lax.conv_general_dilated(u, w[:, None, :].astype(u.dtype), window_strides=(1,),
                                    padding=[(CONV_K - 1, 0)],
                                    dimension_numbers=('NWC', 'WIO', 'NWC'),
                                    feature_group_count=c)

def dense_causal_attention(q, k, v):
    b, s, h, d = q.shape
    nb = s // MLA_Q_BLOCK
    scale = d ** -0.5
    qb = q.reshape(b, nb, MLA_Q_BLOCK, h, d).transpose(1, 0, 2, 3, 4)
    kpos = jnp.arange(s)

    def one(args):
        q_blk, i = args
        t = i * MLA_Q_BLOCK + jnp.arange(MLA_Q_BLOCK)
        sc = jnp.einsum('bqhd,bshd->bhqs', q_blk, k).astype(jnp.float32) * scale
        sc = jnp.where(kpos[None, :] <= t[:, None], sc, NEG)
        p = jax.nn.softmax(sc, axis=-1).astype(v.dtype)
        return jnp.einsum('bhqs,bshd->bqhd', p, v)

    out = lax.map(one, (qb, jnp.arange(nb)))
    return out.transpose(1, 0, 2, 3, 4).reshape(b, s, h, v.shape[-1])

def mixer_a(xn, w_in, conv_w, q_norm, w_q_up, kv_norm, w_kv_up, w_out):
    b, s, _ = xn.shape
    proj = xn @ w_in
    o1 = CONV_WIDTH; o2 = 2 * CONV_WIDTH; o3 = 3 * CONV_WIDTH
    o4 = o3 + MLA_Q_RANK; o5 = o4 + MLA_KV_RANK
    g_b, g_c, hv, c_q, c_kv, k_r = jnp.split(proj, [o1, o2, o3, o4, o5], axis=-1)
    y_conv = g_b * short_conv(g_c * hv, conv_w)
    pos = jnp.arange(s)
    q = (rms_norm(c_q, q_norm) @ w_q_up).reshape(b, s, MLA_HEADS, MLA_NOPE + MLA_ROPE)
    q = jnp.concatenate([q[..., :MLA_NOPE], rope(q[..., MLA_NOPE:], pos)], axis=-1)
    kv = (rms_norm(c_kv, kv_norm) @ w_kv_up).reshape(b, s, MLA_HEADS, MLA_NOPE + MLA_V)
    k_rope = jnp.broadcast_to(rope(k_r[:, :, None, :], pos), (b, s, MLA_HEADS, MLA_ROPE))
    k = jnp.concatenate([kv[..., :MLA_NOPE], k_rope], axis=-1)
    v = kv[..., MLA_NOPE:]
    y_mla = dense_causal_attention(q, k, v).reshape(b, s, MLA_HEADS * MLA_V)
    return jnp.concatenate([y_conv, y_mla], axis=-1) @ w_out

def mixer_c(xn, w_in, pe_k, w1_k, w2_k, pe_v, w1_v, w2_v, w_out):
    b, s, _ = xn.shape
    G, R, Dh, QB = NSA_GROUPS, NSA_REP, NSA_DH, NSA_Q_BLOCK
    proj = xn @ w_in
    q = proj[..., :C_MIX].reshape(b, s, G, R, Dh)
    kvs = jnp.moveaxis(proj[..., C_MIX:C_MIX + 6 * KV_W].reshape(b, s, 6, G, Dh), 2, 0)
    k_c, v_c, k_s, v_s, k_w, v_w = kvs
    gates = jax.nn.sigmoid(proj[..., C_MIX + 6 * KV_W:].astype(jnp.float32))
    gates = gates.reshape(b, s, 3, G, R).astype(xn.dtype)

    n_cmp = (s - CMP_LEN) // CMP_STRIDE + 1
    starts = np.arange(n_cmp) * CMP_STRIDE
    idx = starts[:, None] + np.arange(CMP_LEN)[None, :]

    def compress(z, pe, w1, w2):
        blk = z[:, idx] + pe[:, None, :]
        hdn = jax.nn.gelu(jnp.einsum('bnlgd,lde->bnge', blk, w1))
        return hdn @ w2

    kc = compress(k_c, pe_k, w1_k, w2_k)
    vc = compress(v_c, pe_v, w1_v, w2_v)
    cmp_centre = jnp.asarray(starts + (CMP_LEN - 1) / 2.0, jnp.float32)
    cmp_end = jnp.asarray(starts + CMP_LEN - 1, jnp.int32)

    n_slc = s // SLC_LEN
    n_sel = min(N_SEL, n_slc)
    ss = np.arange(n_slc) * SLC_LEN
    ov = np.clip(np.minimum(starts[:, None] + CMP_LEN, ss[None, :] + SLC_LEN)
                 - np.maximum(starts[:, None], ss[None, :]), 0, None) / CMP_LEN
    ov = jnp.asarray(ov, jnp.float32)
    kb = k_s.reshape(b, n_slc, SLC_LEN, G, Dh).transpose(0, 3, 1, 2, 4)
    vb = v_s.reshape(b, n_slc, SLC_LEN, G, Dh).transpose(0, 3, 1, 2, 4)

    kwp = jnp.pad(k_w, ((0, 0), (WINDOW, 0), (0, 0), (0, 0)))
    vwp = jnp.pad(v_w, ((0, 0), (WINDOW, 0), (0, 0), (0, 0)))

    slopes = alibi_slopes(NSA_HEADS).reshape(G, R)
    scale = Dh ** -0.5
    nb = s // QB
    qb = q.reshape(b, nb, QB, G, R, Dh).transpose(1, 0, 2, 3, 4, 5)
    gb = gates.reshape(b, nb, QB, 3, G, R).transpose(1, 0, 2, 3, 4, 5)
    bi = jnp.arange(b)[:, None, None, None]
    gi = jnp.arange(G)[None, :, None, None]
    jblk = jnp.arange(n_slc)

    def one(args):
        q_blk, g_blk, i = args
        q0 = i * QB
        t = q0 + jnp.arange(QB)
        tf = t.astype(jnp.float32)
        sc = jnp.einsum('bqgrd,bngd->bgrqn', q_blk, kc).astype(jnp.float32) * scale
        sc = sc - slopes[:, :, None, None] * (tf[:, None] - cmp_centre[None, :])
        valid = cmp_end[None, :] <= t[:, None]
        sc = jnp.where(valid, sc, NEG)
        has = jnp.any(valid, axis=-1).astype(jnp.float32)
        p_cmp = jax.nn.softmax(sc, axis=-1) * has[:, None]
        o_cmp = jnp.einsum('bgrqn,bngd->bqgrd', p_cmp.astype(vc.dtype), vc)
        imp = jnp.einsum('bgrqn,nj->bgqj', p_cmp, ov)
        cur = t // SLC_LEN
        forced = ((jblk[None, :] == 0) | (jblk[None, :] == cur[:, None])
                  | (jblk[None, :] == cur[:, None] - 1)).astype(jnp.float32)
        imp = jnp.where(jblk[None, :] > cur[:, None], NEG, imp + FORCE_BONUS * forced)
        _, sel = lax.top_k(imp, n_sel)
        ks = kb[bi, gi, sel]
        vs = vb[bi, gi, sel]
        kpos = sel[..., None] * SLC_LEN + jnp.arange(SLC_LEN)
        dist = (t[None, None, :, None, None] - kpos).astype(jnp.float32)
        sc = jnp.einsum('bqgrd,bgqnld->bgrqnl', q_blk, ks).astype(jnp.float32) * scale
        sc = sc - slopes[None, :, :, None, None, None] * dist[:, :, None]
        sc = jnp.where((dist >= 0)[:, :, None], sc, NEG)
        p = jax.nn.softmax(sc.reshape(b, G, R, QB, -1), axis=-1).reshape(sc.shape)
        o_slc = jnp.einsum('bgrqnl,bgqnld->bqgrd', p.astype(vs.dtype), vs)
        kw = lax.dynamic_slice_in_dim(kwp, q0, WINDOW + QB, axis=1)
        vw = lax.dynamic_slice_in_dim(vwp, q0, WINDOW + QB, axis=1)
        wpos = q0 - WINDOW + jnp.arange(WINDOW + QB)
        d = t[:, None] - wpos[None, :]
        sc = jnp.einsum('bqgrd,bsgd->bgrqs', q_blk, kw).astype(jnp.float32) * scale
        sc = sc - slopes[:, :, None, None] * d.astype(jnp.float32)
        sc = jnp.where((d >= 0) & (d < WINDOW) & (wpos[None, :] >= 0), sc, NEG)
        p = jax.nn.softmax(sc, axis=-1)
        o_win = jnp.einsum('bgrqs,bsgd->bqgrd', p.astype(vw.dtype), vw)
        return (g_blk[:, :, 0, :, :, None] * o_cmp + g_blk[:, :, 1, :, :, None] * o_slc
                + g_blk[:, :, 2, :, :, None] * o_win)

    out = lax.map(one, (qb, gb, jnp.arange(nb)))
    out = out.transpose(1, 0, 2, 3, 4, 5).reshape(b, s, C_MIX)
    return out @ w_out

def sq_relu_mlp(x, w1, w2):
    h = jax.nn.relu(x @ w1)
    return (h * h) @ w2

def _normal(k, shape, scale):
    return scale * jax.random.normal(k, shape, jnp.float32)

def second_inputs(seed: int = 0) -> dict:
    key = jax.random.key(seed)
    ks = jax.random.split(key, 24)
    nA, nC, D = N_A_LAYERS, N_C_LAYERS, D_MODEL
    gain = lambda k, shape: 1.0 + _normal(k, shape, 0.05)
    return {
        "x": _normal(ks[0], (BATCH, SEQ, D), 1.0),
        "norm_mix_pre": gain(ks[1], (DEPTH_2, D)),
        "norm_mix_post": gain(ks[2], (DEPTH_2, D)),
        "norm_mlp_pre": gain(ks[3], (DEPTH_2, D)),
        "norm_mlp_post": gain(ks[4], (DEPTH_2, D)),
        "mlp_w1": _normal(ks[5], (DEPTH_2, D, D_FF), D ** -0.5),
        "mlp_w2": _normal(ks[6], (DEPTH_2, D_FF, D), D_FF ** -0.5),
        "a_w_in": _normal(ks[7], (nA, D, A_IN), D ** -0.5),
        "a_conv_w": _normal(ks[8], (nA, CONV_K, CONV_WIDTH), CONV_K ** -0.5),
        "a_q_norm": gain(ks[9], (nA, MLA_Q_RANK)),
        "a_w_q_up": _normal(ks[10], (nA, MLA_Q_RANK, MLA_HEADS * (MLA_NOPE + MLA_ROPE)), MLA_Q_RANK ** -0.5),
        "a_kv_norm": gain(ks[11], (nA, MLA_KV_RANK)),
        "a_w_kv_up": _normal(ks[12], (nA, MLA_KV_RANK, MLA_HEADS * (MLA_NOPE + MLA_V)), MLA_KV_RANK ** -0.5),
        "a_w_out": _normal(ks[13], (nA, A_MIX, D), A_MIX ** -0.5),
        "c_w_in": _normal(ks[14], (nC, D, C_IN), D ** -0.5),
        "c_cmp_pe_k": _normal(ks[15], (nC, CMP_LEN, NSA_DH), 0.1),
        "c_cmp_w1_k": _normal(ks[16], (nC, CMP_LEN, NSA_DH, NSA_DH), (CMP_LEN * NSA_DH) ** -0.5),
        "c_cmp_w2_k": _normal(ks[17], (nC, NSA_DH, NSA_DH), NSA_DH ** -0.5),
        "c_cmp_pe_v": _normal(ks[18], (nC, CMP_LEN, NSA_DH), 0.1),
        "c_cmp_w1_v": _normal(ks[19], (nC, CMP_LEN, NSA_DH, NSA_DH), (CMP_LEN * NSA_DH) ** -0.5),
        "c_cmp_w2_v": _normal(ks[20], (nC, NSA_DH, NSA_DH), NSA_DH ** -0.5),
        "c_w_out": _normal(ks[21], (nC, C_MIX, D), C_MIX ** -0.5),
    }

def second_block(x, norm_mix_pre, norm_mix_post, norm_mlp_pre, norm_mlp_post, mlp_w1, mlp_w2,
              a_w_in, a_conv_w, a_q_norm, a_w_q_up, a_kv_norm, a_w_kv_up, a_w_out,
              c_w_in, c_cmp_pe_k, c_cmp_w1_k, c_cmp_w2_k, c_cmp_pe_v, c_cmp_w1_v, c_cmp_w2_v,
              c_w_out):
    for layer in range(DEPTH_2):
        i = layer // 2
        h = rms_norm(x, norm_mix_pre[layer])
        if layer % 2 == 0:
            m = mixer_a(h, a_w_in[i], a_conv_w[i], a_q_norm[i], a_w_q_up[i],
                        a_kv_norm[i], a_w_kv_up[i], a_w_out[i])
        else:
            m = mixer_c(h, c_w_in[i], c_cmp_pe_k[i], c_cmp_w1_k[i], c_cmp_w2_k[i],
                        c_cmp_pe_v[i], c_cmp_w1_v[i], c_cmp_w2_v[i], c_w_out[i])
        x = x + rms_norm(m, norm_mix_post[layer])
        h = rms_norm(x, norm_mlp_pre[layer])
        x = x + rms_norm(sq_relu_mlp(h, mlp_w1[layer], mlp_w2[layer]), norm_mlp_post[layer])
    return x


def setup_inputs(seed=0):
    out = dict(first_inputs(seed))
    for name, value in second_inputs(seed + 1).items():
        if name != "x":
            out[name + "_2"] = value
    return out


def reference(
    x, c, ada_w, ada_b, norm1_g, w_in, b_forget, w_branch_fox, w_branch_sb, w_out, norm2_g,
    router_group_w, router_group_b, router_expert_w, router_expert_b, expert_w_gate,
    expert_w_up, expert_w_down, final_g, norm_mix_pre_2, norm_mix_post_2, norm_mlp_pre_2,
    norm_mlp_post_2, mlp_w1_2, mlp_w2_2, a_w_in_2, a_conv_w_2, a_q_norm_2, a_w_q_up_2,
    a_kv_norm_2, a_w_kv_up_2, a_w_out_2, c_w_in_2, c_cmp_pe_k_2, c_cmp_w1_k_2, c_cmp_w2_k_2,
    c_cmp_pe_v_2, c_cmp_w1_v_2, c_cmp_w2_v_2, c_w_out_2,
):
    x = first_block(
        x, c, ada_w, ada_b, norm1_g, w_in, b_forget, w_branch_fox, w_branch_sb, w_out, norm2_g,
        router_group_w, router_group_b, router_expert_w, router_expert_b, expert_w_gate,
        expert_w_up, expert_w_down, final_g,
    )
    return second_block(
        x, norm_mix_pre_2, norm_mix_post_2, norm_mlp_pre_2, norm_mlp_post_2, mlp_w1_2, mlp_w2_2,
        a_w_in_2, a_conv_w_2, a_q_norm_2, a_w_q_up_2, a_kv_norm_2, a_w_kv_up_2, a_w_out_2,
        c_w_in_2, c_cmp_pe_k_2, c_cmp_w1_k_2, c_cmp_w2_k_2, c_cmp_pe_v_2, c_cmp_w1_v_2,
        c_cmp_w2_v_2, c_w_out_2,
    )


_drawn_inputs = setup_inputs


def setup_inputs(seed=0):
    import zlib

    import numpy as np

    out = dict(_drawn_inputs(seed))
    spreads = {}
    factors = {'norm1_g': 5.952,
     'b_forget': 6.237,
     'norm2_g': 3.916,
     'router_group_b': 7.004,
     'router_expert_b': 8.0,
     'a_q_norm_2': 8.0,
     'a_kv_norm_2': 5.044,
     'c_cmp_pe_k_2': 8.0}
    for name, (base, spread) in spreads.items():
        noise = np.random.default_rng([zlib.crc32(name.encode()), seed]).standard_normal(out[name].shape)
        drawn = base * np.exp(spread * noise) if base else spread * noise
        out[name] = jnp.asarray(drawn.astype(out[name].dtype))
    for name, factor in factors.items():
        out[name] = (out[name] * factor).astype(out[name].dtype)
    return out
```

```python
import numpy as np
import concourse.bass as bass
from concourse import mybir

F32 = mybir.dt.float32
F32R = mybir.dt.float32r
BF16 = mybir.dt.bfloat16
I32 = mybir.dt.int32
ALU = mybir.AluOpType
ACT = mybir.ActivationFunctionType
AX = mybir.AxisListType

P = 128
D = 1024
T = 512
NT = T // P
ND = D // P
W = 512
KK = 4
SLOTS = 4
EPS = 1e-6
BIGNUM = 3.0e38
MASKED = -1.0e30
FAR = 1.0e33
DH = 64
NH1 = 8
EXPERTS, PER_GROUP, GROUPS, DFF = 16, 4, 4, 512
SPARE = (2 * T - EXPERTS) // P
ROWS = (EXPERTS + SPARE) * P
MLA_H, NOPE, ROPE_D = 8, 64, 32
QK_D = NOPE + ROPE_D
Q_RANK, KV_RANK = 768, 256
NSA_H, NSA_G, NSA_R = 16, 4, 4
CMP_LEN, CMP_STRIDE = 32, 16
NCMP = (T - CMP_LEN) // CMP_STRIDE + 1
FF = 4 * D

VECS = [("c", 8), ("norm1_g", 8), ("norm2_g", 8), ("norm_mix_pre_2", 16), ("norm_mlp_pre_2", 16),
        ("a_q_norm_2", 6), ("a_kv_norm_2", 2), ("a_conv_w_2", 12)]
VEC_AT = {}
_n = 0
for _name, _rows in VECS:
    VEC_AT[_name] = _n
    _n += _rows
NVEC = _n

SW_FA, SW_KR, SW_GT, SW_RG, SW_RE, SW_N = 0, 8, 40, 88, 92, 108

CH = {}
_n = 0
for _name, _rows in [("mod", 24), ("qkv", 12), ("gates", 12), ("wout", 4), ("moe", 96), ("ain", 10),
                     ("qup", 3), ("kvup", 1), ("aout", 4), ("up0", 16), ("down0", 16), ("cin", 10),
                     ("cout", 4), ("up1", 16), ("down1", 16)]:
    CH[_name] = _n
    _n += _rows

GR = {}
_n = 2
for _name, _rows in [("mod", 12), ("qkv", 6), ("gates", 8), ("wout", 2), ("ain", 6),
                     ("qup", 2), ("kvup", 2), ("aout", 2), ("up0", 8), ("down0", 2), ("cin", 6),
                     ("cout", 2), ("up1", 8), ("down1", 2)]:
    GR[_name] = _n
    _n += _rows


GU_AT = [0, 4, 10, 16]
DN_AT = [8, 14, 20, 22]
DOWN_AFTER = [[], [0], [1], [2, 3]]

SPLIT = {}
_n = 0
for _name, _chunks in [("qkv", 12), ("gates", 8), ("ain", 10), ("up0", 16), ("down0", 16), ("cin", 10), ("up1", 16),
                       ("down1", 16)]:
    SPLIT[_name] = _n
    _n += 2 * _chunks

FOX0, SB0, MLA0, NSA0 = 0, 32, 64, 96
AHEAD = 4


def constants():
    f = np.float32
    p = np.arange(P)[:, None]
    j = np.arange(T)[None, :] - (T - P)
    ident = np.eye(P, dtype=f)
    caus = np.where(j <= p, 0.0, MASKED).astype(f)
    dist = np.where(j <= p, p - j, FAR).astype(f)
    strict = np.where(np.arange(P)[None, :] < p, 0.0, MASKED).astype(f)
    tok = np.arange(T).reshape(NT, P).T.astype(f)
    starts = np.arange(NCMP) * CMP_STRIDE
    centre = (starts + (CMP_LEN - 1) / 2.0).astype(f)
    end = starts + CMP_LEN - 1
    cd = np.where(end[None, None, :] <= tok[:, :, None], tok[:, :, None] - centre[None, None, :], FAR)
    has = (tok >= end[0]).astype(f)
    inv = (f(10000.0) ** (-np.arange(16, dtype=f) / f(16))).astype(f)
    ang = tok[:, :, None].astype(f) * inv[None, None, :]
    slopes = (2.0 ** (-8.0 * np.arange(1, NSA_H + 1) / NSA_H)).astype(f)
    tri = (np.arange(P)[None, :] > p).astype(f)
    sel = np.zeros((NH1, NH1, P), f)
    for h in range(NH1):
        sel[h, h, :] = 1.0
    first = np.tile(-np.arange(PER_GROUP, dtype=f) + PER_GROUP, (P, 1))
    base = np.tile(np.arange(EXPERTS, dtype=f) * P, (P, 1))
    spare = np.tile(np.arange(8, dtype=f)[:, None], (1, EXPERTS)).reshape(1, 8 * EXPERTS)
    return {
        "k_ident": ident, "k_caus": caus, "k_dist": dist, "k_strict": strict,
        "k_cdist": cd.astype(f).reshape(P, NT * NCMP), "k_has": has,
        "k_cos": np.cos(ang).astype(f).reshape(P, NT * 16), "k_sin": np.sin(ang).astype(f).reshape(P, NT * 16),
        "k_slopes": np.tile(-slopes, (P, 1)), "k_tri": tri, "k_ones": np.ones((P, T), f),
        "k_sel": sel.reshape(NH1, NH1 * P), "k_first": first, "k_base": base, "k_spare": spare,
    }


def program(nc, a, out):

    def sb(name, shape, dt=F32):
        return nc.alloc_sbuf_tensor(name, shape, dt)

    def sem(name):
        return nc.alloc_semaphore(name)

    X = sb("X", [P, NT, D])
    ht_at = nc.sbuf_base
    HT = sb("HT", [P, ND, T])
    HTH = nc.alloc_sbuf_tensor_at("HTH", [P, ND, T], F32R, offset=ht_at)
    HTL = sb("HTL", [P, ND, T], F32R)
    WH = sb("WH", [P, 2, 2, W], F32R)
    WL = sb("WL", [P, 2, 2, W], F32R)
    RING = sb("RING", [P, SLOTS, KK, W])
    BIG = sb("BIG", [P, 16384])
    NAT = sb("NAT", [P, NT, D])
    IDENT = sb("IDENT", [P, P])
    IDB = sb("IDB", [P, P], BF16)
    CMB = sb("CMB", [P, P], BF16)
    SMB = sb("SMB", [P, P], BF16)
    ONES = sb("ONES", [P, T])
    SW = sb("SW", [P, ND, SW_N])
    ROW = sb("ROW", [P, D])
    COLS = sb("COLS", [P, NVEC])
    MCOLS = sb("MCOLS", [P, 48])
    GS = sb("GS", [P, 2, ND])
    COS = sb("COS", [P, NT, 16])
    SIN = sb("SIN", [P, NT, 16])
    SCORE = sb("SCORE", [P, 4, T])
    PT = sb("PT", [P, 2, NT, P])
    QS = sb("QS", [P, 2, T])
    STAT = sb("STAT", [P, 64])

    PB = [nc.alloc_psum_tensor(f"PB{i}", [P, T], F32) for i in range(8)]

    def big(at, *shape):
        n = int(np.prod(shape))
        v = BIG[:, at:at + n]
        if len(shape) == 2:
            v = v.rearrange("p (a b) -> p a b", a=shape[0])
        if len(shape) == 3:
            v = v.rearrange("p (a b c) -> p a b c", a=shape[0], b=shape[1])
        return v

    mod_dram = nc.dram_tensor("mod_scratch", (1, 6 * D), F32).ap()
    disp = nc.dram_tensor("dispatch_rows", (ROWS, D), F32).ap()
    back = nc.dram_tensor("expert_rows", (ROWS, D), F32).ap()

    loaded = sem("loaded")
    arrived = [sem(f"chunk_in_slot{s}") for s in range(SLOTS)]
    chunk_begun = sem("chunk_begun")
    acc_done = sem("acc_done")
    acc_free = [sem(f"acc_free{s}") for s in range(2)]
    met = sem("met")

    dve_chain = sem("dve_chain")
    act_chain = sem("act_chain")
    pool_chain = sem("pool_chain")

    waited = sem("waited")

    def wait_apart(eng, s, value):
        eng.wait_ge(s, value)
        eng.sem_inc(waited, 1)

    def part_no(stage, part, turn=0, per_turn=0):
        return SPLIT[stage] + part + turn * per_turn

    meets = {}

    def meet(eng, key):
        n = meets.setdefault(key, 0) + 1
        meets[key] = n
        eng.drain()
        eng.sem_inc(met, 1)
        eng.wait_ge(met, 4 * n)

    def tall(w, k0, c0, kk=KK, width=W):
        return w[k0 * P:(k0 + kk) * P, c0:c0 + width].rearrange("(t p) n -> p t n", p=P)

    def slot_count(n, turn=0, per_turn=0):
        return 16 * (n // SLOTS + 1) + turn * (16 * per_turn // SLOTS)

    def slot(n, kk=KK, width=W):
        if kk == KK and width == W:
            return RING[:, n % SLOTS]
        return RING[:, n % SLOTS].rearrange("p a b -> p (a b)")[:, 0:kk * width].rearrange("p (a b) -> p a b", a=kk)

    high_ready, low_ready = sem("high_parts_written"), sem("low_parts_written")
    part_begun = sem("part_begun")
    norm_high, norm_low = [sem(f"norm_high{s}") for s in range(2)], sem("norm_low_parts")
    vec_t, cols, cact, mod_io = sem("vectors_transposed"), sem("columns_ready"), sem("c_silu"), sem("mod_moved")
    n_sq, n_ms, n_rms, n_rstd = sem("squares_summed"), sem("mean_squares"), sem("rms_ready"), sem("rstd_ready")
    n_xn, n_tp, n_ht, aux_in = sem("rows_normed"), sem("norm_transposed"), sem("HT_written"), sem("later_loads")
    row_in = sem("gain_row_loaded")
    fg_mm, fg_dve, fg_act = sem("forget_products"), sem("forget_vector"), sem("forget_scalar")
    heads_in, qk, scored, exped = sem("heads_copied"), sem("qk_done"), sem("scored"), sem("exped")
    tp, ev = sem("probs_transposed"), [sem("PT0_written"), sem("PT1_written")]
    pv, normed, recip = sem("pv_done"), sem("normed"), sem("recip_ready")
    sb_abs, sb_exp, sb_ln, sb_sum, sb_scan = (sem(f"sb_{x}") for x in ("abs", "exp", "ln", "sum", "scan"))
    o_tp, o_ht = sem("O_transposed"), sem("OT_written")
    r_mm, r_exp_in, r_exp, r_oh, r_rank, routed = (sem(f"route_{x}") for x in
                                                   ("logits", "exp_in", "exp", "onehot", "rank", "done"))
    zeroed, zero_out, sent = sem("zero_tile"), sem("dispatch_cleared"), sem("rows_dispatched")
    x_tp, x_ht, gu_done, silu_done, act_done, a_tp, a_ht, down_done, y_ev = (
        sem(f"moe_{x}") for x in ("rows_transposed", "rows_T", "gate_up", "silu", "act",
                                  "act_transposed", "act_T", "down", "y_copied"))
    half_merged = sem("half_merged")
    xs_in, y_out = [sem(f"moe_rows_in{m}") for m in range(2)], [sem(f"moe_y_stored{m}") for m in range(2)]
    spare_in, gathered = sem("spare_weights_in"), sem("y_gathered")
    l_sq, l_sum, l_ms, l_rms, l_c, conv_in = (sem(f"latent_{x}") for x in
                                              ("squares", "sums", "ms", "rms", "normed", "conv_input"))
    m_qn, m_kn, m_tp, m_ht = sem("q_roped"), sem("k_roped"), sem("mla_transposed"), sem("mla_T")
    c_in, c_dup, c_mm, c_dve, c_act = (sem(f"cmp_{x}") for x in ("loaded", "duplicated", "products", "vector", "scalar"))
    nsa_bias, stored = sem("nsa_bias_ready"), sem("output_stored")

    ADAB, MODR = BIG[0:1, 0:6 * D], BIG[0:1, 6 * D:12 * D]
    VROWS, MROWS = BIG[0:NVEC, 12 * D:12 * D + P], BIG[0:48, 12 * D + P:12 * D + 2 * P]
    TMPB = BIG[:, 12 * D + 2 * P:12 * D + 3 * P]
    BF = sb("BF", [NH1, 1])
    QA, KA, QB, KB = (big(2048 * i, 4, T) for i in range(4))
    VA, VB, GB = big(8192, NT, 512), big(10240, NT, 512), big(12288, NH1, T)
    OT, MT, SIG = big(0, ND, T), big(4096, ND, T), big(8192, 8, T)
    GBS = NAT[:, 0:2, T:D]
    FY, FA, FN, FG = (NAT[0:NH1, i, 0:T] for i in range(4))
    EXACT = ([SCORE[:, d, :] for d in range(4)] + [QS[:, d, :] for d in range(2)]
             + [PT[:, d, :, :].rearrange("p a b -> p (a b)") for d in range(2)])
    XS = [HT[:, 2 * i:2 * i + 2, :].rearrange("p a b -> p (a b)") for i in range(2)]
    XST = [HT[:, 4 + 2 * i:6 + 2 * i, :].rearrange("p a (b c) -> p (a b) c", b=4) for i in range(2)]
    SG = [NAT[:, 0, i * DFF:(i + 1) * DFF] for i in range(2)]
    ACTT = [NAT[:, 1, i * DFF:(i + 1) * DFF].rearrange("p (a b) -> p a b", a=4) for i in range(2)]
    YN = [NAT[:, 2 + i, :] for i in range(2)]
    SPW = big(0, 6, KK, W)
    YG = big(0, 8, D)
    ZERO = BIG[:, 15360:16384]
    GBT, GCT, HVT, CQ, CKV = big(0, 4, T), big(2048, 4, T), big(4096, 4, T), big(6144, 6, T), big(9216, 2, T)
    YC, QM, KN, KM = GBT, big(2048, MLA_H, T), big(6144, NT, MLA_H, QK_D), big(12288, MLA_H, T)
    KRN, KR2, RT = big(10240, NT, 32), big(10368, NT, 32), big(10496, 3, 512)
    OT2, SQ = big(6144, 4, T), NAT
    QN = NAT[:, :, :].rearrange("p a b -> p (a b)")[:, 0:NT * 768].rearrange("p (a b) -> p a b", a=NT)
    KVN = HT[:, :, :].rearrange("p (a c) b -> p a (c b)", c=2)
    MN = NAT
    CONV = big(12288, 4, T)
    Q2, KG, VG = big(0, ND, T), [big(4096, 4, T), big(6144, 4, T)], [big(8192, NT, 256), big(9216, NT, 256)]
    ZT = [big(10240, 2, T), big(11264, 2, T)]
    CW = [big(12288, CMP_LEN, DH), big(14336, CMP_LEN, DH)]
    KS, BIAS, CBIAS = big(10240, 2, T), big(13312, NSA_R, T), big(12800, NSA_R, NT * NCMP)
    DIST = BIG[:, 12288:12800]
    H1 = big(0, FF // P, T)
    CAUS = BIG[:, 9216:9728]
    flat = SCORE[:, :, :].rearrange("p a b -> p (a b)")
    at = [0]

    def small(*shape, parts=P):
        n = int(np.prod(shape))
        v = flat[0:parts, at[0]:at[0] + n]
        at[0] += n
        if len(shape) == 2:
            v = v.rearrange("p (a b) -> p a b", a=shape[0])
        if len(shape) == 3:
            v = v.rearrange("p (a b c) -> p a b c", a=shape[0], b=shape[1])
        return v

    RL, RBIAS, FIRSTK, BASE, TRI = small(NT, 20), small(20), small(4), small(EXPERTS), small(P)
    RS, OH, RG = small(4, NT, EXPERTS), small(3, NT, EXPERTS), small(12, NT, 4)
    RP = small(NT, EXPERTS)
    SPK = small(8 * EXPERTS, parts=1)
    PER, PET, CW2 = small(2, DH, parts=CMP_LEN), small(2, CMP_LEN, parts=DH), small(2, DH, parts=DH)
    HD = small(2, 4, NCMP, parts=DH)
    BC = small(2, parts=DH)
    IDX = sb("IDX", [P, 2 * NT], I32)
    TAB = sb("TAB", [1, 8], I32)
    MW = sb("MW", [P, 2, NT])
    KC = sb("KC", [P, 4, NCMP])
    KCS = sb("KCS", [P, NCMP])
    VC = sb("VC", [NCMP, 4, DH])
    VCS = sb("VCS", [NCMP, 1, DH])
    CDIST = sb("CDIST", [P, NT * NCMP])
    GATE = sb("GATE", [P, NT, 48])
    SLOPE = sb("SLOPE", [P, NSA_H])
    SLS = sb("SLS", [P, NSA_R])
    HAS = sb("HAS", [P, NT])

    block = nc.Block()
    with block as blk:

        @blk.sync
        def _(sp):
            def load(n, src, kk=KK, width=W, turn=0, per_turn=0):
                if n >= SLOTS:
                    sp.wait_ge(chunk_begun, n - SLOTS + 2 + turn * per_turn)
                sp.dma_start(slot(n, kk, width), src).then_inc(arrived[n % SLOTS], 16)

            def halves(n, w, c0, k0=0, turn=0, per_turn=0):
                load(n, tall(w, k0, c0), turn=turn, per_turn=per_turn)
                load(n + 1, tall(w, k0 + KK, c0), turn=turn, per_turn=per_turn)

            ada = a["ada_w"][0]
            for g in range(4):
                halves(2 * g, ada, g * W)
            with sp.Fori(0, 2) as i:
                for g in range(4):
                    n = 8 + 2 * g
                    for h in range(2):
                        load(n + h, ada[h * KK * P:(h + 1) * KK * P, bass.ds((i + 1) * (4 * W) + g * W, W)]
                             .rearrange("(t p) n -> p t n", p=P), turn=i, per_turn=8)
            w_in = a["w_in"][0]
            for g, c0 in enumerate([0, 512, 1024, 1544, 2056, 2568]):
                halves(CH["qkv"] + 2 * g, w_in, c0)
            for half in range(2):
                n = CH["gates"] + 6 * half
                halves(n, w_in, 3080 + half * W)
                load(n + 2, tall(a["w_branch_fox"][0], 0, half * W))
                halves(n + 3, w_in, 4104 + half * W)
                load(n + 5, tall(a["w_branch_sb"][0], 0, half * W))
            for half in range(2):
                halves(CH["wout"] + 2 * half, a["w_out"][0], half * W)
            with sp.Fori(0, EXPERTS // 4) as i:
                for e in range(4):
                    def expert(w, e, k0, c0):
                        return (w[0, bass.ds(i * 4 + e, 1), k0 * P:(k0 + KK) * P, c0:c0 + W]
                                .rearrange("a (t p) n -> p (a t) n", p=P))
                    for m in range(4):
                        w = a["expert_w_gate"] if m < 2 else a["expert_w_up"]
                        load(CH["moe"] + GU_AT[e] + m, expert(w, e, KK * (m % 2), 0), turn=i, per_turn=24)
                    for d in DOWN_AFTER[e]:
                        for half in range(2):
                            load(CH["moe"] + DN_AT[d] + half, expert(a["expert_w_down"], d, 0, half * W),
                                 turn=i, per_turn=24)
            sp.wait_ge(routed, 1)
            n_spare = sp.value_load(TAB[0:1, 7:8], min_val=0, max_val=SPARE)
            with sp.Fori(0, SPARE) as g:
                with sp.If(g < n_spare):
                    e = sp.value_load(TAB[0:1, bass.ds(g, 1)], min_val=0, max_val=EXPERTS - 1)
                    sp.wait_ge(down_done, EXPERTS + g)
                    for m, (w, k0, c0) in enumerate([("expert_w_gate", 0, 0), ("expert_w_gate", KK, 0),
                                                     ("expert_w_up", 0, 0), ("expert_w_up", KK, 0),
                                                     ("expert_w_down", 0, 0), ("expert_w_down", 0, W)]):
                        src = a[w][0, bass.ds(e, 1), k0 * P:(k0 + KK) * P, c0:c0 + W]
                        sp.dma_start(SPW[:, m], src.rearrange("a (t p) n -> p (a t) n", p=P)).then_inc(spare_in, 16)
            aw = a["a_w_in_2"][0]
            for g in range(5):
                halves(CH["ain"] + 2 * g, aw, g * W)
            qup = a["a_w_q_up_2"][0]
            load(CH["qup"], tall(qup, 0, 0))
            load(CH["qup"] + 1, tall(qup, 4, 0, 2), 2)
            load(CH["qup"] + 2, tall(qup, 0, W, 6, 256), 6, 256)
            load(CH["kvup"], tall(a["a_w_kv_up_2"][0], 0, 0, 2, 1024), 2, 1024)
            for half in range(2):
                halves(CH["aout"] + 2 * half, a["a_w_out_2"][0], half * W)

            def mlp(layer):
                w1, w2 = a["mlp_w1_2"][layer], a["mlp_w2_2"][layer]
                with sp.Fori(0, 2) as i:
                    for g in range(4):
                        for h in range(2):
                            load(CH[f"up{layer}"] + 2 * g + h,
                                 w1[h * KK * P:(h + 1) * KK * P, bass.ds(i * (4 * W) + g * W, W)]
                                 .rearrange("(t p) n -> p t n", p=P), turn=i, per_turn=8)
                with sp.Fori(0, 2) as i:
                    for m in range(8):
                        load(CH[f"down{layer}"] + m, w2[m * KK * P:(m + 1) * KK * P, bass.ds(i * W, W)]
                             .rearrange("(t p) n -> p t n", p=P), turn=i, per_turn=8)

            mlp(0)
            cw = a["c_w_in_2"][0]
            for g in range(5):
                halves(CH["cin"] + 2 * g, cw, g * W)
            for half in range(2):
                halves(CH["cout"] + 2 * half, a["c_w_out_2"][0], half * W)
            mlp(1)


        ROW_NO = {name: 16 * (n + 1) for n, name in
                  enumerate(["gate1", "gate2", "final", "post0", "mlppost0", "post1", "mlppost1"])}
        AUX = {"router": 96, "caus": 112, "cmp": 288, "dist": 304}

        def row_on_all(v):
            return v.partition_broadcast(P)

        NORM_LOW = {name: ND * (n + 1) for n, name in enumerate(["qkv", "ain", "up0", "cin", "up1"])}
        NLOADS = 20
        norm_no = {"act": 0, "dve": 0}
        SS, MS, RMS, RSTD = (STAT[:, 8 + 4 * i:12 + 4 * i] for i in range(4))
        CACT = STAT[:, 0:8]
        NM, RSUM = STAT[:, 24:28], STAT[:, 28:32]
        RINV, GSC = STAT[:, 32:36], STAT[:, 36:40]

        ATT = {
            "fox": (FOX0, 4, 2, 1), "sb": (SB0, 4, 2, 1), "mla": (MLA0, 4, 2, 1), "nsa": (NSA0, 4, 4, 3),
        }

        def units(kind):
            _, _, heads, branches = ATT[kind]
            out_, u = [], 0
            for h in range(heads):
                for i in range(NT):
                    for b in range(branches):
                        out_.append((u, h, i, b))
                        u += 1
            return out_

        LAG_T = {"fox": 2, "sb": 3, "mla": 2, "nsa": 2}

        def keys(i, kind, b):
            return NCMP if kind == "nsa" and b == 0 else (i + 1) * P

        def pieces(i, kind, b):
            return [(0, NCMP)] if kind == "nsa" and b == 0 else [(j, P) for j in range(i + 1)]

        def evac_by_scalar(u, i):
            return i in (0, 3)

        def move_probs(eng, copy, kind, n0, it, U, u, i, b):
            eng.wait_ge(tp, n0 + u + 1)
            eng.wait_ge(pv, n0 + u - 1)
            m = pieces(i, kind, b)
            rows = m[0][1]
            src = PB[4 + u % 2][0:rows, 0:len(m) * P]
            copy(PT[0:rows, u % 2, 0:len(m), :], src.rearrange("p (a b) -> p a b", b=P)).then_inc(ev[u % 2], 1)

        def splitter(split, stage, chunks, turn=0, parts_a_turn=0, chunks_a_turn=0):
            done = [0]

            def upto(n):
                while done[0] < min(n, 2 * len(chunks)):
                    q = done[0]
                    split(stage, q, chunks[q // 2], turn, parts_a_turn, chunks_a_turn)
                    done[0] += 1
            return upto

        def chunk_list(stage, count):
            return [CH[stage] + m for m in range(count)]

        GATE_CHUNKS = [CH["gates"] + m for m in (0, 1, 3, 4, 6, 7, 9, 10)]

        def halves_of(n, q):
            return slot(n)[:, 2 * (q % 2):2 * (q % 2) + 2, :]

        def h1_part(q):
            return H1[:, 2 * (q % 16):2 * (q % 16) + 2, :]

        @blk.scalar
        def _(act):
            chain = [0]

            def link(ins):
                ins.then_inc(act_chain, 1)
                chain[0] += 1
                act.wait_ge(act_chain, chain[0])

            nfirst = [0]

            def first(dst, src):
                act.dma_start(dst, src).then_inc(loaded, 16)
                nfirst[0] += 1

            def later(dst, src):
                act.dma_start(dst, src).then_inc(aux_in, 16)

            def gain_row(src):
                act.dma_start(ROW[:, :], src).then_inc(row_in, 16)

            act.sem_inc(exped, AHEAD)
            act.sem_inc(y_ev, 1)
            for name, rows in VECS:
                src = a[name]
                if len(src.shape) == 3:
                    src = src.rearrange("a b c -> (a b) c")
                first(VROWS[VEC_AT[name]:VEC_AT[name] + rows, :], src.rearrange("a (r p) -> (a r) p", p=P))
            first(ADAB, a["ada_b"])
            first(IDENT[:, :], a["k_ident"])
            first(TMPB, a["k_strict"])
            first(X[:, :, :], a["x"][0].rearrange("(i p) d -> p i d", p=P))
            first(SW[:, :, SW_FA:SW_FA + 8], a["w_in"][0][:, 1536:1544].rearrange("(t p) n -> p t n", p=P))
            first(SW[:, :, SW_KR:SW_KR + 32], a["a_w_in_2"][0][:, 2560:2592].rearrange("(t p) n -> p t n", p=P))
            first(SW[:, :, SW_GT:SW_GT + 48], a["c_w_in_2"][0][:, 2560:2608].rearrange("(t p) n -> p t n", p=P))
            first(SW[:, :, SW_RG:SW_RG + 4], a["router_group_w"][0].rearrange("(t p) n -> p t n", p=P))
            first(SW[:, :, SW_RE:SW_RE + 16], a["router_expert_w"][0].rearrange("(t p) n -> p t n", p=P))
            first(BIG[:, 12 * D + 3 * P:12 * D + 4 * P], a["k_caus"][:, T - P:T])
            first(COS[:, :, :], a["k_cos"].rearrange("p (a b) -> p a b", a=NT))
            first(SIN[:, :, :], a["k_sin"].rearrange("p (a b) -> p a b", a=NT))
            assert nfirst[0] == NLOADS

            act.wait_ge(cols, 1)
            nc.scalar.activation(CACT, COLS[:, 0:8], ACT.Silu).then_inc(cact, 1)
            for s in range(2):
                act.wait_ge(acc_free[s], GR["qkv"] // 2)
            act.dma_start(mod_dram, MODR).then_inc(mod_io, 16)
            act.dma_start(BF[:, :], a["b_forget"].rearrange("a b -> b a")).then_inc(mod_io, 16)
            act.wait_ge(mod_io, 32)
            act.dma_start(MROWS, mod_dram[0].rearrange("(r p) -> r p", p=P)).then_inc(mod_io, 16)
            gain_row(row_on_all(mod_dram[0, 2 * D:3 * D]))

            def stats(src, squares=NAT):
                k = norm_no["act"]
                norm_no["act"] += 1
                for i in range(NT):
                    nc.scalar.activation(squares[:, i, :], src[:, i, :], ACT.Square, accum_out=SS[:, i:i + 1]).then_inc(n_sq, 1)
                act.wait_ge(n_ms, k + 1)
                nc.scalar.activation(RMS, MS, ACT.Sqrt).then_inc(n_rms, 1)

            tps = [0]

            def affine(gain, shift, split=True):
                for d in range(0, ND, 2):
                    act.wait_ge(n_tp, tps[0] + d + 1)
                    bias = shift[:, d:d + 1] if shift is not None else 0.0
                    if split:
                        nc.scalar.activation(EXACT[d], PB[d][:, :], ACT.Identity, bias=bias, scale=gain[:, d:d + 1])
                        nc.scalar.activation(HTH[:, d, :], PB[d][:, :], ACT.Identity, bias=bias,
                                             scale=gain[:, d:d + 1]).then_inc(norm_high[0], 1)
                        continue
                    nc.scalar.activation(HT[:, d, :], PB[d][:, :], ACT.Identity, bias=bias,
                                         scale=gain[:, d:d + 1]).then_inc(n_ht, 1)
                tps[0] += ND

            def split(stage, q, n, turn, parts_a_turn, chunks_a_turn):
                act.wait_ge(arrived[n % SLOTS], slot_count(n, turn, chunks_a_turn))
                if SPLIT[stage] + q > 1:
                    act.wait_ge(part_begun, part_no(stage, q, turn, parts_a_turn))
                ins = nc.scalar.copy(WH[:, q % 2], halves_of(n, q))
                if stage.startswith("down"):
                    ins = nc.scalar.copy(HTH[:, 2 * (q % 2):2 * (q % 2) + 2, :], h1_part(q))
                ins.then_inc(high_ready, 1)

            def evac(g, dst, func=ACT.Copy, scale=1.0, banks=4, width=T):
                act.wait_ge(acc_done, g + 1)
                for b in range(banks):
                    ins = nc.scalar.activation(dst(b), PB[b][:, 0:width], func, scale=scale)
                ins.then_inc(acc_free[0], 1)

            def attention(kind):
                u0, turns, heads, branches = ATT[kind]
                us = units(kind)
                U, lag = len(us), LAG_T[kind]
                with act.Fori(0, turns) as it:
                    n0 = AHEAD + u0 + it * U
                    for s in range(U + lag):
                        if s < U:
                            u, h, i, b = us[s]
                            nk, sc = keys(i, kind, b), SCORE[:, u % 4, :]
                            if kind == "sb":
                                act.wait_ge(qk, n0 + u + 1)
                                act.wait_ge(tp, n0 + u - 3)
                                nc.scalar.activation(sc[:, 0:nk], PB[u % 4][:, 0:nk], ACT.Abs).then_inc(sb_abs, 1)
                                act.wait_ge(sb_abs, it * U + u + 1)
                                nc.scalar.activation(sc[:, 0:nk], sc[:, 0:nk], ACT.Exp, scale=-1.0).then_inc(sb_exp, 1)
                                act.wait_ge(sb_exp, it * U + u + 1)
                                nc.scalar.activation(sc[:, 0:nk], sc[:, 0:nk], ACT.Ln, bias=1.0).then_inc(sb_ln, 1)
                            else:
                                act.wait_ge(scored, n0 + u + 1)
                                nc.scalar.activation(sc[:, 0:nk], sc[:, 0:nk], ACT.Exp, bias=NM[:, u % 4:u % 4 + 1],
                                                     scale=-1.0, accum_out=RSUM[:, u % 4:u % 4 + 1]).then_inc(exped, 1)
                        if kind == "sb" and 1 <= s <= U:
                            u, h, i, b = us[s - 1]
                            act.wait_ge(scored, n0 + u + 1)
                            sc = SCORE[:, u % 4, 0:keys(i, kind, b)]
                            nc.scalar.activation(sc, sc, ACT.Exp).then_inc(exped, 1)
                        if s >= lag:
                            u, h, i, b = us[s - lag]
                            if evac_by_scalar(u, i):
                                move_probs(act, nc.scalar.copy, kind, n0, it, U, u, i, b)

            def heads_T(base, dst, count):
                for d in range(0, count, 2):
                    act.wait_ge(o_tp, base + d + 1)
                    nc.scalar.copy(dst[:, d, :], PB[d][:, :]).then_inc(o_ht, 1)

            meet(act, "act")
            stats(X)
            affine(GS[:, 0, :], MCOLS[:, 0:8])
            g = GR["qkv"]
            upto = splitter(split, "qkv", chunk_list("qkv", 12))
            upto(6)
            evac(g, lambda b: QA[:, b, :], scale=DH ** -0.5)
            upto(14)
            evac(g + 2, lambda b: VA[:, b, :])
            upto(22)
            evac(g + 4, lambda b: KB[:, b, :])
            upto(24)
            meet(act, "act")
            act.wait_ge(fg_dve, 1)
            link(nc.scalar.activation(FA, FY, ACT.Abs))
            link(nc.scalar.activation(FA, FA, ACT.Exp, scale=-1.0))
            nc.scalar.activation(FA, FA, ACT.Ln, bias=1.0).then_inc(fg_act, 1)
            for h in range(0, NH1, 2):
                act.wait_ge(fg_mm, h + 2)
                nc.scalar.copy(GB[:, h, :], PB[h][:, :])
            meet(act, "act")
            attention("fox")
            meet(act, "act")
            attention("sb")
            meet(act, "act")
            heads_T(0, OT, ND)
            meet(act, "act")
            g = GR["gates"]
            upto = splitter(split, "gates", GATE_CHUNKS)
            for half in range(2):
                for m in range(2):
                    upto(8 * half + 4 * m + 5)
                    act.wait_ge(acc_free[1], (g + 4 * half) // 2)
                    if half:
                        act.wait_ge(half_merged, half)
                    evac(g + 4 * half + 2 * m, lambda b: SIG[:, 4 * m + b, :], ACT.Sigmoid)
            meet(act, "act")
            meet(act, "act")
            later(RBIAS[:, 0:4], row_on_all(a["router_group_b"][0]))
            later(RBIAS[:, 4:20], row_on_all(a["router_expert_b"][0]))
            later(FIRSTK, a["k_first"])
            later(BASE, a["k_base"])
            later(TRI, a["k_tri"])
            later(SPK, a["k_spare"])
            gain_row(row_on_all(mod_dram[0, 5 * D:6 * D]))
            stats(X)
            affine(GS[:, 1, :], MCOLS[:, 24:32], split=False)
            act.wait_ge(r_exp_in, 1)
            nc.scalar.activation(RG[:, 1], RG[:, 0], ACT.Exp)
            nc.scalar.activation(RG[:, 9, :, 0:1], RG[:, 8, :, 0:1], ACT.Exp).then_inc(r_exp, 1)
            meet(act, "act")

            def expert(E, e):
                act.wait_ge(x_tp, AHEAD + E + 1)
                for d in range(4):
                    ins = nc.scalar.activation(XST[e % 2][:, d, :], PB[0][:, d * P:(d + 1) * P], ACT.Identity,
                                               bias=MCOLS[:, 24 + d:25 + d], scale=GS[:, 1, d:d + 1])
                ins.then_inc(x_ht, 1)

            def silu(E, e):
                act.wait_ge(gu_done, E + 1)
                nc.scalar.activation(SG[e % 2], PB[2][:, :], ACT.Silu).then_inc(silu_done, 1)

            def result(E, e, before):
                act.wait_ge(down_done, E + 1)
                act.wait_ge(y_out[e % 2], (before + 1) * 16)
                nc.scalar.copy(YN[e % 2][:, 0:W], PB[5][:, :])
                nc.scalar.copy(YN[e % 2][:, W:D], PB[6][:, :]).then_inc(y_ev, 1)

            with act.Fori(0, EXPERTS // 4) as it:
                for e in range(4):
                    E = it * 4 + e
                    if e == 0:
                        expert(E, e)
                    silu(E, e)
                    if e < 3:
                        expert(E + 1, e + 1)
                    for d in DOWN_AFTER[e]:
                        result(it * 4 + d, d, it * 2 + d // 2)
            n_spare = act.value_load(TAB[0:1, 7:8], min_val=0, max_val=SPARE)
            with act.Fori(0, SPARE) as t:
                with act.If(t < n_spare):
                    E = t + EXPERTS
                    expert(E, 0)
                    silu(E, 0)
                    result(E, 0, t + EXPERTS // 2)
            meet(act, "act")

            meet(act, "act")
            gain_row(row_on_all(a["final_g"]))
            stats(X)
            meet(act, "act")

            stats(X)
            affine(COLS[:, VEC_AT["norm_mix_pre_2"]:VEC_AT["norm_mix_pre_2"] + 8], None)
            g = GR["ain"]
            upto = splitter(split, "ain", chunk_list("ain", 10))
            upto(6)
            evac(g, lambda b: GBT[:, b, :])
            upto(14)
            evac(g + 2, lambda b: HVT[:, b, :])
            upto(20)
            evac(g + 4, lambda b: CQ[:, 4 + b, :] if b < 2 else CKV[:, b - 2, :])
            act.wait_ge(acc_free[0], (g + 4) // 2 + 1)
            act.wait_ge(acc_free[1], (g + 4) // 2)
            nc.scalar.activation(SQ[:, :, :].rearrange("p a (c b) -> p (a c) b", c=2)[:, 0:6, :], CQ, ACT.Square).then_inc(l_sq, 1)
            nc.scalar.activation(SQ[:, :, :].rearrange("p a (c b) -> p (a c) b", c=2)[:, 6:8, :], CKV, ACT.Square).then_inc(l_sq, 1)
            for m in range(2):
                act.wait_ge(l_ms, m + 1)
                nc.scalar.activation(RT[:, m, :], RT[:, m, :], ACT.Sqrt).then_inc(l_rms, 1)
            evac(GR["qup"], lambda b: QN[:, b, 0:W])
            evac(GR["kvup"], lambda b: KVN[:, b, 0:W])
            act.wait_ge(acc_done, GR["kvup"] + 2)
            later(CAUS, a["k_caus"])
            gain_row(row_on_all(a["norm_mix_post_2"][0]))
            for h in range(0, MLA_H, 2):
                act.wait_ge(m_tp, h + 1)
                nc.scalar.mul(QM[0:QK_D, h, :], PB[h][0:QK_D, :], QK_D ** -0.5).then_inc(m_ht, 1)
            for h in range(0, MLA_H, 2):
                act.wait_ge(m_tp, MLA_H + h + 1)
                nc.scalar.copy(KM[0:QK_D, h, :], PB[h][0:QK_D, :]).then_inc(m_ht, 1)
            meet(act, "act")
            attention("mla")
            meet(act, "act")
            heads_T(8, OT2, 4)
            evac(GR["aout"], lambda b: MN[:, b, 0:W])

            def mlp(layer):
                meet(act, "act")
                stats(MN, KVN)
                meet(act, "act")
                gain_row(row_on_all(a["norm_mlp_post_2"][layer]))
                stats(X)
                v = VEC_AT["norm_mlp_pre_2"] + 8 * layer
                affine(COLS[:, v:v + 8], None)
                g = GR[f"up{layer}"]
                with act.Fori(0, 2) as it:
                    upto = splitter(split, f"up{layer}", chunk_list(f"up{layer}", 8), it, 16, 8)
                    for m in (0, 2):
                        upto(4 * m + 6)
                        wait_apart(act, acc_done, g + m + 1 + it * 4)
                        for b in range(4):
                            dst = H1[:, bass.ds(it * 16 + 4 * m + b, 1), :].rearrange("p a b -> p (a b)")
                            ins = nc.scalar.activation(dst, PB[b][:, :], ACT.Relu)
                        ins.then_inc(acc_free[0], 1)
                        wait_apart(act, acc_free[0], g // 2 + m // 2 + 1 + it * 2)
                        dst = H1[:, bass.ds(it * 16 + 4 * m, 4), :]
                        nc.scalar.activation(dst, dst, ACT.Square)
                    upto(16)
                meet(act, "act")
                upto = splitter(split, f"down{layer}", chunk_list(f"down{layer}", 16))
                upto(18)
                evac(GR[f"down{layer}"], lambda b: MN[:, b, 0:W])
                upto(32)
                meet(act, "act")
                stats(MN, KVN)
                meet(act, "act")

            mlp(0)

            stats(X)
            v = VEC_AT["norm_mix_pre_2"] + 8
            gain_row(row_on_all(a["norm_mix_post_2"][1]))
            for m, x in enumerate("kv"):
                later(CW[m][0:DH], a[f"c_cmp_w1_{x}_2"][0].rearrange("l d e -> d l e"))
                later(CW[m][DH:P], a[f"c_cmp_w1_{x}_2"][0].rearrange("l d e -> d l e"))
            later(CDIST[:, :], a["k_cdist"])
            later(SLOPE[:, :], a["k_slopes"])
            later(HAS[:, :], a["k_has"])
            affine(COLS[:, v:v + 8], None)
            g = GR["cin"]
            upto = splitter(split, "cin", chunk_list("cin", 10))
            upto(6)
            act.wait_ge(norm_low, NORM_LOW["cin"])
            for m, x in enumerate("kv"):
                later(PER[:, m, :], a[f"c_cmp_pe_{x}_2"][0])
                later(CW2[:, m, :], a[f"c_cmp_w2_{x}_2"][0])
            evac(g, lambda b: Q2[:, b, :], scale=DH ** -0.5)
            upto(14)
            evac(g + 2, lambda b: ZT[b // 2][:, b % 2, :])
            upto(20)
            act.wait_ge(acc_done, g + 5)
            for j in range(2):
                nc.scalar.copy(KG[1][0:DH, 2 * j, :], PB[j][0:DH, :])
                nc.scalar.copy(KG[1][DH:P, 2 * j + 1, :], PB[j][DH:P, :])
                ins = nc.scalar.copy(VG[1][:, 2 * j:2 * j + 2, :], PB[2 + j][:, :].rearrange("p (a b) -> p a b", a=2))
            ins.then_inc(acc_free[0], 1)
            act.wait_ge(acc_free[0], (g + 4) // 2 + 1)
            act.wait_ge(acc_free[1], (g + 3) // 2 + 1)
            for m in range(2):
                act.dma_start(KG[m][DH:P, 0:4:2, :], KG[m][0:DH, 0:4:2, :]).then_inc(c_dup, 16)
                act.dma_start(KG[m][0:DH, 1:4:2, :], KG[m][DH:P, 1:4:2, :]).then_inc(c_dup, 16)
            act.wait_ge(acc_free[1], (g + 5) // 2 + 1)
            link(nc.scalar.activation(GATE[:, :, :], GATE[:, :, :], ACT.Sigmoid))
            act.wait_ge(c_dve, 2)
            for m in range(2):
                for par in range(2):
                    act.wait_ge(c_mm, 2 + 2 * m + par + 1)
                    nc.scalar.activation(HD[:, m, 2 * par:2 * par + 2, :].rearrange("p a b -> p (a b)"),
                                         PB[2 * m + par][0:DH, 0:2 * NCMP], ACT.Gelu_apprx_tanh,
                                         bias=BC[:, m:m + 1]).then_inc(c_act, 1)
            act.wait_ge(c_dve, 4)
            act.dma_start(KC[DH:P, :, :], KC[0:DH, :, :]).then_inc(c_dup, 16)
            act.wait_ge(c_dup, 80)
            meet(act, "act")
            later(DIST, a["k_dist"])
            meet(act, "act")
            attention("nsa")
            meet(act, "act")
            heads_T(12, OT, ND)
            evac(GR["cout"], lambda b: MN[:, b, 0:W])
            mlp(1)

        @blk.gpsimd
        def _(pool):
            chain = [0]

            def link(ins):
                ins.then_inc(pool_chain, 1)
                chain[0] += 1
                pool.wait_ge(pool_chain, chain[0])

            nc.gpsimd.memset(ZERO, 0.0).then_inc(zeroed, 1)
            pool.wait_ge(zeroed, 1)
            for r in range(ROWS // P):
                pool.dma_start(disp[r * P:(r + 1) * P, :], ZERO).then_inc(zero_out, 16)
            for r in range(EXPERTS, EXPERTS + SPARE):
                s = y_out[r % 2] if r < EXPERTS + 2 else zero_out
                pool.dma_start(back[r * P:(r + 1) * P, :], ZERO).then_inc(s, 16)
            pool.wait_ge(zero_out, 16 * (ROWS // P + SPARE - 2))
            for m in range(2):
                pool.wait_ge(y_out[m], 16)
            meet(pool, "pool")
            highs = [0]

            def low_parts():
                for d in range(ND):
                    pool.wait_ge(norm_high[d % 2], highs[0] + d // 2 + 1)
                    nc.gpsimd.tensor_tensor(HTL[:, d, :], EXACT[d], HTH[:, d, :].bitcast(F32), ALU.subtract).then_inc(norm_low, 1)
                highs[0] += ND // 2

            low_parts()
            meet(pool, "pool")

            def copy_heads(kind, srcs):
                u0, turns, heads, branches = ATT[kind]
                U = len(units(kind))
                with pool.Fori(0, turns) as it:
                    pool.wait_ge(qk, AHEAD + u0 + it * U)
                    pool.wait_ge(scored, AHEAD + u0 + it * U)
                    for dst, src in srcs(it):
                        ins = nc.gpsimd.tensor_copy(dst, src)
                    ins.then_inc(heads_in, 1)

            def one(v, i):
                return v[:, bass.ds(i, 1), :].rearrange("p a b -> p (a b)")

            meet(pool, "pool")
            copy_heads("fox", lambda it: [(GBS, GB[:, bass.ds(it * 2, 2), :]), (QS[:, 0, :], one(QA, it)), (QS[:, 1, :], one(KA, it))])
            meet(pool, "pool")
            copy_heads("sb", lambda it: [(QS[:, 0, :], one(QB, it)), (QS[:, 1, :], one(KB, it))])
            meet(pool, "pool")
            for _ in range(3):
                meet(pool, "pool")
            pool.wait_ge(routed, 1)
            for k in range(2):
                for i in range(NT):
                    pool.indirect_dma_start(disp, bass.IndirectOffsetOnAxis(ap=IDX[:, k * NT + i:k * NT + i + 1], axis=0),
                                            NAT[:, i, :], None).then_inc(sent, 16)
            pool.wait_ge(sent, 16 * 2 * NT)
            meet(pool, "pool")

            def rows_in(E, e, lag, src):
                wait_apart(pool, x_tp, AHEAD + E + 1 - lag)
                pool.dma_start(XS[e % 2], src).then_inc(xs_in[e % 2], 16)

            def rows_out(E, e, dst):
                wait_apart(pool, y_ev, E + 2)
                pool.dma_start(dst, YN[e % 2]).then_inc(y_out[e % 2], 16)

            with pool.Fori(0, EXPERTS // 4) as it:
                for e in range(4):
                    E = it * 4 + e
                    if e == 0:
                        rows_in(E, e, 2, disp[bass.ds(E * P, P), :])
                    if e < 3:
                        rows_in(E + 1, e + 1, 2, disp[bass.ds((E + 1) * P, P), :])
                    for d in DOWN_AFTER[e]:
                        rows_out(it * 4 + d, d, back[bass.ds((it * 4 + d) * P, P), :])
            for m in range(2):
                pool.wait_ge(y_out[m], 16 * (EXPERTS // 2 + 1))
            n_spare = pool.value_load(TAB[0:1, 7:8], min_val=0, max_val=SPARE)
            with pool.Fori(0, SPARE) as t:
                with pool.If(t < n_spare):
                    E = t + EXPERTS
                    rows_in(E, 0, 1, disp[bass.ds(E * P, P), :])
                    rows_out(E, 0, back[bass.ds(E * P, P), :])
                    pool.wait_ge(y_out[0], (t + EXPERTS // 2 + 2) * 16)
            meet(pool, "pool")
            for k in range(2):
                for i in range(NT):
                    pool.indirect_dma_start(YG[:, k * NT + i, :], None, back,
                                            bass.IndirectOffsetOnAxis(ap=IDX[:, k * NT + i:k * NT + i + 1], axis=0)
                                            ).then_inc(gathered, 16)
            for _ in range(2):
                meet(pool, "pool")
            low_parts()
            g = GR["ain"]
            pool.wait_ge(acc_free[0], (g + 2) // 2 + 1)
            pool.wait_ge(acc_free[1], (g + 1) // 2 + 1)
            nc.gpsimd.tensor_tensor(GCT, GCT, HVT, ALU.mult).then_inc(conv_in, 1)
            pool.wait_ge(acc_free[0], GR["kvup"] // 2 + 1)
            pool.wait_ge(acc_free[1], (GR["kvup"] + 1) // 2 + 1)
            pool.wait_ge(m_kn, 1)
            for i in range(NT):
                kv = KVN[:, i, :].rearrange("p (h d) -> p h d", h=MLA_H)
                nc.gpsimd.tensor_copy(KN[:, i, :, 0:NOPE], kv[:, :, 0:NOPE])
                nc.gpsimd.tensor_copy(KN[:, i, :, NOPE:QK_D],
                                      KR2[:, i, :].unsqueeze(1).broadcast_to([P, MLA_H, ROPE_D])).then_inc(m_kn, 1)
            meet(pool, "pool")

            def mla_copy(it):
                return [(QS[0:QK_D, :, :], QM[0:QK_D, bass.ds(it * 2, 2), :])]

            copy_heads("mla", mla_copy)
            meet(pool, "pool")

            def mlp():
                for _ in range(2):
                    meet(pool, "pool")
                low_parts()
                for _ in range(3):
                    meet(pool, "pool")

            mlp()
            low_parts()
            meet(pool, "pool")
            meet(pool, "pool")
            u0, turns, heads, branches = ATT["nsa"]
            U = len(units("nsa"))
            with pool.Fori(0, turns) as it:
                pool.wait_ge(qk, AHEAD + u0 + it * U)
                nc.gpsimd.tensor_copy(QS[:, :, :], Q2[:, bass.ds(it * 2, 2), :])
                nc.gpsimd.tensor_copy(KS[:, 0, :], one(KG[0], it))
                nc.gpsimd.tensor_copy(KS[:, 1, :], one(KG[1], it))
                pool.wait_ge(pv, AHEAD + u0 + it * U)
                nc.gpsimd.tensor_copy(VCS[:, :, :], VC[:, bass.ds(it, 1), :])
                nc.gpsimd.tensor_copy(KCS[:, :], one(KC, it)).then_inc(heads_in, 1)
                pool.wait_ge(scored, AHEAD + u0 + it * U)
                nc.gpsimd.tensor_copy(SLS[:, :], SLOPE[:, bass.ds(it * NSA_R, NSA_R)]).then_inc(nsa_bias, 1)
                wait_apart(pool, nsa_bias, it * 2 + 1)
                for r in range(NSA_R):
                    nc.gpsimd.tensor_scalar(BIAS[:, r, :], DIST, SLS[:, r:r + 1], None, ALU.mult)
                    ins = nc.gpsimd.tensor_scalar(CBIAS[:, r, :], CDIST[:, :], SLS[:, r:r + 1], None, ALU.mult)
                ins.then_inc(nsa_bias, 1)
            meet(pool, "pool")
            mlp()

        @blk.tensor
        def _(pe):

            def begin(ins, n):
                ins.then_inc(chunk_begun, 1)

            def await_chunk(n, turn=0, per_turn=0):
                pe.wait_ge(arrived[n % SLOTS], slot_count(n, turn, per_turn))

            def await_set(g, turn=0, per_turn=0):
                pe.wait_ge(acc_free[g % 2], g // 2 + turn * (per_turn // 2))

            def group(g, c, kind, src, chunks=2, turn=0, groups_a_turn=0, chunks_a_turn=0, k_base=0,
                      k_total=None, opens=True, closes=True):
                if opens:
                    await_set(g, turn, groups_a_turn)
                for m in range(chunks):
                    await_chunk(c + m, turn, chunks_a_turn)
                    w = slot(c + m)
                    for b in range(4):
                        for k in range(KK):
                            kk = k_base + m * KK + k
                            if kind == "T":
                                lhs, rhs = w[:, k, b * P:(b + 1) * P], src[:, kk, :]
                            else:
                                lhs, rhs = src[:, kk, b * P:(b + 1) * P], w[:, k, :]
                            ins = pe.matmul(PB[4 * (g % 2) + b][:, :], lhs, rhs,
                                            start=(opens and m == 0 and k == 0),
                                            stop=(closes and m == chunks - 1 and k == KK - 1))
                            if b == 0 and k == 0:
                                begin(ins, c + m)
                if closes:
                    ins.then_inc(acc_done, 1)

            def three(dst, w, k, x, kk, kind, cols_of_b, start, stop_):
                for n, (wp, xp) in enumerate(((w[0], x[0]), (w[0], x[1]), (w[1], x[0]))):
                    if kind == "T":
                        lhs, rhs = wp[:, k, cols_of_b], xp[:, kk, :]
                    else:
                        lhs, rhs = xp[:, kk, cols_of_b], wp[:, k, :]
                    yield pe.matmul(dst, lhs, rhs, start=(start and n == 0), stop=(stop_ and n == 2))

            def split_group(g, stage, q0, kind, parts=4, turn=0, groups_a_turn=0, parts_a_turn=0, wait_norm=None):
                await_set(g, turn, groups_a_turn)
                for m in range(parts):
                    q = q0 + m
                    pe.wait_ge(low_ready, part_no(stage, q, turn, parts_a_turn) + 1)
                    w = (WH[:, q % 2], WL[:, q % 2])
                    for b in range(4):
                        for k in range(2):
                            kk = 2 * (q % 2) + k if kind == "D" else 2 * m + k
                            if wait_norm is not None and (b == 0 or m == 0 and k == 0):
                                pe.wait_ge(norm_low, wait_norm - ND + max(kk, b) + 1)
                            for n, ins in enumerate(three(PB[4 * (g % 2) + b][:, :], w, k, (HTH, HTL), kk, kind,
                                                          slice(b * P, (b + 1) * P), m == 0 and k == 0,
                                                          m == parts - 1 and k == 1)):
                                if b == 0 and k == 0 and n == 0:
                                    ins.then_inc(part_begun, 1)
                                if b == 0 and k == 0 and n == 1 and q % 2 == 0:
                                    begin(ins, None)
                ins.then_inc(acc_done, 1)

            pe.sem_inc(acc_done, GR["mod"])
            pe.sem_inc(tp, AHEAD)
            pe.sem_inc(qk, AHEAD)
            pe.sem_inc(pv, AHEAD)
            pe.sem_inc(x_tp, AHEAD)

            pe.wait_ge(loaded, 16 * NLOADS)
            pe.transpose(PB[7][:, 0:NVEC], VROWS, IDENT[0:NVEC, 0:NVEC]).then_inc(vec_t, 1)
            pe.wait_ge(cact, 1)
            with pe.Fori(0, 3) as it:
                for g in range(4):
                    await_set(GR["mod"] + g, it, 4)
                    for m in range(2):
                        c = 2 * g + m
                        await_chunk(c, it, 8)
                        for k in range(KK):
                            ins = pe.matmul(PB[4 * (g % 2)][0:1, :], CACT[:, m * KK + k:m * KK + k + 1],
                                            slot(c)[:, k, :], start=(m == 0 and k == 0), stop=(m == 1 and k == KK - 1))
                            if k == 0:
                                begin(ins, c)
                    ins.then_inc(acc_done, 1)
            pe.wait_ge(mod_io, 48)
            pe.transpose(PB[6][:, 0:48], MROWS, IDENT[0:48, 0:48]).then_inc(vec_t, 1)
            meet(pe, "pe")

            rows = [0]

            def rows_to_T():
                for d in range(ND):
                    for i in range(NT):
                        if d == 0:
                            pe.wait_ge(n_xn, rows[0] * NT + i + 1)
                        ins = pe.transpose(PB[d][:, i * P:(i + 1) * P], NAT[:, i, d * P:(d + 1) * P], IDENT[:, :])
                    ins.then_inc(n_tp, 1)
                rows[0] += 1

            def attention(kind, q, k, v, width=DH):
                u0, turns, heads, branches = ATT[kind]
                us = units(kind)
                U, lag = len(us), LAG_T[kind]
                base_turn = {"fox": 0, "sb": 4, "mla": 8, "nsa": 12}[kind]
                with pe.Fori(0, turns) as it:
                    n0 = AHEAD + u0 + it * U
                    pe.wait_ge(heads_in, it + base_turn + 1)
                    for s in range(U + lag + 1):
                        if s < U:
                            u, h, i, b = us[s]
                            nk = keys(i, kind, b)
                            pe.wait_ge(scored, n0 + u - 3)
                            masked = kind in ("fox", "sb")
                            ins = pe.matmul(PB[u % 4][:, 0:nk], q(h, i), k(it, h, b, nk), start=True, stop=not masked)
                            if masked:
                                mask = CMB if kind == "fox" else SMB
                                ins = pe.matmul(PB[u % 4][:, i * P:nk], IDB[:, :], mask[:, :], start=False, stop=True)
                            ins.then_inc(qk, 1)
                        if lag <= s < U + lag:
                            u, h, i, b = us[s - lag]
                            pe.wait_ge(exped, n0 + u + 1)
                            pe.wait_ge(ev[u % 2], (u0 + u) // 2 + it * (U // 2) + AHEAD)
                            for j, n in pieces(i, kind, b):
                                ins = pe.transpose(PB[4 + u % 2][0:n, j * P:(j + 1) * P],
                                                   SCORE[:, u % 4, j * P:j * P + n], IDENT[:, :])
                            ins.then_inc(tp, 1)
                        if s > lag:
                            u, h, i, b = us[s - lag - 1]
                            pe.wait_ge(ev[u % 2], (u0 + u) // 2 + it * (U // 2) + AHEAD + 1)
                            pe.wait_ge(normed, n0 + u - 1)
                            m = pieces(i, kind, b)
                            for j, n in m:
                                ins = pe.matmul(PB[6 + u % 2][:, 0:DH], PT[0:n, u % 2, j, :], v(it, h, b, j, n),
                                                start=(j == 0), stop=(j == len(m) - 1))
                            ins.then_inc(pv, 1)

            def heads_T(count):
                for d in range(count):
                    for i in range(NT):
                        ins = pe.transpose(PB[d][:, i * P:(i + 1) * P], NAT[:, i, d * P:(d + 1) * P], IDENT[:, :])
                    ins.then_inc(o_tp, 1)

            rows_to_T()
            for m, kind in enumerate("TTNTTN"):
                split_group(GR["qkv"] + m, "qkv", 4 * m, kind, wait_norm=NORM_LOW["qkv"] if m == 0 else None)
            meet(pe, "pe")
            for k in range(ND):
                for n, x in enumerate((HTH, HTL)):
                    ins = pe.matmul(PB[0][0:NH1, :], SW[:, k, SW_FA:SW_FA + NH1], x[:, k, :].bitcast(F32),
                                    start=(k == 0 and n == 0), stop=(k == ND - 1 and n == 1))
            ins.then_inc(fg_mm, 1)
            pe.wait_ge(fg_dve, 2)
            for h in range(NH1):
                pe.matmul(PB[h][:, :], IDENT[0:NH1, h:h + 1].broadcast_to([NH1, P]), FG, start=True, stop=True).then_inc(fg_mm, 1)
            meet(pe, "pe")

            def pair(h):
                return slice(h * DH, (h + 1) * DH)

            attention("fox", lambda h, i: QS[pair(h), 0, i * P:(i + 1) * P], lambda it, h, b, nk: QS[pair(h), 1, 0:nk],
                      lambda it, h, b, j, n: VA[:, j, bass.ds((it * 2 + h) * DH, DH)])
            meet(pe, "pe")
            attention("sb", lambda h, i: QS[pair(h), 0, i * P:(i + 1) * P], lambda it, h, b, nk: QS[pair(h), 1, 0:nk],
                      lambda it, h, b, j, n: VB[:, j, bass.ds((it * 2 + h) * DH, DH)])
            meet(pe, "pe")
            heads_T(ND)
            pe.wait_ge(o_ht, ND)
            meet(pe, "pe")
            for half in range(2):
                c, g = CH["gates"] + 6 * half, GR["gates"] + 4 * half
                split_group(g, "gates", 8 * half, "T")
                group(g + 1, c + 2, "T", OT, chunks=1)
                split_group(g + 2, "gates", 8 * half + 4, "T")
                group(g + 3, c + 5, "T", OT, chunks=1, k_base=4)
            meet(pe, "pe")
            for half in range(2):
                group(GR["wout"] + half, CH["wout"] + 2 * half, "N", MT)
            meet(pe, "pe")
            rows_to_T()
            pe.wait_ge(n_ht, ND)
            for i in range(NT):
                for k in range(ND):
                    ins = pe.matmul(PB[0][:, i * 32:i * 32 + 20], HT[:, k, i * P:(i + 1) * P], SW[:, k, SW_RG:SW_N],
                                    start=(k == 0), stop=(k == ND - 1))
            ins.then_inc(r_mm, 1)
            pe.wait_ge(r_oh, 1)
            for i in range(NT):
                for m in range(i + 1):
                    pe.matmul(PB[1][:, i * EXPERTS:(i + 1) * EXPERTS], TRI if m == i else ONES[:, 0:P], OH[:, 2, m, :],
                              start=(m == 0), stop=(m == i))
            for i in range(NT):
                ins = pe.matmul(PB[2][:, 0:EXPERTS], ONES[:, 0:P], OH[:, 2, i, :], start=(i == 0), stop=(i == NT - 1))
            ins.then_inc(r_rank, 1)
            meet(pe, "pe")

            def rows_T(E, e, before):
                pe.wait_ge(xs_in[e % 2], (before + 1) * 16)
                for d in range(ND):
                    ins = pe.transpose(PB[d // 4][:, (d % 4) * P:(d % 4 + 1) * P], XS[e % 2][:, d * P:(d + 1) * P], IDENT[:, :])
                ins.then_inc(x_tp, 1)

            def gate_up(E, e, weights, starts):
                pe.wait_ge(x_ht, (E + 1) * 2)
                pe.wait_ge(act_done, E + 1)
                for m in range(4):
                    w = weights(m)
                    for k in range(KK):
                        ins = pe.matmul(PB[2 + m // 2][:, :], XST[e % 2][:, (m % 2) * KK + k, :], w[:, k, :],
                                        start=(m % 2 == 0 and k == 0), stop=(m % 2 == 1 and k == KK - 1))
                        if k == 0 and starts:
                            begin(ins, None)
                ins.then_inc(gu_done, 1)

            def act_T(E, e):
                pe.wait_ge(act_done, E + 2)
                for d in range(4):
                    ins = pe.transpose(PB[4][:, d * P:(d + 1) * P], SG[e % 2][:, d * P:(d + 1) * P], IDENT[:, :])
                ins.then_inc(a_tp, 1)

            def down(E, e, weights, starts):
                pe.wait_ge(a_ht, E + 1)
                pe.wait_ge(y_ev, E + 1)
                for m in range(2):
                    w = weights(m)
                    for k in range(KK):
                        ins = pe.matmul(PB[5 + m][:, :], ACTT[e % 2][:, k, :], w[:, k, :], start=(k == 0), stop=(k == KK - 1))
                        if k == 0 and starts:
                            begin(ins, None)
                ins.then_inc(down_done, 1)

            with pe.Fori(0, EXPERTS // 4) as it:
                def ring(at):
                    def chunk(m):
                        await_chunk(CH["moe"] + at + m, it, 24)
                        return slot(CH["moe"] + at + m)
                    return chunk
                for e in range(4):
                    if e == 0:
                        rows_T(it * 4, 0, it * 2)
                    gate_up(it * 4 + e, e, ring(GU_AT[e]), True)
                    for n, d in enumerate(DOWN_AFTER[e]):
                        act_T(it * 4 + d, d)
                        if n == 0 and e < 3:
                            rows_T(it * 4 + e + 1, e + 1, it * 2 + (e + 1) // 2)
                        down(it * 4 + d, d, ring(DN_AT[d]), True)
                    if e == 0:
                        rows_T(it * 4 + 1, 1, it * 2)
            n_spare = pe.value_load(TAB[0:1, 7:8], min_val=0, max_val=SPARE)
            with pe.Fori(0, SPARE) as t:
                with pe.If(t < n_spare):
                    E = t + EXPERTS
                    rows_T(E, 0, t + EXPERTS // 2)
                    pe.wait_ge(spare_in, (t + 1) * 96)
                    gate_up(E, 0, lambda m: SPW[:, m], False)
                    act_T(E, 0)
                    down(E, 0, lambda m: SPW[:, 4 + m], False)
            meet(pe, "pe")
            meet(pe, "pe")
            meet(pe, "pe")

            rows_to_T()
            for m in range(5):
                split_group(GR["ain"] + m, "ain", 4 * m, "T", wait_norm=NORM_LOW["ain"] if m == 0 else None)
            g = GR["ain"] + 5
            await_set(g)
            for i in range(NT):
                for k in range(ND):
                    for n, x in enumerate((HTH, HTL)):
                        ins = pe.matmul(PB[4][:, i * 32:(i + 1) * 32], x[:, k, i * P:(i + 1) * P].bitcast(F32),
                                        SW[:, k, SW_KR:SW_KR + 32], start=(k == 0 and n == 0), stop=(k == ND - 1 and n == 1))
            ins.then_inc(acc_done, 1)
            pe.wait_ge(acc_free[0], (g + 1) // 2)
            sq = SQ[:, :, :].rearrange("p a (c b) -> p (a c) b", c=2)
            pe.wait_ge(l_sq, 1)
            for k in range(6):
                ins = pe.matmul(PB[0][:, :], ONES[:, 0:P], sq[:, k, :], start=(k == 0), stop=(k == 5))
            ins.then_inc(l_sum, 1)
            pe.wait_ge(l_sq, 2)
            for k in range(2):
                ins = pe.matmul(PB[1][:, :], ONES[:, 0:P], sq[:, 6 + k, :], start=(k == 0), stop=(k == 1))
            ins.then_inc(l_sum, 1)
            g, c = GR["qup"], CH["qup"]
            await_set(g)
            pe.wait_ge(l_c, 1)
            parts = [(slot(c), 0, 4), (slot(c + 1, 2), 4, 2)]
            for m, (w, k0, kk) in enumerate(parts):
                await_chunk(c + m)
                for b in range(NT):
                    for k in range(kk):
                        ins = pe.matmul(PB[b][:, :], CQ[:, k0 + k, b * P:(b + 1) * P], w[:, k, :],
                                        start=(m == 0 and k == 0), stop=(m == 1 and k == kk - 1))
                        if b == 0 and k == 0:
                            begin(ins, c + m)
            ins.then_inc(acc_done, 1)
            await_set(g + 1)
            await_chunk(c + 2)
            w = slot(c + 2, 6, 256)
            for b in range(NT):
                for k in range(6):
                    ins = pe.matmul(PB[4 + b][:, 0:256], CQ[:, k, b * P:(b + 1) * P], w[:, k, :], start=(k == 0), stop=(k == 5))
                    if b == 0 and k == 0:
                        begin(ins, c + 2)
            ins.then_inc(acc_done, 1)
            g, c = GR["kvup"], CH["kvup"]
            await_chunk(c)
            w = slot(c, 2, 1024)
            for m in range(2):
                await_set(g + m)
                for b in range(NT):
                    for k in range(2):
                        ins = pe.matmul(PB[4 * m + b][:, :], CKV[:, k, b * P:(b + 1) * P], w[:, k, m * W:(m + 1) * W],
                                        start=(k == 0), stop=(k == 1))
                        if m == 0 and b == 0 and k == 0:
                            begin(ins, c)
                ins.then_inc(acc_done, 1)
            for m in range(2):
                pe.wait_ge(m_qn if m == 0 else m_kn, 1 if m == 0 else 1 + NT)
                for h in range(MLA_H):
                    if m == 0 and h in (0, 4):
                        pe.wait_ge(acc_free[h // 4], (GR["kvup"] + h // 4) // 2 + 1)
                    if m == 1:
                        pe.wait_ge(m_ht, MLA_H)
                    for i in range(NT):
                        src = QN[:, i, h * QK_D:(h + 1) * QK_D] if m == 0 else KN[:, i, h, :]
                        ins = pe.transpose(PB[h][0:QK_D, i * P:(i + 1) * P], src, IDENT[:, :])
                    ins.then_inc(m_tp, 1)
            meet(pe, "pe")
            attention("mla", lambda h, i: QS[0:QK_D, h, i * P:(i + 1) * P],
                      lambda it, h, b, nk: KM[0:QK_D, bass.ds(it * 2 + h, 1), 0:nk].rearrange("p a b -> p (a b)"),
                      lambda it, h, b, j, n: KVN[:, j, bass.ds((it * 2 + h) * P + NOPE, DH)])
            meet(pe, "pe")
            heads_T(4)
            pe.wait_ge(o_ht, ND + 4)
            for half in range(2):
                g, c = GR["aout"] + half, CH["aout"] + 2 * half
                group(g, c, "N", YC, chunks=1, closes=False)
                group(g, c + 1, "N", OT2, chunks=1, opens=False)

            def mlp(layer):
                meet(pe, "pe")
                meet(pe, "pe")
                rows_to_T()
                pe.wait_ge(norm_low, NORM_LOW[f"up{layer}"])
                with pe.Fori(0, 2) as it:
                    for m in range(4):
                        split_group(GR[f"up{layer}"] + m, f"up{layer}", 4 * m, "T", turn=it, groups_a_turn=4, parts_a_turn=16)
                meet(pe, "pe")
                for half in range(2):
                    split_group(GR[f"down{layer}"] + half, f"down{layer}", 16 * half, "D", parts=16)
                meet(pe, "pe")
                meet(pe, "pe")

            mlp(0)

            rows_to_T()
            g = GR["cin"]
            for m in range(3):
                split_group(g + m, "cin", 4 * m, "T", wait_norm=NORM_LOW["cin"] if m == 0 else None)
            for m in range(3, 5):
                await_set(g + m)
                bank = 4 * ((g + m) % 2)
                for n in range(4):
                    q = 4 * m + n
                    pe.wait_ge(low_ready, part_no("cin", q) + 1)
                    w = (WH[:, q % 2], WL[:, q % 2])
                    wv = tuple(t[:, :, 256:512] for t in w)
                    for b in range(2 + NT):
                        for k in range(2):
                            kk, ends = 2 * n + k, (n == 0 and k == 0, n == 3 and k == 1)
                            if b < 2:
                                mms = three(PB[bank + b][:, :], w, k, (HTH, HTL), kk, "T", slice(b * P, (b + 1) * P), *ends)
                            else:
                                i = b - 2
                                ends = (ends[0] and i % 2 == 0, ends[1] and i % 2 == 1)
                                mms = three(PB[bank + 2 + i // 2][:, (i % 2) * 256:(i % 2) * 256 + 256], wv, k, (HTH, HTL),
                                            kk, "N", slice(i * P, (i + 1) * P), *ends)
                            for x, ins in enumerate(mms):
                                if b == 0 and k == 0 and x == 0:
                                    ins.then_inc(part_begun, 1)
                                if b == 0 and k == 0 and x == 1 and q % 2 == 0:
                                    begin(ins, None)
                ins.then_inc(acc_done, 1)
            await_set(g + 5)
            bank = 4 * ((g + 5) % 2)
            for i in range(NT):
                for k in range(ND):
                    for n, x in enumerate((HTH, HTL)):
                        ins = pe.matmul(PB[bank][:, i * 48:(i + 1) * 48], x[:, k, i * P:(i + 1) * P].bitcast(F32),
                                        SW[:, k, SW_GT:SW_GT + 48], start=(k == 0 and n == 0), stop=(k == ND - 1 and n == 1))
            ins.then_inc(acc_done, 1)
            pe.wait_ge(aux_in, AUX["cmp"])
            for s in range(2):
                pe.wait_ge(acc_free[s], (g + 4 + s) // 2 + 1)
            for m in range(2):
                ins = pe.transpose(PB[6][0:DH, m * CMP_LEN:(m + 1) * CMP_LEN], PER[:, m, :], IDENT[0:CMP_LEN, 0:CMP_LEN])
            ins.then_inc(c_mm, 1)
            pe.wait_ge(c_dve, 1)
            for m in range(2):
                for l in range(CMP_LEN):
                    ins = pe.matmul(PB[4 + m][0:DH, 0:1], CW[m][0:DH, l, :], PET[:, m, l:l + 1], start=(l == 0), stop=(l == CMP_LEN - 1))
            ins.then_inc(c_mm, 1)
            for m in range(2):
                for par in range(2):
                    half = slice(par * DH, (par + 1) * DH)
                    for l in range(CMP_LEN):
                        z = ZT[m][half, :, l:l + CMP_STRIDE * (NCMP - 1) + 1:CMP_STRIDE]
                        dst = PB[2 * m + par][0:DH, 0:2 * NCMP].rearrange("p (a b) -> p a b", a=2)
                        ins = pe.matmul(dst, CW[m][half, l, :], z, start=(l == 0), stop=(l == CMP_LEN - 1))
                    ins.then_inc(c_mm, 1)
            pe.wait_ge(c_act, 4)
            pe.matmul(PB[7][0:DH, 0:4 * NCMP], CW2[:, 0, :], HD[:, 0, :, :].rearrange("p a b -> p (a b)"),
                      start=True, stop=True).then_inc(c_mm, 1)
            for q in range(4):
                ins = pe.matmul(PB[6][0:NCMP, q * DH:(q + 1) * DH], HD[:, 1, q, :], CW2[:, 1, :], start=True, stop=True)
            ins.then_inc(c_mm, 1)
            meet(pe, "pe")
            meet(pe, "pe")

            def nsa_k(it, h, b, nk):
                r = slice((h % 2) * DH, (h % 2 + 1) * DH)
                return KCS[r, :] if b == 0 else KS[r, b - 1, 0:nk]

            def nsa_v(it, h, b, j, n):
                if b == 0:
                    return VCS[:, 0, :]
                return VG[b - 1][:, j, bass.ds(it * DH, DH)]

            attention("nsa", lambda h, i: QS[(h % 2) * DH:(h % 2 + 1) * DH, h // 2, i * P:(i + 1) * P], nsa_k, nsa_v)
            meet(pe, "pe")
            heads_T(ND)
            pe.wait_ge(o_ht, 2 * ND + 4)
            for half in range(2):
                group(GR["cout"] + half, CH["cout"] + 2 * half, "N", OT)
            mlp(1)

        @blk.vector
        def _(dve):
            chain = [0]

            def link(ins):
                ins.then_inc(dve_chain, 1)
                chain[0] += 1
                dve.wait_ge(dve_chain, chain[0])

            V = nc.vector
            for s in (scored, normed, ev[0], ev[1]):
                dve.sem_inc(s, AHEAD)
            for s in (acc_free[0], acc_free[1], act_done):
                dve.sem_inc(s, 1)
            V.memset(ONES[:, :], 1.0)
            dve.wait_ge(loaded, 16 * NLOADS)
            V.tensor_copy(IDB[:, :], IDENT[:, :])
            V.tensor_copy(SMB[:, :], TMPB)
            V.tensor_copy(CMB[:, :], BIG[:, 12 * D + 3 * P:12 * D + 4 * P])
            dve.wait_ge(vec_t, 1)
            V.tensor_copy(COLS[:, :], PB[7][:, 0:NVEC]).then_inc(cols, 1)
            with dve.Fori(0, 3) as it:
                for g in range(4):
                    dve.wait_ge(acc_done, GR["mod"] + g + 1 + it * 4)
                    at_ = bass.ds(it * (4 * W) + g * W, W)
                    V.tensor_tensor(MODR[:, at_], PB[4 * (g % 2)][0:1, :], ADAB[:, at_], ALU.add).then_inc(acc_free[g % 2], 1)
            dve.wait_ge(vec_t, 2)
            link(V.tensor_copy(MCOLS[:, :], PB[6][:, 0:48]))
            for k in range(2):
                norm = VEC_AT[f"norm{k + 1}_g"]
                V.scalar_tensor_tensor(out=GS[:, k, :], in0=MCOLS[:, 24 * k + 8:24 * k + 16], scalar=1.0,
                                       in1=COLS[:, norm:norm + 8], op0=ALU.add, op1=ALU.mult)
            meet(dve, "dve")

            def stats():
                k = norm_no["dve"]
                norm_no["dve"] += 1
                dve.wait_ge(n_sq, NT * (k + 1))
                V.tensor_scalar(MS, SS, 1.0 / D, EPS, ALU.mult, ALU.add).then_inc(n_ms, 1)
                dve.wait_ge(n_rms, k + 1)
                V.reciprocal(RSTD, RMS).then_inc(n_rstd, 1)
                dve.wait_ge(n_rstd, k + 1)

            tps = [0]

            def split(stage, q, n, turn, parts_a_turn, chunks_a_turn):
                dve.wait_ge(high_ready, part_no(stage, q, turn, parts_a_turn) + 1)
                ins = V.tensor_tensor(WL[:, q % 2], halves_of(n, q), WH[:, q % 2].bitcast(F32), ALU.subtract)
                if stage.startswith("down"):
                    rows = slice(2 * (q % 2), 2 * (q % 2) + 2)
                    ins = V.tensor_tensor(HTL[:, rows, :], h1_part(q), HTH[:, rows, :].bitcast(F32), ALU.subtract)
                ins.then_inc(low_ready, 1)

            def normed_T(gain, shift, split=True):
                stats()
                for i in range(NT):
                    V.tensor_scalar(NAT[:, i, :], X[:, i, :], RSTD[:, i:i + 1], None, ALU.mult).then_inc(n_xn, 1)
                for d in range(1, ND, 2):
                    dve.wait_ge(n_tp, tps[0] + d + 1)
                    for dst in (EXACT[d], HTH[:, d, :]) if split else (HT[:, d, :],):
                        if shift is None:
                            ins = V.tensor_scalar(dst, PB[d][:, :], gain[:, d:d + 1], None, ALU.mult)
                        else:
                            ins = V.tensor_scalar(dst, PB[d][:, :], gain[:, d:d + 1], shift[:, d:d + 1], ALU.mult, ALU.add)
                    ins.then_inc(norm_high[1] if split else n_ht, 1)
                tps[0] += ND

            def evac(g, dst, banks=4, width=T, scale=None):
                dve.wait_ge(acc_done, g + 1)
                for b in range(banks):
                    if scale is None:
                        ins = V.tensor_copy(dst(b), PB[4 + b][:, 0:width])
                    else:
                        ins = V.tensor_scalar(dst(b), PB[4 + b][:, 0:width], scale, None, ALU.mult)
                ins.then_inc(acc_free[1], 1)

            def attention(kind, bias, dst):
                u0, turns, heads, branches = ATT[kind]
                us = units(kind)
                U, lag = len(us), LAG_T[kind]
                with dve.Fori(0, turns) as it:
                    n0 = AHEAD + u0 + it * U
                    if kind == "nsa":
                        dve.wait_ge(nsa_bias, it * 2 + 2)
                    for s in range(U + lag + 1):
                        if s < U:
                            u, h, i, b = us[s]
                            nk, sc, ps = keys(i, kind, b), SCORE[:, u % 4, :], PB[u % 4]
                            if kind == "sb":
                                dve.wait_ge(sb_ln, it * U + u + 1)
                                V.scalar_tensor_tensor(out=sc[:, 0:nk], in0=ps[:, 0:nk], scalar=0.0, in1=sc[:, 0:nk],
                                                       op0=ALU.max, op1=ALU.add).then_inc(sb_sum, 1)
                                dve.wait_ge(sb_sum, it * U + u + 1)
                                rev = SCORE[:, u % 4, 0:nk][:, ::-1]
                                V.tensor_tensor_scan(rev, ONES[:, 0:nk], rev, 0.0, ALU.mult, ALU.add).then_inc(sb_scan, 1)
                                dve.wait_ge(sb_scan, it * U + u + 1)
                                V.tensor_tensor(sc[:, 0:nk], ps[:, 0:nk], sc[:, 0:nk], ALU.subtract).then_inc(scored, 1)
                            else:
                                dve.wait_ge(qk, n0 + u + 1)
                                wait_apart(dve, tp, n0 + u - 3)
                                V.tensor_tensor_reduce(out=sc[:, 0:nk], in0=ps[:, 0:nk], in1=bias(it, h, i, b, nk), scale=-1.0,
                                                       scalar=BIGNUM, op0=ALU.add, op1=ALU.min,
                                                       accum_out=NM[:, u % 4:u % 4 + 1]).then_inc(scored, 1)
                        if lag <= s < U + lag:
                            u, h, i, b = us[s - lag]
                            if not evac_by_scalar(u, i):
                                move_probs(dve, V.tensor_copy, kind, n0, it, U, u, i, b)
                        if s > lag:
                            u, h, i, b = us[s - lag - 1]
                            o = dst(it, h, i)
                            if kind == "sb":
                                dve.wait_ge(pv, n0 + u + 1)
                                V.tensor_copy(o, PB[6 + u % 2][:, 0:DH]).then_inc(normed, 1)
                                continue
                            dve.wait_ge(exped, n0 + u + 1)
                            r = RINV[:, u % 4:u % 4 + 1]
                            V.reciprocal(r, RSUM[:, u % 4:u % 4 + 1]).then_inc(recip, 1)
                            base = (n0 - AHEAD) - (32 if kind != "fox" else 0)
                            mult = 2 if kind == "nsa" else 1
                            if kind == "nsa":
                                first_ = 64 + it * (2 * U) + 2 * u
                                dve.wait_ge(recip, first_ + 1)
                                gate = GATE[:, i, bass.ds(it * NSA_R + (b * NSA_H + h), 1)]
                                s_ = GSC[:, u % 4:u % 4 + 1]
                                V.tensor_tensor(s_, r, gate, ALU.mult).then_inc(recip, 1)
                                dve.wait_ge(recip, first_ + 2)
                                dve.wait_ge(pv, n0 + u + 1)
                                if b == 0:
                                    V.tensor_scalar(o, PB[6 + u % 2][:, 0:DH], s_, None, ALU.mult).then_inc(normed, 1)
                                else:
                                    dve.wait_ge(normed, n0 + u)
                                    V.scalar_tensor_tensor(out=o, in0=PB[6 + u % 2][:, 0:DH], scalar=s_, in1=o,
                                                           op0=ALU.mult, op1=ALU.add).then_inc(normed, 1)
                            else:
                                dve.wait_ge(recip, base + u + 1)
                                dve.wait_ge(pv, n0 + u + 1)
                                V.tensor_scalar(o, PB[6 + u % 2][:, 0:DH], r, None, ALU.mult).then_inc(normed, 1)

            def heads_T(base, dst, count):
                for d in range(1, count, 2):
                    dve.wait_ge(o_tp, base + d + 1)
                    V.tensor_copy(dst[:, d, :], PB[d][:, :]).then_inc(o_ht, 1)

            normed_T(GS[:, 0, :], MCOLS[:, 0:8])
            g = GR["qkv"]
            upto = splitter(split, "qkv", chunk_list("qkv", 12))
            upto(10)
            evac(g + 1, lambda b: KA[:, b, :])
            upto(18)
            evac(g + 3, lambda b: QB[:, b, :], scale=DH ** -0.5)
            upto(24)
            evac(g + 5, lambda b: VB[:, b, :])
            meet(dve, "dve")
            dve.wait_ge(fg_mm, 1)
            V.tensor_scalar(FY, PB[0][0:NH1, :], BF[:, 0:1], None, ALU.add).then_inc(fg_dve, 1)
            dve.wait_ge(fg_dve, 1)
            link(V.tensor_scalar(FN, FY, -1.0, 0.0, ALU.mult, ALU.max))
            dve.wait_ge(fg_act, 1)
            link(V.tensor_tensor(FN, FN, FA, ALU.add))
            V.tensor_tensor_scan(FG, ONES[0:NH1, :], FN, 0.0, ALU.mult, ALU.add).then_inc(fg_dve, 1)
            for h in range(1, NH1, 2):
                dve.wait_ge(fg_mm, h + 2)
                V.tensor_copy(GB[:, h, :], PB[h][:, :])
            meet(dve, "dve")

            attention("fox", lambda it, h, i, b, nk: GBS[:, h, 0:nk],
                      lambda it, h, i: NAT[:, i, bass.ds((it * 2 + h) * DH, DH)])
            meet(dve, "dve")
            attention("sb", None, lambda it, h, i: NAT[:, i, bass.ds((it * 2 + h) * DH + 512, DH)])
            meet(dve, "dve")
            heads_T(0, OT, ND)
            meet(dve, "dve")
            g = GR["gates"]
            upto = splitter(split, "gates", GATE_CHUNKS)
            for half in range(2):
                for m in range(2):
                    upto(8 * half + 4 * m + 5)
                    n = g + 4 * half + 2 * m
                    dve.wait_ge(acc_free[0], n // 2 + 1)
                    dve.wait_ge(acc_done, n + 2)
                    for b in range(4):
                        dst = MT[:, 4 * half + b, :]
                        if m == 0:
                            ins = V.tensor_tensor(dst, PB[4 + b][:, :], SIG[:, b, :], ALU.mult)
                        else:
                            ins = V.tensor_tensor(SIG[:, 4 + b, :], PB[4 + b][:, :], SIG[:, 4 + b, :], ALU.mult)
                    ins.then_inc(acc_free[1], 1)
                    if m == 1:
                        dve.wait_ge(acc_free[1], (n + 1) // 2 + 1)
                        for b in range(4):
                            dst = MT[:, 4 * half + b, :]
                            ins = V.tensor_tensor(dst, dst, SIG[:, 4 + b, :], ALU.add)
                        ins.then_inc(half_merged, 1)
            meet(dve, "dve")
            dve.wait_ge(row_in, ROW_NO["gate1"])
            for half in range(2):
                g = GR["wout"] + half
                dve.wait_ge(acc_done, g + 1)
                at_ = slice(half * W, (half + 1) * W)
                for b in range(NT):
                    ins = V.tensor_tensor(SCORE[:, b, :], PB[4 * half + b][:, :], ROW[:, at_], ALU.mult)
                ins.then_inc(acc_free[half], 1)
                dve.wait_ge(acc_free[half], g // 2 + 1)
                for b in range(NT):
                    link(V.tensor_tensor(X[:, b, at_], X[:, b, at_], SCORE[:, b, :], ALU.add))
            meet(dve, "dve")

            normed_T(GS[:, 1, :], MCOLS[:, 24:32], split=False)
            dve.wait_ge(aux_in, AUX["router"])
            dve.wait_ge(r_mm, 1)
            for i in range(NT):
                link(V.tensor_tensor(RL[:, i, :], PB[0][:, i * 32:i * 32 + 20], RBIAS, ALU.add))

            def on4(v):
                return v.unsqueeze(2).broadcast_to([P, NT, 4])

            def pick(vals, diff, key, top, onehot):
                link(V.tensor_reduce(top[:, :, 0], vals, AX.X, ALU.max))
                link(V.tensor_tensor(diff, vals, on4(top[:, :, 0]), ALU.subtract))
                link(V.tensor_scalar(key, diff, 0.0, None, ALU.is_equal))
                link(V.tensor_tensor(key, key, FIRSTK.unsqueeze(1).broadcast_to([P, NT, 4]), ALU.mult))
                link(V.tensor_reduce(top[:, :, 1], key, AX.X, ALU.max))
                link(V.tensor_tensor(onehot, key, on4(top[:, :, 1]), ALU.is_equal))

            GD, GE, KEY, TOP, OHG, ES, OH1, OH2, D2, P2, ES2, TOP2 = (RG[:, m] for m in range(12))
            pick(RL[:, :, 0:4], GD, KEY, TOP, OHG)
            prod = RP.rearrange("p t (g j) -> p t g j", g=GROUPS)
            link(V.tensor_tensor(prod, RL[:, :, 4:20].rearrange("p t (g j) -> p t g j", g=GROUPS),
                                 OHG.unsqueeze(3).broadcast_to([P, NT, GROUPS, PER_GROUP]), ALU.mult))
            link(V.tensor_reduce(ES, prod.rearrange("p t g j -> p t j g"), AX.X, ALU.add))
            pick(ES, D2, KEY, TOP, OH1)
            link(V.scalar_tensor_tensor(out=ES2, in0=OH1, scalar=MASKED, in1=ES, op0=ALU.mult, op1=ALU.add))
            pick(ES2, D2, KEY, TOP2, OH2)
            V.tensor_tensor(D2[:, :, 0], TOP2[:, :, 0], TOP[:, :, 0], ALU.subtract).then_inc(r_exp_in, 1)
            for m, oh in ((0, OH1), (1, OH2)):
                link(V.tensor_tensor(OH[:, m].rearrange("p t (g j) -> p t g j", g=GROUPS),
                                     OHG.unsqueeze(3).broadcast_to([P, NT, GROUPS, PER_GROUP]),
                                     oh.unsqueeze(2).broadcast_to([P, NT, GROUPS, PER_GROUP]), ALU.mult))
            V.tensor_tensor(OH[:, 2], OH[:, 0], OH[:, 1], ALU.add).then_inc(r_oh, 1)
            dve.wait_ge(r_exp, 1)
            link(V.tensor_reduce(KEY[:, :, 0], GE, AX.X, ALU.add))
            link(V.scalar_tensor_tensor(out=KEY[:, :, 1], in0=P2[:, :, 0], scalar=1.0, in1=KEY[:, :, 0], op0=ALU.add, op1=ALU.mult))
            link(V.reciprocal(MW[:, 0, :], KEY[:, :, 1]))
            link(V.tensor_tensor(MW[:, 1, :], MW[:, 0, :], P2[:, :, 0], ALU.mult))
            dve.wait_ge(r_rank, 1)
            R, TE, CS, SH = (RS[:, m] for m in range(4))
            link(V.tensor_copy(R.rearrange("p t e -> p (t e)"), PB[1][:, 0:NT * EXPERTS]))
            n_e, te, cs, sh = PB[2][:, 0:EXPERTS], TE[:, 0, :], CS[:, 0, :], SH[:, 0, :]
            link(V.tensor_scalar(te, n_e, float(P), None, ALU.is_gt))
            for m in (2, 3):
                link(V.scalar_tensor_tensor(out=te, in0=n_e, scalar=float(m * P), in1=te, op0=ALU.is_gt, op1=ALU.add))
            link(V.tensor_tensor_scan(cs, ONES[:, 0:EXPERTS], te, 0.0, ALU.mult, ALU.add))
            link(V.tensor_tensor(sh, cs, te, ALU.subtract))
            link(V.tensor_scalar(sh, sh, float(P), float(EXPERTS * P - P), ALU.mult, ALU.add))
            link(V.tensor_tensor(sh, sh, BASE, ALU.subtract))
            on_tiles = lambda v: v.unsqueeze(1).broadcast_to([P, NT, EXPERTS])
            for i in range(NT):
                link(V.scalar_tensor_tensor(out=RP[:, i], in0=R[:, i], scalar=float(P), in1=sh, op0=ALU.is_ge, op1=ALU.mult))
            link(V.tensor_tensor(R, R, RP, ALU.add))
            link(V.tensor_tensor(R, R, on_tiles(BASE), ALU.add))
            for m in range(2):
                link(V.tensor_tensor(OH[:, m], OH[:, m], R, ALU.mult))
                link(V.tensor_reduce(KEY[:, :, m], OH[:, m], AX.X, ALU.add))
                link(V.tensor_copy(IDX[:, m * NT:(m + 1) * NT], KEY[:, :, m]))
            spk = SPK.rearrange("p (g e) -> p g e", e=EXPERTS)
            link(V.tensor_tensor(spk, spk, CS[0:1, 0, :].unsqueeze(1).broadcast_to([1, 8, EXPERTS]), ALU.is_ge))
            link(V.tensor_reduce(TE[0:1, 1, 0:8], spk, AX.X, ALU.add))
            link(V.tensor_scalar(TE[0:1, 1, 0:7], TE[0:1, 1, 0:7], float(EXPERTS - 1), None, ALU.min))
            link(V.tensor_copy(TE[0:1, 1, 7:8], CS[0:1, 0, EXPERTS - 1:EXPERTS]))
            V.tensor_copy(TAB[:, :], TE[0:1, 1, 0:8]).then_inc(routed, 1)
            meet(dve, "dve")

            def rows_T(E, e):
                dve.wait_ge(x_tp, AHEAD + E + 1)
                for d in range(4):
                    ins = V.tensor_scalar(XST[e % 2][:, 4 + d, :], PB[1][:, d * P:(d + 1) * P], GS[:, 1, 4 + d:5 + d],
                                          MCOLS[:, 28 + d:29 + d], ALU.mult, ALU.add)
                ins.then_inc(x_ht, 1)

            def product(E, e):
                dve.wait_ge(silu_done, E + 1)
                V.tensor_tensor(SG[e % 2], SG[e % 2], PB[3][:, :], ALU.mult).then_inc(act_done, 1)

            def product_T(E, e):
                dve.wait_ge(a_tp, E + 1)
                V.tensor_copy(ACTT[e % 2].rearrange("p a b -> p (a b)"), PB[4][:, :]).then_inc(a_ht, 1)

            with dve.Fori(0, EXPERTS // 4) as it:
                for e in range(4):
                    if e == 0:
                        rows_T(it * 4, 0)
                    product(it * 4 + e, e)
                    if e == 0:
                        rows_T(it * 4 + 1, 1)
                    for n, d in enumerate(DOWN_AFTER[e]):
                        product_T(it * 4 + d, d)
                        if n == 0 and e < 3:
                            rows_T(it * 4 + e + 1, e + 1)
            n_spare = dve.value_load(TAB[0:1, 7:8], min_val=0, max_val=SPARE)
            with dve.Fori(0, SPARE) as t:
                with dve.If(t < n_spare):
                    E = t + EXPERTS
                    rows_T(E, 0)
                    product(E, 0)
                    product_T(E, 0)
            meet(dve, "dve")
            dve.wait_ge(row_in, ROW_NO["gate2"])
            dve.wait_ge(gathered, 16 * 2 * NT)
            for i in range(NT):
                y1, y2 = YG[:, i, :], YG[:, NT + i, :]
                link(V.tensor_scalar(y1, y1, MW[:, 0, i:i + 1], None, ALU.mult))
                link(V.scalar_tensor_tensor(out=y1, in0=y2, scalar=MW[:, 1, i:i + 1], in1=y1, op0=ALU.mult, op1=ALU.add))
                link(V.tensor_tensor(y1, y1, ROW[:, :], ALU.mult))
                V.tensor_tensor(X[:, i, :], X[:, i, :], y1, ALU.add)
            meet(dve, "dve")
            stats()
            dve.wait_ge(row_in, ROW_NO["final"])
            for i in range(NT):
                V.scalar_tensor_tensor(out=X[:, i, :], in0=X[:, i, :], scalar=RSTD[:, i:i + 1], in1=ROW[:, :],
                                       op0=ALU.mult, op1=ALU.mult)
            meet(dve, "dve")

            normed_T(COLS[:, VEC_AT["norm_mix_pre_2"]:VEC_AT["norm_mix_pre_2"] + 8], None)
            g = GR["ain"]
            upto = splitter(split, "ain", chunk_list("ain", 10))
            upto(10)
            evac(g + 1, lambda b: GCT[:, b, :])
            upto(18)
            evac(g + 3, lambda b: CQ[:, b, :])
            upto(20)
            evac(g + 5, lambda b: KRN.rearrange("p a b -> p (a b)"), banks=1, width=NT * 32)
            for m, rank in enumerate((Q_RANK, KV_RANK)):
                dve.wait_ge(l_sum, m + 1)
                V.tensor_scalar(RT[:, m, :], PB[m][:, :], 1.0 / rank, EPS, ALU.mult, ALU.add).then_inc(l_ms, 1)
            for m, (v, name, tiles) in enumerate(((CQ, "a_q_norm_2", 6), (CKV, "a_kv_norm_2", 2))):
                dve.wait_ge(l_rms, m + 1)
                link(V.reciprocal(RT[:, m, :], RT[:, m, :]))
                for k in range(tiles):
                    at_ = VEC_AT[name] + k
                    ins = V.scalar_tensor_tensor(out=v[:, k, :], in0=v[:, k, :], scalar=COLS[:, at_:at_ + 1], in1=RT[:, m, :],
                                                 op0=ALU.mult, op1=ALU.mult)
            ins.then_inc(l_c, 1)

            def rope(v, heads, out_):
                shape = [P, NT, heads, 16] if heads else [P, NT, 16]
                wide = (lambda t: t[:, :, :].unsqueeze(2).broadcast_to(shape)) if heads else (lambda t: t[:, :, :])
                n = NT * max(heads, 1) * 16
                tmp = [RT[:, m, 0:n].rearrange("p (a h b) -> p a h b", a=NT, h=heads) if heads
                       else RT[:, m, 0:n].rearrange("p (a b) -> p a b", a=NT) for m in range(3)]
                x1 = v[:, :, :, NOPE:NOPE + 16] if heads else v[:, :, 0:16]
                x2 = v[:, :, :, NOPE + 16:QK_D] if heads else v[:, :, 16:32]
                o1 = x1 if heads else out_[:, :, 0:16]
                o2 = x2 if heads else out_[:, :, 16:32]
                link(V.tensor_tensor(tmp[0], x1, wide(COS), ALU.mult))
                link(V.tensor_tensor(tmp[1], x2, wide(SIN), ALU.mult))
                link(V.tensor_tensor(tmp[0], tmp[0], tmp[1], ALU.subtract))
                link(V.tensor_tensor(tmp[1], x2, wide(COS), ALU.mult))
                link(V.tensor_tensor(tmp[2], x1, wide(SIN), ALU.mult))
                link(V.tensor_copy(o1, tmp[0]))
                return V.tensor_tensor(o2, tmp[1], tmp[2], ALU.add)

            rope(KRN, 0, KR2).then_inc(m_kn, 1)
            dve.wait_ge(m_kn, 1)
            dve.wait_ge(conv_in, 1)
            for k in range(4):
                w = VEC_AT["a_conv_w_2"] + k
                y = RT[:, 0, :]
                link(V.tensor_scalar(y, GCT[:, k, :], COLS[:, w + 8:w + 9], None, ALU.mult))
                for lag in (1, 2):
                    tap = w + 4 * (2 - lag)
                    link(V.scalar_tensor_tensor(out=y[:, lag:T], in0=GCT[:, k, 0:T - lag], scalar=COLS[:, tap:tap + 1],
                                                in1=y[:, lag:T], op0=ALU.mult, op1=ALU.add))
                link(V.tensor_tensor(YC[:, k, :], GBT[:, k, :], y, ALU.mult))
            evac(GR["qup"] + 1, lambda b: QN[:, b, W:768], width=256)
            evac(GR["kvup"] + 1, lambda b: KVN[:, b, W:D])
            dve.wait_ge(acc_free[0], GR["qup"] // 2 + 1)
            rope(QN.rearrange("p t (h d) -> p t h d", h=MLA_H), MLA_H, None).then_inc(m_qn, 1)
            for m in range(2):
                for h in range(1, MLA_H, 2):
                    dve.wait_ge(m_tp, m * MLA_H + h + 1)
                    if m == 0:
                        V.tensor_scalar(QM[0:QK_D, h, :], PB[h][0:QK_D, :], QK_D ** -0.5, None, ALU.mult).then_inc(m_ht, 1)
                    else:
                        V.tensor_copy(KM[0:QK_D, h, :], PB[h][0:QK_D, :]).then_inc(m_ht, 1)
            meet(dve, "dve")
            dve.wait_ge(aux_in, AUX["caus"])
            attention("mla", lambda it, h, i, b, nk: CAUS[:, T - P - i * P:T],
                      lambda it, h, i: NAT[:, i, bass.ds((it * 2 + h) * DH, DH)])
            meet(dve, "dve")
            heads_T(8, OT2, 4)
            evac(GR["aout"] + 1, lambda b: MN[:, b, W:D])

            def add_normed(row):
                stats()
                dve.wait_ge(row_in, ROW_NO[row])
                for i in range(NT):
                    link(V.scalar_tensor_tensor(out=MN[:, i, :], in0=MN[:, i, :], scalar=RSTD[:, i:i + 1], in1=ROW[:, :],
                                                op0=ALU.mult, op1=ALU.mult))
                    V.tensor_tensor(X[:, i, :], X[:, i, :], MN[:, i, :], ALU.add)

            def mlp(layer):
                meet(dve, "dve")
                add_normed(f"post{layer}")
                meet(dve, "dve")
                v = VEC_AT["norm_mlp_pre_2"] + 8 * layer
                normed_T(COLS[:, v:v + 8], None)
                g = GR[f"up{layer}"]
                with dve.Fori(0, 2) as it:
                    upto = splitter(split, f"up{layer}", chunk_list(f"up{layer}", 8), it, 16, 8)
                    for m in (1, 3):
                        upto(4 * m + 6)
                        dve.wait_ge(acc_done, g + m + 1 + it * 4)
                        for b in range(4):
                            dst = H1[:, bass.ds(it * 16 + 4 * m + b, 1), :].rearrange("p a b -> p (a b)")
                            ins = V.tensor_scalar(dst, PB[4 + b][:, :], 0.0, None, ALU.max)
                        ins.then_inc(acc_free[1], 1)
                        dve.wait_ge(acc_free[1], (g + m) // 2 + 1 + it * 2)
                        dst = H1[:, bass.ds(it * 16 + 4 * m, 4), :]
                        V.tensor_tensor(dst, dst, dst, ALU.mult)
                meet(dve, "dve")
                upto = splitter(split, f"down{layer}", chunk_list(f"down{layer}", 16))
                upto(32)
                evac(GR[f"down{layer}"] + 1, lambda b: MN[:, b, W:D])
                meet(dve, "dve")
                add_normed(f"mlppost{layer}")
                meet(dve, "dve")

            mlp(0)

            normed_T(COLS[:, VEC_AT["norm_mix_pre_2"] + 8:VEC_AT["norm_mix_pre_2"] + 16], None)
            g = GR["cin"]
            upto = splitter(split, "cin", chunk_list("cin", 10))
            upto(10)
            evac(g + 1, lambda b: Q2[:, 4 + b, :], scale=DH ** -0.5)
            upto(18)
            dve.wait_ge(acc_done, g + 4)
            for j in range(2):
                V.tensor_copy(KG[0][0:DH, 2 * j, :], PB[4 + j][0:DH, :])
                V.tensor_copy(KG[0][DH:P, 2 * j + 1, :], PB[4 + j][DH:P, :])
                ins = V.tensor_copy(VG[0][:, 2 * j:2 * j + 2, :], PB[6 + j][:, :].rearrange("p (a b) -> p a b", a=2))
            ins.then_inc(acc_free[1], 1)
            upto(20)
            evac(g + 5, lambda b: GATE[:, :, :].rearrange("p a b -> p (a b)"), banks=1, width=NT * 48)
            dve.wait_ge(c_mm, 1)
            V.tensor_copy(PET.rearrange("p a b -> p (a b)"), PB[6][0:DH, 0:2 * CMP_LEN]).then_inc(c_dve, 1)
            dve.wait_ge(c_mm, 2)
            V.tensor_copy(BC[:, 0:1], PB[4][0:DH, 0:1])
            V.tensor_copy(BC[:, 1:2], PB[5][0:DH, 0:1]).then_inc(c_dve, 1)
            dve.wait_ge(c_act, 1)
            for i in range(NT):
                V.tensor_scalar(GATE[:, i, 0:NSA_H], GATE[:, i, 0:NSA_H], HAS[:, i:i + 1], None, ALU.mult)
            dve.wait_ge(c_mm, 7)
            V.tensor_copy(KC[0:DH, :, :].rearrange("p (b a) n -> p a b n", a=2),
                          PB[7][0:DH, 0:4 * NCMP].rearrange("p (a b n) -> p a b n", a=2, b=2)).then_inc(c_dve, 1)
            dve.wait_ge(c_mm, 8)
            V.tensor_copy(VC[:, :, :].rearrange("p (b a) n -> p a b n", a=2),
                          PB[6][0:NCMP, 0:4 * DH].rearrange("p (a b n) -> p a b n", a=2, b=2)).then_inc(c_dve, 1)
            meet(dve, "dve")
            dve.wait_ge(aux_in, AUX["dist"])
            meet(dve, "dve")

            def nsa_bias_of(it, h, i, b, nk):
                return CBIAS[:, h, i * NCMP:(i + 1) * NCMP] if b == 0 else BIAS[:, h, T - P - i * P:T]

            attention("nsa", nsa_bias_of, lambda it, h, i: NAT[:, i, bass.ds((it * NSA_R + h) * DH, DH)])
            meet(dve, "dve")
            heads_T(12, OT, ND)
            evac(GR["cout"] + 1, lambda b: MN[:, b, W:D])
            mlp(1)
            dve.drain()
            dve.sem_inc(stored, 1)

        @blk.sync
        def _(sp):
            sp.wait_ge(stored, 1)
            sp.dma_start(out[0].rearrange("(i p) d -> p i d", p=P), X[:, :, :]).then_inc(stored, 16)
            sp.wait_ge(stored, 17)


_INS = ["x", "c", "ada_w", "ada_b", "norm1_g", "w_in", "b_forget", "w_branch_fox", "w_branch_sb", "w_out", "norm2_g",
        "router_group_w", "router_group_b", "router_expert_w", "router_expert_b", "expert_w_gate", "expert_w_up",
        "expert_w_down", "final_g", "norm_mix_pre_2", "norm_mix_post_2", "norm_mlp_pre_2", "norm_mlp_post_2",
        "mlp_w1_2", "mlp_w2_2", "a_w_in_2", "a_conv_w_2", "a_q_norm_2", "a_w_q_up_2", "a_kv_norm_2", "a_w_kv_up_2",
        "a_w_out_2", "c_w_in_2", "c_cmp_pe_k_2", "c_cmp_w1_k_2", "c_cmp_w2_k_2", "c_cmp_pe_v_2", "c_cmp_w1_v_2",
        "c_cmp_w2_v_2", "c_w_out_2"]


def kernel(**inputs):
    import concourse.bacc as bacc
    from concourse.bass_utils import run_bass_kernel_spmd

    nc = bacc.Bacc("TRN2", target_bir_lowering=False, num_devices=1)
    arrays, aps = {}, {}
    given = {name: np.ascontiguousarray(inputs[name]) for name in _INS}
    given.update(constants())
    for name, v in given.items():
        arrays[f"in_{name}"] = v
        aps[name] = nc.dram_tensor(f"in_{name}", v.shape, mybir.dt.from_np(v.dtype), kind="ExternalInput").ap()
    out = nc.dram_tensor("out", (1, T, D), F32, kind="ExternalOutput").ap()
    program(nc, aps, out)
    r = run_bass_kernel_spmd(nc, [arrays], core_ids=[0])
    return r.results[0]["out"]
```

```python
import numpy as np
import concourse.bass as bass
from concourse import mybir

F32 = mybir.dt.float32
F32R = mybir.dt.float32r
BF16 = mybir.dt.bfloat16
I32 = mybir.dt.int32
ALU = mybir.AluOpType
ACT = mybir.ActivationFunctionType
AX = mybir.AxisListType

P = 128
D = 1024
T = 512
NT = T // P
ND = D // P
W = 512
KK = 4
SLOTS = 4
EPS = 1e-6
BIGNUM = 3.0e38
MASKED = -1.0e30
FAR = 1.0e33
DH = 64
NH1 = 8
EXPERTS, PER_GROUP, GROUPS, DFF = 16, 4, 4, 512
SPARE = (2 * T - EXPERTS) // P
ROWS = (EXPERTS + SPARE) * P
MLA_H, NOPE, ROPE_D = 8, 64, 32
QK_D = NOPE + ROPE_D
Q_RANK, KV_RANK = 768, 256
NSA_H, NSA_G, NSA_R = 16, 4, 4
CMP_LEN, CMP_STRIDE = 32, 16
NCMP = (T - CMP_LEN) // CMP_STRIDE + 1
FF = 4 * D

VECS = [("c", 8), ("norm1_g", 8), ("norm2_g", 8), ("norm_mix_pre_2", 16), ("norm_mlp_pre_2", 16),
        ("a_q_norm_2", 6), ("a_kv_norm_2", 2), ("a_conv_w_2", 12)]
VEC_AT = {}
_n = 0
for _name, _rows in VECS:
    VEC_AT[_name] = _n
    _n += _rows
NVEC = _n

SW_FA, SW_KR, SW_GT, SW_RG, SW_RE, SW_N = 0, 8, 40, 88, 92, 108

CH = {}
_n = 0
for _name, _rows in [("mod", 24), ("qkv", 12), ("gates", 12), ("wout", 4), ("moe", 96), ("ain", 10),
                     ("qup", 3), ("kvup", 1), ("aout", 4), ("up0", 16), ("down0", 16), ("cin", 10),
                     ("cout", 4), ("up1", 16), ("down1", 16)]:
    CH[_name] = _n
    _n += _rows

GR = {}
_n = 2
for _name, _rows in [("mod", 12), ("qkv", 6), ("gates", 8), ("wout", 2), ("ain", 6),
                     ("qup", 2), ("kvup", 2), ("aout", 2), ("up0", 8), ("down0", 2), ("cin", 6),
                     ("cout", 2), ("up1", 8), ("down1", 2)]:
    GR[_name] = _n
    _n += _rows


GU_AT = [0, 4, 10, 16]
DN_AT = [8, 14, 20, 22]
DOWN_AFTER = [[], [0], [1], [2, 3]]

SPLIT = {}
_n = 0
for _name, _chunks in [("qkv", 12), ("gates", 8), ("wout", 4), ("ain", 10), ("aout", 4), ("up0", 16), ("down0", 16),
                       ("cin", 10), ("cout", 4), ("up1", 16), ("down1", 16)]:
    SPLIT[_name] = _n
    _n += 2 * _chunks

FOX0, SB0, MLA0, NSA0 = 0, 32, 64, 96
AHEAD = 16


def constants():
    f = np.float32
    p = np.arange(P)[:, None]
    j = np.arange(T)[None, :] - (T - P)
    ident = np.eye(P, dtype=f)
    caus = np.where(j <= p, 0.0, MASKED).astype(f)
    dist = np.where(j <= p, p - j, FAR).astype(f)
    strict = np.where(np.arange(P)[None, :] < p, 0.0, MASKED).astype(f)
    tok = np.arange(T).reshape(NT, P).T.astype(f)
    starts = np.arange(NCMP) * CMP_STRIDE
    centre = (starts + (CMP_LEN - 1) / 2.0).astype(f)
    end = starts + CMP_LEN - 1
    cd = np.where(end[None, None, :] <= tok[:, :, None], tok[:, :, None] - centre[None, None, :], FAR)
    has = (tok >= end[0]).astype(f)
    inv = (f(10000.0) ** (-np.arange(16, dtype=f) / f(16))).astype(f)
    ang = tok[:, :, None].astype(f) * inv[None, None, :]
    slopes = (2.0 ** (-8.0 * np.arange(1, NSA_H + 1) / NSA_H)).astype(f)
    tri = (np.arange(P)[None, :] > p).astype(f)
    first = np.tile(-np.arange(PER_GROUP, dtype=f) + PER_GROUP, (P, 1))
    base = np.tile(np.arange(EXPERTS, dtype=f) * P, (P, 1))
    spare = np.tile(np.arange(8, dtype=f)[:, None], (1, EXPERTS)).reshape(1, 8 * EXPERTS)
    return {
        "k_ident": ident, "k_caus": caus, "k_dist": dist, "k_strict": strict,
        "k_cdist": cd.astype(f).reshape(P, NT * NCMP), "k_has": has,
        "k_cos": np.cos(ang).astype(f).reshape(P, NT * 16), "k_sin": np.sin(ang).astype(f).reshape(P, NT * 16),
        "k_slopes": np.tile(-slopes, (P, 1)), "k_tri": tri, "k_ones": np.ones((P, T), f),
        "k_first": first, "k_base": base, "k_spare": spare,
    }


def program(nc, a, out):

    def sb(name, shape, dt=F32):
        return nc.alloc_sbuf_tensor(name, shape, dt)

    def sem(name):
        return nc.alloc_semaphore(name)

    X = sb("X", [P, NT, D])
    ht_at = nc.sbuf_base
    HT = sb("HT", [P, ND, T])
    HTH = nc.alloc_sbuf_tensor_at("HTH", [P, ND, T], F32R, offset=ht_at)
    HTL = sb("HTL", [P, ND, T], F32R)
    WH = sb("WH", [P, 2, 2, W], F32R)
    WL = sb("WL", [P, 2, 2, W], F32R)
    KCH = sb("KCH", [P, 4, NCMP + 1], F32R)
    KCL = sb("KCL", [P, 4, NCMP + 1], F32R)
    RING = sb("RING", [P, SLOTS, KK, W])
    BIG = sb("BIG", [P, 16384])
    NAT = sb("NAT", [P, NT, D])
    IDENT = sb("IDENT", [P, P])
    IDB = sb("IDB", [P, P], BF16)
    CMB = sb("CMB", [P, P], BF16)
    SMB = sb("SMB", [P, P], BF16)
    ONES = sb("ONES", [P, T])
    SW = sb("SW", [P, ND, SW_N])
    ROW = sb("ROW", [P, D])
    COLS = sb("COLS", [P, NVEC])
    MCOLS = sb("MCOLS", [P, 48])
    GS = sb("GS", [P, 2, ND])
    COS = sb("COS", [P, NT, 16])
    SIN = sb("SIN", [P, NT, 16])
    SCORE = sb("SCORE", [P, 4, T])
    PT = sb("PT", [P, 2, NT, P])
    QS = sb("QS", [P, 2, T])
    STAT = sb("STAT", [P, 64])

    PB = [nc.alloc_psum_tensor(f"PB{i}", [P, T], F32) for i in range(8)]

    def big(at, *shape):
        n = int(np.prod(shape))
        v = BIG[:, at:at + n]
        if len(shape) == 2:
            v = v.rearrange("p (a b) -> p a b", a=shape[0])
        if len(shape) == 3:
            v = v.rearrange("p (a b c) -> p a b c", a=shape[0], b=shape[1])
        return v

    mod_dram = nc.dram_tensor("mod_scratch", (1, 6 * D), F32).ap()
    disp = nc.dram_tensor("dispatch_rows", (ROWS + P, D), F32).ap()
    back = nc.dram_tensor("expert_rows", (ROWS, D), F32).ap()

    loaded = sem("loaded")
    loaded_rest = sem("loaded_rest")
    arrived = [sem(f"chunk_in_slot{s}") for s in range(SLOTS)]
    chunk_begun = sem("chunk_begun")
    acc_done = sem("acc_done")
    acc_free = [sem(f"acc_free{s}") for s in range(2)]
    met = sem("met")

    dve_chain = sem("dve_chain")
    act_chain = sem("act_chain")
    pool_chain = sem("pool_chain")

    waited = sem("waited")

    def wait_apart(eng, s, value):
        eng.wait_ge(s, value)
        eng.sem_inc(waited, 1)

    def part_no(stage, part, turn=0, per_turn=0):
        return SPLIT[stage] + part + turn * per_turn

    meets = {}

    def meet(eng, key):
        n = meets.setdefault(key, 0) + 1
        meets[key] = n
        eng.drain()
        eng.sem_inc(met, 1)
        eng.wait_ge(met, 4 * n)

    def tall(w, k0, c0, kk=KK, width=W):
        return w[k0 * P:(k0 + kk) * P, c0:c0 + width].rearrange("(t p) n -> p t n", p=P)

    def slot_count(n, turn=0, per_turn=0):
        return 16 * (n // SLOTS + 1) + turn * (16 * per_turn // SLOTS)

    def slot(n, kk=KK, width=W):
        if kk == KK and width == W:
            return RING[:, n % SLOTS]
        return RING[:, n % SLOTS].rearrange("p a b -> p (a b)")[:, 0:kk * width].rearrange("p (a b) -> p a b", a=kk)

    high_ready, low_ready = sem("high_parts_written"), sem("low_parts_written")
    part_begun = sem("part_begun")
    norm_high, norm_low = [sem(f"norm_high{s}") for s in range(2)], sem("norm_low_parts")
    vec_t, cols, cact, mod_io = sem("vectors_transposed"), sem("columns_ready"), sem("c_silu"), sem("mod_moved")
    n_sq, n_ms, n_rms, n_rstd = sem("squares_summed"), sem("mean_squares"), sem("rms_ready"), sem("rstd_ready")
    n_xn, n_tp, aux_in = sem("rows_normed"), sem("norm_transposed"), sem("later_loads")
    n_ht = [sem(f"HT_written{m}") for m in range(2)]
    row_in = sem("gain_row_loaded")
    x_rows = sem("X_rows_updated")
    final_row_in = sem("final_row_loaded")
    fw_high, fw_low = sem("forget_weights_high"), sem("forget_weights_low")
    fg_mm, fg_dve, fg_act = sem("forget_products"), sem("forget_vector"), sem("forget_scalar")
    heads_in, qk, scored, exped = sem("heads_copied"), sem("qk_done"), sem("scored"), sem("exped")
    tp, ev = sem("probs_transposed"), [sem("PT0_written"), sem("PT1_written")]
    pv, normed, recip = sem("pv_done"), sem("normed"), sem("recip_ready")
    sb_beta, sb_scan = sem("sb_sigmoids_ready"), sem("sb_products_ready")
    o_tp, o_ht = sem("O_transposed"), sem("OT_written")
    r_lt = sem("route_logits_copied")
    r_mm, r_exp_in, r_exp, r_oh, r_rank, routed = (sem(f"route_{x}") for x in
                                                   ("logits", "exp_in", "exp", "onehot", "rank", "done"))
    zeroed, zero_out, sent = sem("zero_tile"), sem("dispatch_cleared"), sem("rows_dispatched")
    x_tp, x_ht, gu_done, silu_done, act_done, a_tp, a_ht, down_done, y_ev = (
        sem(f"moe_{x}") for x in ("rows_transposed", "rows_T", "gate_up", "silu", "act",
                                  "act_transposed", "act_T", "down", "y_copied"))
    half_merged = sem("half_merged")
    xs_in, y_out = [sem(f"moe_rows_in{m}") for m in range(2)], [sem(f"moe_y_stored{m}") for m in range(2)]
    spare_in, gathered = sem("spare_weights_in"), [sem(f"y_gathered{i}") for i in range(NT)]
    l_sq, l_sum, l_ms, l_rms, l_c, conv_in = (sem(f"latent_{x}") for x in
                                              ("squares", "sums", "ms", "rms", "normed", "conv_input"))
    m_qn, m_kn, m_tp, m_ht = sem("q_roped"), sem("k_roped"), sem("mla_transposed"), sem("mla_T")
    c_dup, c_mm, c_dve, c_act = (sem(f"cmp_{x}") for x in ("duplicated", "products", "vector", "scalar"))
    pair_high, sums_in = sem("pair_high"), sem("forget_sums_ready")
    q_high, q_ready = sem("q_high"), sem("q_stack_ready")
    kg_high, kg_low, cmp_ready, sls_ready = (sem(f"nsa_{x}") for x in ("keys_high", "keys_low", "values_ready", "slopes_ready"))
    nsa_bias, stored = sem("nsa_bias_ready"), sem("output_stored")

    ADAB, MODR = BIG[0:1, 0:6 * D], BIG[0:1, 6 * D:12 * D]
    VROWS, MROWS = BIG[0:NVEC, 12 * D:12 * D + P], BIG[0:48, 12 * D + P:12 * D + 2 * P]
    TMPB = BIG[:, 12 * D + 2 * P:12 * D + 3 * P]
    BF = sb("BF", [NH1, 1])
    QA, KA, QB, KB = (big(2048 * i, 4, T) for i in range(4))
    VA, VB, GB = big(8192, NT, 512), big(10240, NT, 512), big(12288, NH1, T)
    OT, MT, SIG = big(0, ND, T), big(4096, ND, T), big(8192, 8, T)
    GBS = NAT[:, :, T:D]
    FY, FA, FN, FG = (NAT[0:NH1, i, 0:T] for i in range(4))
    EXACT = ([SCORE[:, d, :] for d in range(4)] + [QS[:, d, :] for d in range(2)]
             + [PT[:, d, :, :].rearrange("p a b -> p (a b)") for d in range(2)])
    XS = [HT[:, 2 * i:2 * i + 2, :].rearrange("p a b -> p (a b)") for i in range(2)]
    XST = [HT[:, 4 + 2 * i:6 + 2 * i, :].rearrange("p a (b c) -> p (a b) c", b=4) for i in range(2)]
    SG = [NAT[:, 0, i * DFF:(i + 1) * DFF] for i in range(2)]
    ACTT = [NAT[:, 1, i * DFF:(i + 1) * DFF].rearrange("p (a b) -> p a b", a=4) for i in range(2)]
    YN = [NAT[:, 2 + i, :] for i in range(2)]
    SPW = big(0, 6, KK, W)
    YG = big(0, 8, D)
    ZERO = BIG[:, 15360:16384]
    FINAL_ROW = BIG[:, 8192:8192 + D]
    GBT, GCT, HVT, CQ, CKV = big(0, 4, T), big(2048, 4, T), big(4096, 4, T), big(6144, 6, T), big(9216, 2, T)
    YC, QM, KN, KM = GBT, big(2048, MLA_H, T), big(6144, NT, MLA_H, QK_D), big(12288, MLA_H, T)
    KRN, KR2, RT = big(10240, NT, 32), big(10368, NT, 32), big(10496, 3, 512)
    OT2, SQ = big(6144, 4, T), NAT
    QN = NAT[:, :, :].rearrange("p a b -> p (a b)")[:, 0:NT * 768].rearrange("p (a b) -> p a b", a=NT)
    KVN = HT[:, :, :].rearrange("p (a c) b -> p a (c b)", c=2)
    PAIR_H, PAIR_L = [WH[:, m] for m in range(2)], [WL[:, m] for m in range(2)]
    QST = [WH[:, m // 2, m % 2, :] for m in range(4)]
    FWH, FWL = (t[:, 0:2, :].rearrange("p a b -> p (a b)").rearrange("p (k h) -> p k h", h=NH1) for t in (KCH, KCL))
    KGH, KGL = HTH, HTL
    MN = NAT
    CONV = big(12288, 4, T)
    Q2, KG, VG = big(0, ND, T), [big(4096, 4, T), big(6144, 4, T)], [big(8192, NT, 256), big(9216, NT, 256)]
    ZT = [big(10240, 2, T), big(11264, 2, T)]
    CW = [big(12288, CMP_LEN, DH), big(14336, CMP_LEN, DH)]
    BIAS, CBIAS = big(13312, NSA_R, T), big(12800, NSA_R, NT * NCMP)
    DIST = BIG[:, 12288:12800]
    H1 = big(0, FF // P, T)
    CAUS = BIG[:, 9216:9728]
    flat = SCORE[:, :, :].rearrange("p a b -> p (a b)")
    at = [0]

    def small(*shape, parts=P):
        n = int(np.prod(shape))
        v = flat[0:parts, at[0]:at[0] + n]
        at[0] += n
        if len(shape) == 2:
            v = v.rearrange("p (a b) -> p a b", a=shape[0])
        if len(shape) == 3:
            v = v.rearrange("p (a b c) -> p a b c", a=shape[0], b=shape[1])
        return v

    RLT = QS[0:20, 0, :]
    RL, RBIAS, FIRSTK, BASE, TRI = small(NT, 20), small(20), small(4), small(EXPERTS), small(P)
    RS, OH, RG = small(4, NT, EXPERTS), small(3, NT, EXPERTS), small(12, NT, 4)
    RP = small(NT, EXPERTS)
    SPK = small(8 * EXPERTS, parts=1)
    PER, PET, CW2 = small(2, DH, parts=CMP_LEN), small(2, CMP_LEN, parts=DH), small(2, DH, parts=DH)
    HD = small(2, 4, NCMP, parts=DH)
    BC = small(2, parts=DH)
    KC = small(4, NCMP + 1)
    assert at[0] <= 4 * T
    IDX = sb("IDX", [P, 2 * NT], I32)
    TAB = sb("TAB", [1, 8], I32)
    MW = sb("MW", [P, 2, NT])
    VC = sb("VC", [NCMP, 4, DH])
    VCS = sb("VCS", [NCMP, 1, DH])
    CDIST = sb("CDIST", [P, NT * NCMP])
    GATE = sb("GATE", [P, NT, 48])
    SLOPE = sb("SLOPE", [P, NSA_H])
    SLS = sb("SLS", [P, NSA_R])
    HAS = sb("HAS", [P, NT])

    block = nc.Block()
    with block as blk:

        @blk.sync
        def _(sp):
            def load(n, src, kk=KK, width=W, turn=0, per_turn=0):
                if n >= SLOTS:
                    sp.wait_ge(chunk_begun, n - SLOTS + 2 + turn * per_turn)
                sp.dma_start(slot(n, kk, width), src).then_inc(arrived[n % SLOTS], 16)

            def halves(n, w, c0, k0=0, turn=0, per_turn=0):
                load(n, tall(w, k0, c0), turn=turn, per_turn=per_turn)
                load(n + 1, tall(w, k0 + KK, c0), turn=turn, per_turn=per_turn)

            ada = a["ada_w"][0]
            for g in range(4):
                halves(2 * g, ada, g * W)
            with sp.Fori(0, 2) as i:
                for g in range(4):
                    n = 8 + 2 * g
                    for h in range(2):
                        load(n + h, ada[h * KK * P:(h + 1) * KK * P, bass.ds((i + 1) * (4 * W) + g * W, W)]
                             .rearrange("(t p) n -> p t n", p=P), turn=i, per_turn=8)
            w_in = a["w_in"][0]
            for g, c0 in enumerate([0, 512, 1024, 1544, 2056, 2568]):
                halves(CH["qkv"] + 2 * g, w_in, c0)
            for half in range(2):
                n = CH["gates"] + 6 * half
                halves(n, w_in, 3080 + half * W)
                load(n + 2, tall(a["w_branch_fox"][0], 0, half * W))
                halves(n + 3, w_in, 4104 + half * W)
                load(n + 5, tall(a["w_branch_sb"][0], 0, half * W))
            for half in range(2):
                halves(CH["wout"] + 2 * half, a["w_out"][0], half * W)
            with sp.Fori(0, EXPERTS // 4) as i:
                for e in range(4):
                    def expert(w, e, k0, c0):
                        return (w[0, bass.ds(i * 4 + e, 1), k0 * P:(k0 + KK) * P, c0:c0 + W]
                                .rearrange("a (t p) n -> p (a t) n", p=P))
                    for m in range(4):
                        w = a["expert_w_gate"] if m < 2 else a["expert_w_up"]
                        load(CH["moe"] + GU_AT[e] + m, expert(w, e, KK * (m % 2), 0), turn=i, per_turn=24)
                    for d in DOWN_AFTER[e]:
                        for half in range(2):
                            load(CH["moe"] + DN_AT[d] + half, expert(a["expert_w_down"], d, 0, half * W),
                                 turn=i, per_turn=24)
            sp.wait_ge(routed, 1)
            n_spare = sp.value_load(TAB[0:1, 7:8], min_val=0, max_val=SPARE)
            with sp.Fori(0, SPARE) as g:
                with sp.If(g < n_spare):
                    e = sp.value_load(TAB[0:1, bass.ds(g, 1)], min_val=0, max_val=EXPERTS - 1)
                    sp.wait_ge(down_done, EXPERTS + g)
                    for m, (w, k0, c0) in enumerate([("expert_w_gate", 0, 0), ("expert_w_gate", KK, 0),
                                                     ("expert_w_up", 0, 0), ("expert_w_up", KK, 0),
                                                     ("expert_w_down", 0, 0), ("expert_w_down", 0, W)]):
                        src = a[w][0, bass.ds(e, 1), k0 * P:(k0 + KK) * P, c0:c0 + W]
                        sp.dma_start(SPW[:, m], src.rearrange("a (t p) n -> p (a t) n", p=P)).then_inc(spare_in, 16)
            aw = a["a_w_in_2"][0]
            for g in range(5):
                halves(CH["ain"] + 2 * g, aw, g * W)
            qup = a["a_w_q_up_2"][0]
            load(CH["qup"], tall(qup, 0, 0))
            load(CH["qup"] + 1, tall(qup, 4, 0, 2), 2)
            load(CH["qup"] + 2, tall(qup, 0, W, 6, 256), 6, 256)
            load(CH["kvup"], tall(a["a_w_kv_up_2"][0], 0, 0, 2, 1024), 2, 1024)
            for half in range(2):
                halves(CH["aout"] + 2 * half, a["a_w_out_2"][0], half * W)

            def mlp(layer):
                w1, w2 = a["mlp_w1_2"][layer], a["mlp_w2_2"][layer]
                with sp.Fori(0, 2) as i:
                    for g in range(4):
                        for h in range(2):
                            load(CH[f"up{layer}"] + 2 * g + h,
                                 w1[h * KK * P:(h + 1) * KK * P, bass.ds(i * (4 * W) + g * W, W)]
                                 .rearrange("(t p) n -> p t n", p=P), turn=i, per_turn=8)
                with sp.Fori(0, 2) as i:
                    for m in range(8):
                        load(CH[f"down{layer}"] + m, w2[m * KK * P:(m + 1) * KK * P, bass.ds(i * W, W)]
                             .rearrange("(t p) n -> p t n", p=P), turn=i, per_turn=8)

            mlp(0)
            cw = a["c_w_in_2"][0]
            for g in range(5):
                halves(CH["cin"] + 2 * g, cw, g * W)
            for half in range(2):
                halves(CH["cout"] + 2 * half, a["c_w_out_2"][0], half * W)
            mlp(1)


        ROW_NO = {name: 16 * (n + 1) for n, name in
                  enumerate(["gate1", "gate2", "post0", "mlppost0", "post1", "mlppost1"])}
        AUX = {"router": 96, "caus": 112, "cmp": 288, "dist": 304}

        def row_on_all(v):
            return v.partition_broadcast(P)

        NORM_LOW = {name: ND * (n + 1) for n, name in enumerate(["qkv", "ain", "up0", "cin", "up1"])}
        NFIRST = len(VECS) + 2
        NREST = 10
        norm_no = {"act": 0, "dve": 0}
        SS, MS, RMS, RSTD = (STAT[:, 8 + 4 * i:12 + 4 * i] for i in range(4))
        CACT = STAT[:, 0:8]
        NM, RSUM = STAT[:, 24:28], STAT[:, 28:32]
        RINV, GSC = STAT[:, 32:36], STAT[:, 36:40]

        ATT = {
            "fox": (FOX0, 2, 4, 1), "sb": (SB0, 2, 4, 1), "mla": (MLA0, 4, 2, 1), "nsa": (NSA0, 4, 4, 3),
        }

        def units(kind):
            _, _, heads, branches = ATT[kind]
            out_, u = [], 0
            for h in range(heads):
                for i in range(NT):
                    for b in range(branches):
                        out_.append((u, h, i, b))
                        u += 1
            return out_

        RECIP0 = {"fox": 0, "mla": 32, "nsa": 64}
        LAG_T = {"fox": 2, "sb": 2, "mla": 2, "nsa": 2}

        def keys(i, kind, b):
            return NCMP if kind == "nsa" and b == 0 else (i + 1) * P

        def pieces(i, kind, b):
            return [(0, NCMP)] if kind == "nsa" and b == 0 else [(j, P) for j in range(i + 1)]

        BY_SCALAR = {"fox": (0, 2, 3), "sb": (1, 3), "mla": (0, 3), "nsa": (0, 3)}

        def move_probs(eng, copy, kind, n0, it, U, u, i, b):
            eng.wait_ge(tp, n0 + u + 1)
            eng.wait_ge(pv, n0 + u - 1)
            m = pieces(i, kind, b)
            rows = m[0][1]
            src = PB[4 + u % 2][0:rows, 0:len(m) * P]
            copy(PT[0:rows, u % 2, 0:len(m), :], src.rearrange("p (a b) -> p a b", b=P)).then_inc(ev[u % 2], 1)

        def splitter(split, stage, chunks, turn=0, parts_a_turn=0, chunks_a_turn=0):
            done = [0]

            def upto(n):
                while done[0] < min(n, 2 * len(chunks)):
                    q = done[0]
                    split(stage, q, chunks[q // 2], turn, parts_a_turn, chunks_a_turn)
                    done[0] += 1
            return upto

        def chunk_list(stage, count):
            return [CH[stage] + m for m in range(count)]

        GATE_CHUNKS = [CH["gates"] + m for m in (0, 1, 3, 4, 6, 7, 9, 10)]

        def halves_of(n, q):
            return slot(n)[:, 2 * (q % 2):2 * (q % 2) + 2, :]

        def tiles_of(v, q):
            return v[:, 2 * q:2 * q + 2, :]

        INPUTS = {
            "wout": lambda q: tiles_of(MT, q % 4), "cout": lambda q: tiles_of(OT, q % 4),
            "aout": lambda q: tiles_of(YC if q % 4 < 2 else OT2, q % 2),
            "down0": lambda q: tiles_of(H1, q % 16), "down1": lambda q: tiles_of(H1, q % 16),
        }

        @blk.scalar
        def _(act):
            chain = [0]

            def link(ins):
                ins.then_inc(act_chain, 1)
                chain[0] += 1
                act.wait_ge(act_chain, chain[0])

            def first(dst, src):
                act.dma_start(dst, src).then_inc(loaded, 16)

            def rest(dst, src):
                act.dma_start(dst, src).then_inc(loaded_rest, 16)

            def later(dst, src):
                act.dma_start(dst, src).then_inc(aux_in, 16)

            def gain_row(src):
                act.dma_start(ROW[:, :], src).then_inc(row_in, 16)

            act.sem_inc(exped, AHEAD)
            act.sem_inc(y_ev, 1)
            for name, rows in VECS:
                src = a[name]
                if len(src.shape) == 3:
                    src = src.rearrange("a b c -> (a b) c")
                first(VROWS[VEC_AT[name]:VEC_AT[name] + rows, :], src.rearrange("a (r p) -> (a r) p", p=P))
            first(ADAB, a["ada_b"])
            first(IDENT[:, :], a["k_ident"])
            act.wait_ge(cols, 1)
            nc.scalar.activation(CACT, COLS[:, 0:8], ACT.Silu).then_inc(cact, 1)
            rest(TMPB, a["k_strict"])
            rest(X[:, :, :], a["x"][0].rearrange("(i p) d -> p i d", p=P))
            rest(SW[:, :, SW_FA:SW_FA + 8], a["w_in"][0][:, 1536:1544].rearrange("(t p) n -> p t n", p=P))
            rest(SW[:, :, SW_KR:SW_KR + 32], a["a_w_in_2"][0][:, 2560:2592].rearrange("(t p) n -> p t n", p=P))
            rest(SW[:, :, SW_GT:SW_GT + 48], a["c_w_in_2"][0][:, 2560:2608].rearrange("(t p) n -> p t n", p=P))
            rest(SW[:, :, SW_RG:SW_RG + 4], a["router_group_w"][0].rearrange("(t p) n -> p t n", p=P))
            rest(SW[:, :, SW_RE:SW_RE + 16], a["router_expert_w"][0].rearrange("(t p) n -> p t n", p=P))
            rest(BIG[:, 12 * D + 3 * P:12 * D + 4 * P], a["k_caus"][:, T - P:T])
            rest(COS[:, :, :], a["k_cos"].rearrange("p (a b) -> p a b", a=NT))
            rest(SIN[:, :, :], a["k_sin"].rearrange("p (a b) -> p a b", a=NT))
            for s in range(2):
                act.wait_ge(acc_free[s], GR["qkv"] // 2)
            act.dma_start(mod_dram, MODR).then_inc(mod_io, 16)
            act.dma_start(BF[:, :], a["b_forget"].rearrange("a b -> b a")).then_inc(mod_io, 16)
            act.wait_ge(mod_io, 32)
            act.dma_start(MROWS, mod_dram[0].rearrange("(r p) -> r p", p=P)).then_inc(mod_io, 16)
            gain_row(row_on_all(mod_dram[0, 2 * D:3 * D]))

            def stats(src, squares=NAT, fresh=False):
                k = norm_no["act"]
                norm_no["act"] += 1
                for i in range(NT):
                    if fresh:
                        row_tiles[0] += 1
                        act.wait_ge(x_rows, row_tiles[0])
                    nc.scalar.activation(squares[:, i, :], src[:, i, :], ACT.Square, accum_out=SS[:, i:i + 1]).then_inc(n_sq, 1)
                act.wait_ge(n_ms, k + 1)
                nc.scalar.activation(RMS, MS, ACT.Sqrt).then_inc(n_rms, 1)

            row_tiles = [0]

            def projection_in(g):
                act.wait_ge(acc_free[0], g // 2 + 1)
                act.wait_ge(acc_free[1], (g + 1) // 2 + 1)

            tps = [0]

            def affine(gain, shift, split=True):
                for d in range(0, ND, 2):
                    act.wait_ge(n_tp, tps[0] + d + 1)
                    bias = shift[:, d:d + 1] if shift is not None else 0.0
                    if split:
                        nc.scalar.activation(EXACT[d], PB[d][:, :], ACT.Identity, bias=bias, scale=gain[:, d:d + 1])
                        nc.scalar.activation(HTH[:, d, :], PB[d][:, :], ACT.Identity, bias=bias,
                                             scale=gain[:, d:d + 1]).then_inc(norm_high[0], 1)
                        continue
                    nc.scalar.activation(HT[:, d, :], PB[d][:, :], ACT.Identity, bias=bias,
                                         scale=gain[:, d:d + 1]).then_inc(n_ht[0], 1)
                tps[0] += ND

            def split(stage, q, n, turn, parts_a_turn, chunks_a_turn):
                act.wait_ge(arrived[n % SLOTS], slot_count(n, turn, chunks_a_turn))
                if SPLIT[stage] + q > 1:
                    act.wait_ge(part_begun, part_no(stage, q, turn, parts_a_turn))
                ins = nc.scalar.copy(WH[:, q % 2], halves_of(n, q))
                if stage in INPUTS:
                    ins = nc.scalar.copy(HTH[:, 2 * (q % 2):2 * (q % 2) + 2, :], INPUTS[stage](q))
                ins.then_inc(high_ready, 1)

            def evac(g, dst, func=ACT.Copy, scale=1.0, banks=4, width=T):
                act.wait_ge(acc_done, g + 1)
                for b in range(banks):
                    ins = nc.scalar.activation(dst(b), PB[b][:, 0:width], func, scale=scale)
                ins.then_inc(acc_free[0], 1)

            def pair_highs(kind, it, p):
                u0, U = ATT[kind][0], len(units(kind))
                used = AHEAD + u0 + it * U - U + 8 * (p + 1)
                wait_apart(act, qk, used)
                q, k = (QA, KA) if kind == "fox" else (QB, KB)
                for m, src in enumerate((q, k)):
                    at_ = bass.ds(it * 2 + p, 1)
                    ins = nc.scalar.copy(PAIR_H[p][:, m, :], src[:, at_, :].rearrange("p a b -> p (a b)"))
                ins.then_inc(pair_high, 1)
                if kind == "fox":
                    wait_apart(act, scored, used)
                    nc.scalar.copy(GBS[:, 2 * p:2 * p + 2, :], GB[:, bass.ds(it * 4 + 2 * p, 2), :]).then_inc(sums_in, 1)

            def attention(kind):
                u0, turns, heads, branches = ATT[kind]
                us = units(kind)
                U, lag = len(us), LAG_T[kind]
                with act.Fori(0, turns) as it:
                    n0 = AHEAD + u0 + it * U
                    for s in range(U + lag):
                        if kind in ("fox", "sb") and s in (0, NT):
                            pair_highs(kind, it, s // NT)
                        if s < U:
                            u, h, i, b = us[s]
                            nk, sc = keys(i, kind, b), SCORE[:, u % 4, :]
                            if kind == "sb":
                                act.wait_ge(qk, n0 + u + 1)
                                wait_apart(act, tp, n0 + u - 3)
                                nc.scalar.activation(sc[:, 0:nk], PB[u % 4][:, 0:nk], ACT.Sigmoid)
                                act.wait_ge(scored, n0 + u - 1)
                                nc.scalar.activation(QS[:, u % 2, 0:nk], PB[u % 4][:, 0:nk], ACT.Sigmoid,
                                                     scale=-1.0).then_inc(sb_beta, 1)
                            else:
                                act.wait_ge(scored, n0 + u + 1)
                                nc.scalar.activation(sc[:, 0:nk], sc[:, 0:nk], ACT.Exp, bias=NM[:, u % 4:u % 4 + 1],
                                                     scale=-1.0, accum_out=RSUM[:, u % 4:u % 4 + 1]).then_inc(exped, 1)
                        if s >= lag:
                            u, h, i, b = us[s - lag]
                            if i in BY_SCALAR[kind]:
                                move_probs(act, nc.scalar.copy, kind, n0, it, U, u, i, b)

            def heads_T(base, dst, count):
                for d in range(0, count, 2):
                    act.wait_ge(o_tp, base + d + 1)
                    nc.scalar.copy(dst[:, d, :], PB[d][:, :]).then_inc(o_ht, 1)

            meet(act, "act")
            stats(X)
            affine(GS[:, 0, :], MCOLS[:, 0:8])
            g = GR["qkv"]
            upto = splitter(split, "qkv", chunk_list("qkv", 12))
            upto(6)
            nc.scalar.copy(FWH, SW[:, :, SW_FA:SW_FA + NH1]).then_inc(fw_high, 1)
            evac(g, lambda b: QA[:, b, :], scale=DH ** -0.5)
            upto(14)
            evac(g + 2, lambda b: VA[:, b, :])
            upto(22)
            evac(g + 4, lambda b: KB[:, b, :])
            upto(24)
            meet(act, "act")
            act.wait_ge(fg_dve, 1)
            link(nc.scalar.activation(FA, FY, ACT.Abs))
            link(nc.scalar.activation(FA, FA, ACT.Exp, scale=-1.0))
            nc.scalar.activation(FA, FA, ACT.Ln, bias=1.0).then_inc(fg_act, 1)
            for h in range(0, NH1, 2):
                act.wait_ge(fg_mm, h + 2)
                nc.scalar.copy(GB[:, h, :], PB[h][:, :])
            meet(act, "act")
            attention("fox")
            meet(act, "act")
            attention("sb")
            act.sem_inc(exped, MLA0 - SB0)
            meet(act, "act")
            heads_T(0, OT, ND)
            meet(act, "act")
            g = GR["gates"]
            upto = splitter(split, "gates", GATE_CHUNKS)
            for half in range(2):
                for m in range(2):
                    upto(8 * half + 4 * m + 5)
                    act.wait_ge(acc_free[1], (g + 4 * half) // 2)
                    if half:
                        act.wait_ge(half_merged, half)
                    evac(g + 4 * half + 2 * m, lambda b: SIG[:, 4 * m + b, :], ACT.Sigmoid)
            meet(act, "act")
            upto = splitter(split, "wout", chunk_list("wout", 4))
            upto(8)
            meet(act, "act")
            later(RBIAS[:, 0:4], row_on_all(a["router_group_b"][0]))
            later(RBIAS[:, 4:20], row_on_all(a["router_expert_b"][0]))
            later(FIRSTK, a["k_first"])
            later(BASE, a["k_base"])
            later(TRI, a["k_tri"])
            later(SPK, a["k_spare"])
            gain_row(row_on_all(mod_dram[0, 5 * D:6 * D]))
            stats(X)
            affine(GS[:, 1, :], MCOLS[:, 24:32], split=False)
            act.wait_ge(r_exp_in, 1)
            nc.scalar.activation(RG[:, 1], RG[:, 0], ACT.Exp)
            nc.scalar.activation(RG[:, 9, :, 0:1], RG[:, 8, :, 0:1], ACT.Exp).then_inc(r_exp, 1)
            meet(act, "act")

            def expert(E, e):
                act.wait_ge(x_tp, AHEAD + E + 1)
                for d in range(4):
                    ins = nc.scalar.activation(XST[e % 2][:, d, :], PB[0][:, d * P:(d + 1) * P], ACT.Identity,
                                               bias=MCOLS[:, 24 + d:25 + d], scale=GS[:, 1, d:d + 1])
                ins.then_inc(x_ht, 1)

            def silu(E, e):
                act.wait_ge(gu_done, E + 1)
                nc.scalar.activation(SG[e % 2], PB[2][:, :], ACT.Silu).then_inc(silu_done, 1)

            def result(E, e, before):
                act.wait_ge(down_done, E + 1)
                act.wait_ge(y_out[e % 2], (before + 1) * 16)
                nc.scalar.copy(YN[e % 2][:, 0:W], PB[5][:, :])
                nc.scalar.copy(YN[e % 2][:, W:D], PB[6][:, :]).then_inc(y_ev, 1)

            expert(0, 0)
            with act.Fori(0, EXPERTS // 4) as it:
                for e in range(4):
                    E = it * 4 + e
                    silu(E, e)
                    expert(E + 1, e + 1)
                    for d in DOWN_AFTER[e]:
                        result(it * 4 + d, d, it * 2 + d // 2)
            n_spare = act.value_load(TAB[0:1, 7:8], min_val=0, max_val=SPARE)
            with act.Fori(0, SPARE) as t:
                with act.If(t < n_spare):
                    E = t + EXPERTS
                    silu(E, 0)
                    expert(E + 1, 0)
                    result(E, 0, t + EXPERTS // 2)
            meet(act, "act")

            act.dma_start(FINAL_ROW, row_on_all(a["final_g"])).then_inc(final_row_in, 16)
            stats(X, fresh=True)

            stats(X, fresh=True)
            affine(COLS[:, VEC_AT["norm_mix_pre_2"]:VEC_AT["norm_mix_pre_2"] + 8], None)
            g = GR["ain"]
            upto = splitter(split, "ain", chunk_list("ain", 10))
            upto(6)
            evac(g, lambda b: GBT[:, b, :])
            upto(14)
            evac(g + 2, lambda b: HVT[:, b, :])
            upto(20)
            evac(g + 4, lambda b: CQ[:, 4 + b, :] if b < 2 else CKV[:, b - 2, :])
            act.wait_ge(acc_free[0], (g + 4) // 2 + 1)
            act.wait_ge(acc_free[1], (g + 4) // 2)
            nc.scalar.activation(SQ[:, :, :].rearrange("p a (c b) -> p (a c) b", c=2)[:, 0:6, :], CQ, ACT.Square).then_inc(l_sq, 1)
            nc.scalar.activation(SQ[:, :, :].rearrange("p a (c b) -> p (a c) b", c=2)[:, 6:8, :], CKV, ACT.Square).then_inc(l_sq, 1)
            for m in range(2):
                act.wait_ge(l_ms, m + 1)
                nc.scalar.activation(RT[:, m, :], RT[:, m, :], ACT.Sqrt).then_inc(l_rms, 1)
            evac(GR["qup"], lambda b: QN[:, b, 0:W])
            evac(GR["kvup"], lambda b: KVN[:, b, 0:W])
            act.wait_ge(acc_done, GR["kvup"] + 2)
            later(CAUS, a["k_caus"])
            gain_row(row_on_all(a["norm_mix_post_2"][0]))
            for h in range(0, MLA_H, 2):
                act.wait_ge(m_tp, h + 1)
                nc.scalar.mul(QM[0:QK_D, h, :], PB[h][0:QK_D, :], QK_D ** -0.5).then_inc(m_ht, 1)
            for h in range(0, MLA_H, 2):
                act.wait_ge(m_tp, MLA_H + h + 1)
                nc.scalar.copy(KM[0:QK_D, h, :], PB[h][0:QK_D, :]).then_inc(m_ht, 1)
            meet(act, "act")
            attention("mla")
            meet(act, "act")
            heads_T(8, OT2, 4)
            act.wait_ge(o_ht, ND + 4)
            upto = splitter(split, "aout", chunk_list("aout", 4))
            upto(6)
            evac(GR["aout"], lambda b: MN[:, b, 0:W])
            upto(8)

            def mlp(layer):
                projection_in(GR["aout" if layer == 0 else "cout"])
                stats(MN, KVN)
                stats(X, fresh=True)
                gain_row(row_on_all(a["norm_mlp_post_2"][layer]))
                v = VEC_AT["norm_mlp_pre_2"] + 8 * layer
                affine(COLS[:, v:v + 8], None)
                g = GR[f"up{layer}"]
                with act.Fori(0, 2) as it:
                    upto = splitter(split, f"up{layer}", chunk_list(f"up{layer}", 8), it, 16, 8)
                    for m in (0, 2):
                        upto(4 * m + 6)
                        wait_apart(act, acc_done, g + m + 1 + it * 4)
                        for b in range(4):
                            dst = H1[:, bass.ds(it * 16 + 4 * m + b, 1), :].rearrange("p a b -> p (a b)")
                            ins = nc.scalar.activation(dst, PB[b][:, :], ACT.Relu)
                        ins.then_inc(acc_free[0], 1)
                        wait_apart(act, acc_free[0], g // 2 + m // 2 + 1 + it * 2)
                        dst = H1[:, bass.ds(it * 16 + 4 * m, 4), :]
                        nc.scalar.activation(dst, dst, ACT.Square)
                    upto(16)
                meet(act, "act")
                upto = splitter(split, f"down{layer}", chunk_list(f"down{layer}", 16))
                upto(18)
                evac(GR[f"down{layer}"], lambda b: MN[:, b, 0:W])
                upto(32)
                projection_in(GR[f"down{layer}"])
                stats(MN, KVN)

            mlp(0)

            stats(X, fresh=True)
            v = VEC_AT["norm_mix_pre_2"] + 8
            gain_row(row_on_all(a["norm_mix_post_2"][1]))
            for m, x in enumerate("kv"):
                later(CW[m][0:DH], a[f"c_cmp_w1_{x}_2"][0].rearrange("l d e -> d l e"))
                later(CW[m][DH:P], a[f"c_cmp_w1_{x}_2"][0].rearrange("l d e -> d l e"))
            later(CDIST[:, :], a["k_cdist"])
            later(SLOPE[:, :], a["k_slopes"])
            later(HAS[:, :], a["k_has"])
            affine(COLS[:, v:v + 8], None)
            g = GR["cin"]
            upto = splitter(split, "cin", chunk_list("cin", 10))
            upto(6)
            act.wait_ge(norm_low, NORM_LOW["cin"])
            for m, x in enumerate("kv"):
                later(PER[:, m, :], a[f"c_cmp_pe_{x}_2"][0])
                later(CW2[:, m, :], a[f"c_cmp_w2_{x}_2"][0])
            evac(g, lambda b: Q2[:, b, :], scale=DH ** -0.5)
            upto(14)
            evac(g + 2, lambda b: ZT[b // 2][:, b % 2, :])
            upto(20)
            act.wait_ge(acc_done, g + 5)
            for j in range(2):
                nc.scalar.copy(KG[1][0:DH, 2 * j, :], PB[j][0:DH, :])
                nc.scalar.copy(KG[1][DH:P, 2 * j + 1, :], PB[j][DH:P, :])
                ins = nc.scalar.copy(VG[1][:, 2 * j:2 * j + 2, :], PB[2 + j][:, :].rearrange("p (a b) -> p a b", a=2))
            ins.then_inc(acc_free[0], 1)
            act.wait_ge(acc_free[0], (g + 4) // 2 + 1)
            act.wait_ge(acc_free[1], (g + 3) // 2 + 1)
            for m in range(2):
                act.dma_start(KG[m][DH:P, 0:4:2, :], KG[m][0:DH, 0:4:2, :]).then_inc(c_dup, 16)
                act.dma_start(KG[m][0:DH, 1:4:2, :], KG[m][DH:P, 1:4:2, :]).then_inc(c_dup, 16)
            act.wait_ge(acc_free[1], (g + 5) // 2 + 1)
            link(nc.scalar.activation(GATE[:, :, :], GATE[:, :, :], ACT.Sigmoid))
            act.wait_ge(c_dup, 64)
            for g in range(NSA_G):
                for m in range(2):
                    nc.scalar.copy(KGH[:, 2 * g + m, :], KG[m][:, g, :]).then_inc(kg_high, 1)
            act.wait_ge(c_dve, 2)
            for m in range(2):
                for par in range(2):
                    act.wait_ge(c_mm, 2 + 2 * m + par + 1)
                    nc.scalar.activation(HD[:, m, 2 * par:2 * par + 2, :].rearrange("p a b -> p (a b)"),
                                         PB[2 * m + par][0:DH, 0:2 * NCMP], ACT.Gelu_apprx_tanh,
                                         bias=BC[:, m:m + 1]).then_inc(c_act, 1)
            act.wait_ge(c_dve, 4)
            act.dma_start(KC[DH:P, :, :], KC[0:DH, :, :]).then_inc(c_dup, 16)
            act.wait_ge(c_dup, 80)
            nc.scalar.copy(KCH[:, :, :], KC[:, :, :]).then_inc(kg_high, 1)
            meet(act, "act")
            later(DIST, a["k_dist"])
            meet(act, "act")
            attention("nsa")
            meet(act, "act")
            heads_T(12, OT, ND)
            act.wait_ge(o_ht, 2 * ND + 4)
            upto = splitter(split, "cout", chunk_list("cout", 4))
            upto(6)
            evac(GR["cout"], lambda b: MN[:, b, 0:W])
            upto(8)
            mlp(1)

        @blk.gpsimd
        def _(pool):
            chain = [0]

            def link(ins):
                ins.then_inc(pool_chain, 1)
                chain[0] += 1
                pool.wait_ge(pool_chain, chain[0])

            nc.gpsimd.memset(ZERO, 0.0).then_inc(zeroed, 1)
            meet(pool, "pool")
            highs = [0]

            def low_parts():
                for d in range(ND):
                    pool.wait_ge(norm_high[d % 2], highs[0] + d // 2 + 1)
                    nc.gpsimd.tensor_tensor(HTL[:, d, :], EXACT[d], HTH[:, d, :].bitcast(F32), ALU.subtract).then_inc(norm_low, 1)
                highs[0] += ND // 2

            low_parts()
            pool.wait_ge(zeroed, 1)
            for r in range(ROWS // P + 1):
                pool.dma_start(disp[r * P:(r + 1) * P, :], ZERO).then_inc(zero_out, 16)
            for r in range(EXPERTS, EXPERTS + SPARE):
                s = y_out[r % 2] if r < EXPERTS + 2 else zero_out
                pool.dma_start(back[r * P:(r + 1) * P, :], ZERO).then_inc(s, 16)
            pool.wait_ge(zero_out, 16 * (ROWS // P + 1 + SPARE - 2))
            for m in range(2):
                pool.wait_ge(y_out[m], 16)
            meet(pool, "pool")

            def copy_heads(kind, srcs):
                u0, turns, heads, branches = ATT[kind]
                U = len(units(kind))
                with pool.Fori(0, turns) as it:
                    pool.wait_ge(qk, AHEAD + u0 + it * U)
                    pool.wait_ge(scored, AHEAD + u0 + it * U)
                    for dst, src in srcs(it):
                        ins = nc.gpsimd.tensor_copy(dst, src)
                    ins.then_inc(heads_in, 1)

            def one(v, i):
                return v[:, bass.ds(i, 1), :].rearrange("p a b -> p (a b)")

            def pair_lows(kind, before, q, k):
                with pool.Fori(0, ATT[kind][1]) as it:
                    for p in range(2):
                        wait_apart(pool, pair_high, before + it * 2 + p + 1)
                        for m, src in enumerate((q, k)):
                            ins = nc.gpsimd.tensor_tensor(PAIR_L[p][:, m, :], one(src, it * 2 + p),
                                                          PAIR_H[p][:, m, :].bitcast(F32), ALU.subtract)
                        ins.then_inc(heads_in, 1)

            def one_of(v, i):
                return v[:, bass.ds(i, 1), :].rearrange("p a b -> p (a b)")

            meet(pool, "pool")
            pair_lows("fox", 0, QA, KA)
            meet(pool, "pool")
            pair_lows("sb", NH1 // 2, QB, KB)
            meet(pool, "pool")
            for _ in range(3):
                meet(pool, "pool")
            pool.wait_ge(routed, 1)
            for k in range(2):
                for i in range(NT):
                    pool.indirect_dma_start(disp, bass.IndirectOffsetOnAxis(ap=IDX[:, k * NT + i:k * NT + i + 1], axis=0),
                                            NAT[:, i, :], None).then_inc(sent, 16)
            pool.wait_ge(sent, 16 * 2 * NT)
            meet(pool, "pool")

            def rows_in(E, e, lag, src):
                wait_apart(pool, x_tp, AHEAD + E + 1 - lag)
                pool.dma_start(XS[e % 2], src).then_inc(xs_in[e % 2], 16)

            def rows_out(E, e, dst):
                wait_apart(pool, y_ev, E + 2)
                pool.dma_start(dst, YN[e % 2]).then_inc(y_out[e % 2], 16)

            pool.dma_start(XS[0], disp[0:P, :]).then_inc(xs_in[0], 16)
            with pool.Fori(0, EXPERTS // 4) as it:
                for e in range(4):
                    E = it * 4 + e
                    rows_in(E + 1, e + 1, 2, disp[bass.ds((E + 1) * P, P), :])
                    for d in DOWN_AFTER[e]:
                        rows_out(it * 4 + d, d, back[bass.ds((it * 4 + d) * P, P), :])
            for m in range(2):
                pool.wait_ge(y_out[m], 16 * (EXPERTS // 2 + 1))
            n_spare = pool.value_load(TAB[0:1, 7:8], min_val=0, max_val=SPARE)
            with pool.Fori(0, SPARE) as t:
                with pool.If(t < n_spare):
                    E = t + EXPERTS
                    rows_in(E + 1, 0, 1, disp[bass.ds((E + 1) * P, P), :])
                    rows_out(E, 0, back[bass.ds(E * P, P), :])
                    pool.wait_ge(y_out[0], (t + EXPERTS // 2 + 2) * 16)
            meet(pool, "pool")
            for i in range(NT):
                for k in range(2):
                    pool.indirect_dma_start(YG[:, k * NT + i, :], None, back,
                                            bass.IndirectOffsetOnAxis(ap=IDX[:, k * NT + i:k * NT + i + 1], axis=0)
                                            ).then_inc(gathered[i], 16)
            low_parts()
            g = GR["ain"]
            pool.wait_ge(acc_free[0], (g + 2) // 2 + 1)
            pool.wait_ge(acc_free[1], (g + 1) // 2 + 1)
            nc.gpsimd.tensor_tensor(GCT, GCT, HVT, ALU.mult).then_inc(conv_in, 1)
            pool.wait_ge(acc_free[0], GR["kvup"] // 2 + 1)
            pool.wait_ge(acc_free[1], (GR["kvup"] + 1) // 2 + 1)
            pool.wait_ge(m_kn, 1)
            for i in range(NT):
                kv = KVN[:, i, :].rearrange("p (h d) -> p h d", h=MLA_H)
                nc.gpsimd.tensor_copy(KN[:, i, :, 0:NOPE], kv[:, :, 0:NOPE])
                nc.gpsimd.tensor_copy(KN[:, i, :, NOPE:QK_D],
                                      KR2[:, i, :].unsqueeze(1).broadcast_to([P, MLA_H, ROPE_D])).then_inc(m_kn, 1)
            meet(pool, "pool")

            def mla_copy(it):
                return [(QS[0:QK_D, :, :], QM[0:QK_D, bass.ds(it * 2, 2), :])]

            copy_heads("mla", mla_copy)
            meet(pool, "pool")

            def mlp():
                low_parts()
                meet(pool, "pool")

            mlp()
            low_parts()
            for g in range(NSA_G):
                for m in range(2):
                    pool.wait_ge(kg_high, 2 * g + m + 1)
                    n = 2 * g + m
                    nc.gpsimd.tensor_tensor(KGL[:, n, :], KG[m][:, g, :], KGH[:, n, :].bitcast(F32), ALU.subtract)
            pool.wait_ge(kg_high, 9)
            nc.gpsimd.tensor_tensor(KCL[:, :, :], KC[:, :, :], KCH[:, :, :].bitcast(F32), ALU.subtract)
            meet(pool, "pool")
            meet(pool, "pool")
            u0, turns, heads, branches = ATT["nsa"]
            U = len(units("nsa"))
            with pool.Fori(0, turns) as it:
                nc.gpsimd.tensor_copy(SLS[:, :], SLOPE[:, bass.ds(it * NSA_R, NSA_R)]).then_inc(sls_ready, 1)
                wait_apart(pool, sls_ready, it + 1)
                for r in range(NSA_R):
                    own, other = slice((r % 2) * DH, (r % 2 + 1) * DH), slice((1 - r % 2) * DH, (2 - r % 2) * DH)
                    used = AHEAD + u0 + it * U - U + (U // NSA_R) * (r + 1)
                    q = one_of(Q2, it * 2 + r // 2)
                    wait_apart(pool, qk, used)
                    nc.gpsimd.tensor_copy(QST[r][own, :], q[own, :]).then_inc(q_high, 1)
                    wait_apart(pool, q_high, it * NSA_R + r + 1)
                    nc.gpsimd.tensor_tensor(QST[r][other, :], q[own, :], QST[r][own, :].bitcast(F32), ALU.subtract).then_inc(q_ready, 1)
                    wait_apart(pool, q_ready, it * NSA_R + r + 1)
                    wait_apart(pool, scored, used)
                    nc.gpsimd.tensor_scalar(BIAS[:, r, :], DIST, SLS[:, r:r + 1], None, ALU.mult)
                    nc.gpsimd.tensor_scalar(CBIAS[:, r, :], CDIST[:, :], SLS[:, r:r + 1], None, ALU.mult).then_inc(nsa_bias, 1)
                    wait_apart(pool, nsa_bias, it * NSA_R + r + 1)
                    if r == 0:
                        wait_apart(pool, pv, AHEAD + u0 + it * U)
                        nc.gpsimd.tensor_copy(VCS[:, :, :], VC[:, bass.ds(it, 1), :]).then_inc(cmp_ready, 1)
            meet(pool, "pool")
            mlp()

        @blk.tensor
        def _(pe):

            def begin(ins, n):
                ins.then_inc(chunk_begun, 1)

            def await_chunk(n, turn=0, per_turn=0):
                pe.wait_ge(arrived[n % SLOTS], slot_count(n, turn, per_turn))

            def await_set(g, turn=0, per_turn=0):
                pe.wait_ge(acc_free[g % 2], g // 2 + turn * (per_turn // 2))

            def group(g, c, kind, src, chunks=2, turn=0, groups_a_turn=0, chunks_a_turn=0, k_base=0,
                      k_total=None, opens=True, closes=True):
                if opens:
                    await_set(g, turn, groups_a_turn)
                for m in range(chunks):
                    await_chunk(c + m, turn, chunks_a_turn)
                    w = slot(c + m)
                    for b in range(4):
                        for k in range(KK):
                            kk = k_base + m * KK + k
                            if kind == "T":
                                lhs, rhs = w[:, k, b * P:(b + 1) * P], src[:, kk, :]
                            else:
                                lhs, rhs = src[:, kk, b * P:(b + 1) * P], w[:, k, :]
                            ins = pe.matmul(PB[4 * (g % 2) + b][:, :], lhs, rhs,
                                            start=(opens and m == 0 and k == 0),
                                            stop=(closes and m == chunks - 1 and k == KK - 1))
                            if b == 0 and k == 0:
                                begin(ins, c + m)
                if closes:
                    ins.then_inc(acc_done, 1)

            def three(dst, w, k, x, kk, kind, cols_of_b, start, stop_):
                for n, (wp, xp) in enumerate(((w[0], x[0]), (w[0], x[1]), (w[1], x[0]))):
                    if kind == "T":
                        lhs, rhs = wp[:, k, cols_of_b], xp[:, kk, :]
                    else:
                        lhs, rhs = xp[:, kk, cols_of_b], wp[:, k, :]
                    yield pe.matmul(dst, lhs, rhs, start=(start and n == 0), stop=(stop_ and n == 2))

            def split_group(g, stage, q0, kind, parts=4, turn=0, groups_a_turn=0, parts_a_turn=0, wait_norm=None):
                await_set(g, turn, groups_a_turn)
                for m in range(parts):
                    q = q0 + m
                    pe.wait_ge(low_ready, part_no(stage, q, turn, parts_a_turn) + 1)
                    w = (WH[:, q % 2], WL[:, q % 2])
                    for b in range(4):
                        for k in range(2):
                            kk = 2 * (q % 2) + k if kind == "D" else 2 * m + k
                            if wait_norm is not None and (b == 0 or m == 0 and k == 0):
                                pe.wait_ge(norm_low, wait_norm - ND + max(kk, b) + 1)
                            for n, ins in enumerate(three(PB[4 * (g % 2) + b][:, :], w, k, (HTH, HTL), kk, kind,
                                                          slice(b * P, (b + 1) * P), m == 0 and k == 0,
                                                          m == parts - 1 and k == 1)):
                                if b == 0 and k == 0 and n == 0:
                                    ins.then_inc(part_begun, 1)
                                if b == 0 and k == 0 and n == 1 and q % 2 == 0:
                                    begin(ins, None)
                ins.then_inc(acc_done, 1)

            pe.sem_inc(acc_done, GR["mod"])
            pe.sem_inc(tp, AHEAD)
            pe.sem_inc(qk, AHEAD)
            pe.sem_inc(pv, AHEAD)
            pe.sem_inc(x_tp, AHEAD)

            pe.wait_ge(loaded, 16 * NFIRST)
            pe.transpose(PB[7][:, 0:NVEC], VROWS, IDENT[0:NVEC, 0:NVEC]).then_inc(vec_t, 1)
            pe.wait_ge(cact, 1)
            with pe.Fori(0, 3) as it:
                for g in range(4):
                    await_set(GR["mod"] + g, it, 4)
                    for m in range(2):
                        c = 2 * g + m
                        await_chunk(c, it, 8)
                        for k in range(KK):
                            ins = pe.matmul(PB[4 * (g % 2)][0:1, :], CACT[:, m * KK + k:m * KK + k + 1],
                                            slot(c)[:, k, :], start=(m == 0 and k == 0), stop=(m == 1 and k == KK - 1))
                            if k == 0:
                                begin(ins, c)
                    ins.then_inc(acc_done, 1)
            pe.wait_ge(mod_io, 48)
            pe.transpose(PB[6][:, 0:48], MROWS, IDENT[0:48, 0:48]).then_inc(vec_t, 1)
            meet(pe, "pe")

            rows = [0]

            def rows_to_T():
                for d in range(ND):
                    for i in range(NT):
                        if d == 0:
                            pe.wait_ge(n_xn, rows[0] * NT + i + 1)
                        ins = pe.transpose(PB[d][:, i * P:(i + 1) * P], NAT[:, i, d * P:(d + 1) * P], IDENT[:, :])
                    ins.then_inc(n_tp, 1)
                rows[0] += 1

            def attention(kind, products, v, before_head):
                u0, turns, heads, branches = ATT[kind]
                us = units(kind)
                U, lag = len(us), LAG_T[kind]
                with pe.Fori(0, turns) as it:
                    n0 = AHEAD + u0 + it * U
                    for s in range(U + lag + 1):
                        if s < U:
                            u, h, i, b = us[s]
                            nk = keys(i, kind, b)
                            if u % (U // heads) == 0:
                                before_head(it, h)
                            pe.wait_ge(scored, n0 + u - 3)
                            masked = kind in ("fox", "sb")
                            pairs = products(it, h, i, b, nk)
                            for n, (lhs, rhs) in enumerate(pairs):
                                ins = pe.matmul(PB[u % 4][:, 0:nk + nk % 2], lhs, rhs, start=(n == 0),
                                                stop=(n == len(pairs) - 1 and not masked))
                            if masked:
                                mask = CMB if kind == "fox" else SMB
                                ins = pe.matmul(PB[u % 4][:, i * P:nk], IDB[:, :], mask[:, :], start=False, stop=True)
                            ins.then_inc(qk, 1)
                        if lag <= s < U + lag:
                            u, h, i, b = us[s - lag]
                            pe.wait_ge(scored if kind == "sb" else exped, n0 + u + 1)
                            pe.wait_ge(ev[u % 2], (u0 + u) // 2 + it * (U // 2) + AHEAD)
                            for j, n in pieces(i, kind, b):
                                ins = pe.transpose(PB[4 + u % 2][0:n, j * P:(j + 1) * P],
                                                   SCORE[:, u % 4, j * P:j * P + n], IDENT[:, :])
                            ins.then_inc(tp, 1)
                        if s > lag:
                            u, h, i, b = us[s - lag - 1]
                            pe.wait_ge(ev[u % 2], (u0 + u) // 2 + it * (U // 2) + AHEAD + 1)
                            pe.wait_ge(normed, n0 + u - 1)
                            m = pieces(i, kind, b)
                            if kind == "nsa" and u == 0:
                                pe.wait_ge(cmp_ready, it + 1)
                            for j, n in m:
                                ins = pe.matmul(PB[6 + u % 2][:, 0:DH], PT[0:n, u % 2, j, :], v(it, h, b, j, n),
                                                start=(j == 0), stop=(j == len(m) - 1))
                            ins.then_inc(pv, 1)

            def heads_T(count):
                for d in range(count):
                    for i in range(NT):
                        ins = pe.transpose(PB[d][:, i * P:(i + 1) * P], NAT[:, i, d * P:(d + 1) * P], IDENT[:, :])
                    ins.then_inc(o_tp, 1)

            rows_to_T()
            for m, kind in enumerate("TTNTTN"):
                split_group(GR["qkv"] + m, "qkv", 4 * m, kind, wait_norm=NORM_LOW["qkv"] if m == 0 else None)
            meet(pe, "pe")
            pe.wait_ge(fw_low, 1)
            for k in range(ND):
                for n, (w, x) in enumerate(((FWH, HTH), (FWH, HTL), (FWL, HTH))):
                    ins = pe.matmul(PB[0][0:NH1, :], w[:, k, :], x[:, k, :], start=(k == 0 and n == 0),
                                    stop=(k == ND - 1 and n == 2))
            ins.then_inc(fg_mm, 1)
            pe.wait_ge(fg_dve, 2)
            for h in range(NH1):
                pe.matmul(PB[h][:, :], IDENT[0:NH1, h:h + 1].broadcast_to([NH1, P]), FG, start=True, stop=True).then_inc(fg_mm, 1)
            meet(pe, "pe")

            def pair_products(it, h, i, b, nk):
                r, p = slice((h % 2) * DH, (h % 2 + 1) * DH), h // 2
                q = [x[p][r, 0, i * P:(i + 1) * P] for x in (PAIR_H, PAIR_L)]
                k = [x[p][r, 1, 0:nk] for x in (PAIR_H, PAIR_L)]
                return [(q[0], k[0]), (q[0], k[1]), (q[1], k[0])]

            def await_pair(before):
                return lambda it, h: pe.wait_ge(heads_in, before + it * 2 + h // 2 + 1) if h % 2 == 0 else None

            attention("fox", pair_products, lambda it, h, b, j, n: VA[:, j, bass.ds((it * 4 + h) * DH, DH)], await_pair(0))
            meet(pe, "pe")
            attention("sb", pair_products, lambda it, h, b, j, n: VB[:, j, bass.ds((it * 4 + h) * DH, DH)],
                      await_pair(NH1 // 2))
            meet(pe, "pe")
            heads_T(ND)
            pe.wait_ge(o_ht, ND)
            meet(pe, "pe")
            for half in range(2):
                c, g = CH["gates"] + 6 * half, GR["gates"] + 4 * half
                split_group(g, "gates", 8 * half, "T")
                group(g + 1, c + 2, "T", OT, chunks=1)
                split_group(g + 2, "gates", 8 * half + 4, "T")
                group(g + 3, c + 5, "T", OT, chunks=1, k_base=4)
            meet(pe, "pe")
            for half in range(2):
                split_group(GR["wout"] + half, "wout", 4 * half, "D")
            meet(pe, "pe")
            rows_to_T()
            for k in range(ND):
                pe.wait_ge(n_ht[k % 2], k // 2 + 1)
                ins = pe.matmul(PB[0][0:20, :], SW[:, k, SW_RG:SW_N], HT[:, k, :], start=(k == 0), stop=(k == ND - 1))
            ins.then_inc(r_mm, 1)
            pe.wait_ge(r_lt, 1)
            for i in range(NT):
                ins = pe.transpose(PB[3][:, i * 32:i * 32 + 20], RLT[:, i * P:(i + 1) * P], IDENT[0:20, 0:20])
            ins.then_inc(r_mm, 1)
            pe.wait_ge(r_oh, 1)
            chosen = OH[:, 2, :, :].rearrange("p a b -> p (a b)")
            pe.matmul(PB[1][:, 0:NT * EXPERTS], TRI, chosen, start=True, stop=True)
            ins = pe.matmul(PB[2][:, 0:NT * EXPERTS], ONES[:, 0:P], chosen, start=True, stop=True)
            ins.then_inc(r_rank, 1)
            meet(pe, "pe")

            def rows_T(E, e, before):
                pe.wait_ge(xs_in[e % 2], (before + 1) * 16)
                for d in range(ND):
                    ins = pe.transpose(PB[d // 4][:, (d % 4) * P:(d % 4 + 1) * P], XS[e % 2][:, d * P:(d + 1) * P], IDENT[:, :])
                ins.then_inc(x_tp, 1)

            def gate_up(E, e, weights, starts):
                pe.wait_ge(x_ht, (E + 1) * 2)
                pe.wait_ge(act_done, E + 1)
                for m in range(4):
                    w = weights(m)
                    for k in range(KK):
                        ins = pe.matmul(PB[2 + m // 2][:, :], XST[e % 2][:, (m % 2) * KK + k, :], w[:, k, :],
                                        start=(m % 2 == 0 and k == 0), stop=(m % 2 == 1 and k == KK - 1))
                        if k == 0 and starts:
                            begin(ins, None)
                ins.then_inc(gu_done, 1)

            def act_T(E, e):
                pe.wait_ge(act_done, E + 2)
                for d in range(4):
                    ins = pe.transpose(PB[4][:, d * P:(d + 1) * P], SG[e % 2][:, d * P:(d + 1) * P], IDENT[:, :])
                ins.then_inc(a_tp, 1)

            def down(E, e, weights, starts):
                pe.wait_ge(a_ht, E + 1)
                pe.wait_ge(y_ev, E + 1)
                for m in range(2):
                    w = weights(m)
                    for k in range(KK):
                        ins = pe.matmul(PB[5 + m][:, :], ACTT[e % 2][:, k, :], w[:, k, :], start=(k == 0), stop=(k == KK - 1))
                        if k == 0 and starts:
                            begin(ins, None)
                ins.then_inc(down_done, 1)

            rows_T(0, 0, 0)
            with pe.Fori(0, EXPERTS // 4) as it:
                def ring(at):
                    def chunk(m):
                        await_chunk(CH["moe"] + at + m, it, 24)
                        return slot(CH["moe"] + at + m)
                    return chunk
                for e in range(4):
                    gate_up(it * 4 + e, e, ring(GU_AT[e]), True)
                    for n, d in enumerate(DOWN_AFTER[e]):
                        act_T(it * 4 + d, d)
                        if n == 0:
                            rows_T(it * 4 + e + 1, e + 1, it * 2 + (e + 1) // 2)
                        down(it * 4 + d, d, ring(DN_AT[d]), True)
                    if e == 0:
                        rows_T(it * 4 + 1, 1, it * 2)
            n_spare = pe.value_load(TAB[0:1, 7:8], min_val=0, max_val=SPARE)
            with pe.Fori(0, SPARE) as t:
                with pe.If(t < n_spare):
                    E = t + EXPERTS
                    pe.wait_ge(spare_in, (t + 1) * 96)
                    gate_up(E, 0, lambda m: SPW[:, m], False)
                    rows_T(E + 1, 0, t + EXPERTS // 2 + 1)
                    act_T(E, 0)
                    down(E, 0, lambda m: SPW[:, 4 + m], False)
            meet(pe, "pe")

            rows_to_T()
            for m in range(5):
                split_group(GR["ain"] + m, "ain", 4 * m, "T", wait_norm=NORM_LOW["ain"] if m == 0 else None)
            g = GR["ain"] + 5
            await_set(g)
            for i in range(NT):
                for k in range(ND):
                    for n, x in enumerate((HTH, HTL)):
                        ins = pe.matmul(PB[4][:, i * 32:(i + 1) * 32], x[:, k, i * P:(i + 1) * P].bitcast(F32),
                                        SW[:, k, SW_KR:SW_KR + 32], start=(k == 0 and n == 0), stop=(k == ND - 1 and n == 1))
            ins.then_inc(acc_done, 1)
            pe.wait_ge(acc_free[0], (g + 1) // 2)
            sq = SQ[:, :, :].rearrange("p a (c b) -> p (a c) b", c=2)
            pe.wait_ge(l_sq, 1)
            for k in range(6):
                ins = pe.matmul(PB[0][:, :], ONES[:, 0:P], sq[:, k, :], start=(k == 0), stop=(k == 5))
            ins.then_inc(l_sum, 1)
            pe.wait_ge(l_sq, 2)
            for k in range(2):
                ins = pe.matmul(PB[1][:, :], ONES[:, 0:P], sq[:, 6 + k, :], start=(k == 0), stop=(k == 1))
            ins.then_inc(l_sum, 1)
            g, c = GR["qup"], CH["qup"]
            await_set(g)
            pe.wait_ge(l_c, 1)
            parts = [(slot(c), 0, 4), (slot(c + 1, 2), 4, 2)]
            for m, (w, k0, kk) in enumerate(parts):
                await_chunk(c + m)
                for b in range(NT):
                    for k in range(kk):
                        ins = pe.matmul(PB[b][:, :], CQ[:, k0 + k, b * P:(b + 1) * P], w[:, k, :],
                                        start=(m == 0 and k == 0), stop=(m == 1 and k == kk - 1))
                        if b == 0 and k == 0:
                            begin(ins, c + m)
            ins.then_inc(acc_done, 1)
            await_set(g + 1)
            await_chunk(c + 2)
            w = slot(c + 2, 6, 256)
            for b in range(NT):
                for k in range(6):
                    ins = pe.matmul(PB[4 + b][:, 0:256], CQ[:, k, b * P:(b + 1) * P], w[:, k, :], start=(k == 0), stop=(k == 5))
                    if b == 0 and k == 0:
                        begin(ins, c + 2)
            ins.then_inc(acc_done, 1)
            g, c = GR["kvup"], CH["kvup"]
            await_chunk(c)
            w = slot(c, 2, 1024)
            for m in range(2):
                await_set(g + m)
                for b in range(NT):
                    for k in range(2):
                        ins = pe.matmul(PB[4 * m + b][:, :], CKV[:, k, b * P:(b + 1) * P], w[:, k, m * W:(m + 1) * W],
                                        start=(k == 0), stop=(k == 1))
                        if m == 0 and b == 0 and k == 0:
                            begin(ins, c)
                ins.then_inc(acc_done, 1)
            for m in range(2):
                pe.wait_ge(m_qn if m == 0 else m_kn, 1 if m == 0 else 1 + NT)
                for h in range(MLA_H):
                    if m == 0 and h in (0, 4):
                        pe.wait_ge(acc_free[h // 4], (GR["kvup"] + h // 4) // 2 + 1)
                    if m == 1:
                        pe.wait_ge(m_ht, MLA_H)
                    for i in range(NT):
                        src = QN[:, i, h * QK_D:(h + 1) * QK_D] if m == 0 else KN[:, i, h, :]
                        ins = pe.transpose(PB[h][0:QK_D, i * P:(i + 1) * P], src, IDENT[:, :])
                    ins.then_inc(m_tp, 1)
            meet(pe, "pe")
            attention("mla", lambda it, h, i, b, nk: [(QS[0:QK_D, h, i * P:(i + 1) * P],
                                                       KM[0:QK_D, bass.ds(it * 2 + h, 1), 0:nk].rearrange("p a b -> p (a b)"))],
                      lambda it, h, b, j, n: KVN[:, j, bass.ds((it * 2 + h) * P + NOPE, DH)],
                      lambda it, h: pe.wait_ge(heads_in, it + NH1 + 1) if h == 0 else None)
            meet(pe, "pe")
            heads_T(4)
            pe.wait_ge(o_ht, ND + 4)
            for half in range(2):
                split_group(GR["aout"] + half, "aout", 4 * half, "D")

            def mlp(layer):
                rows_to_T()
                pe.wait_ge(norm_low, NORM_LOW[f"up{layer}"])
                with pe.Fori(0, 2) as it:
                    for m in range(4):
                        split_group(GR[f"up{layer}"] + m, f"up{layer}", 4 * m, "T", turn=it, groups_a_turn=4, parts_a_turn=16)
                meet(pe, "pe")
                for half in range(2):
                    split_group(GR[f"down{layer}"] + half, f"down{layer}", 16 * half, "D", parts=16)

            mlp(0)

            rows_to_T()
            g = GR["cin"]
            for m in range(3):
                split_group(g + m, "cin", 4 * m, "T", wait_norm=NORM_LOW["cin"] if m == 0 else None)
            for m in range(3, 5):
                await_set(g + m)
                bank = 4 * ((g + m) % 2)
                for n in range(4):
                    q = 4 * m + n
                    pe.wait_ge(low_ready, part_no("cin", q) + 1)
                    w = (WH[:, q % 2], WL[:, q % 2])
                    wv = tuple(t[:, :, 256:512] for t in w)
                    for b in range(2 + NT):
                        for k in range(2):
                            kk, ends = 2 * n + k, (n == 0 and k == 0, n == 3 and k == 1)
                            if b < 2:
                                mms = three(PB[bank + b][:, :], w, k, (HTH, HTL), kk, "T", slice(b * P, (b + 1) * P), *ends)
                            else:
                                i = b - 2
                                ends = (ends[0] and i % 2 == 0, ends[1] and i % 2 == 1)
                                mms = three(PB[bank + 2 + i // 2][:, (i % 2) * 256:(i % 2) * 256 + 256], wv, k, (HTH, HTL),
                                            kk, "N", slice(i * P, (i + 1) * P), *ends)
                            for x, ins in enumerate(mms):
                                if b == 0 and k == 0 and x == 0:
                                    ins.then_inc(part_begun, 1)
                                if b == 0 and k == 0 and x == 1 and q % 2 == 0:
                                    begin(ins, None)
                ins.then_inc(acc_done, 1)
            await_set(g + 5)
            bank = 4 * ((g + 5) % 2)
            for i in range(NT):
                for k in range(ND):
                    for n, x in enumerate((HTH, HTL)):
                        ins = pe.matmul(PB[bank][:, i * 48:(i + 1) * 48], x[:, k, i * P:(i + 1) * P].bitcast(F32),
                                        SW[:, k, SW_GT:SW_GT + 48], start=(k == 0 and n == 0), stop=(k == ND - 1 and n == 1))
            ins.then_inc(acc_done, 1)
            pe.wait_ge(aux_in, AUX["cmp"])
            for s in range(2):
                pe.wait_ge(acc_free[s], (g + 4 + s) // 2 + 1)
            for m in range(2):
                ins = pe.transpose(PB[6][0:DH, m * CMP_LEN:(m + 1) * CMP_LEN], PER[:, m, :], IDENT[0:CMP_LEN, 0:CMP_LEN])
            ins.then_inc(c_mm, 1)
            pe.wait_ge(c_dve, 1)
            for m in range(2):
                for l in range(CMP_LEN):
                    ins = pe.matmul(PB[4 + m][0:DH, 0:1], CW[m][0:DH, l, :], PET[:, m, l:l + 1], start=(l == 0), stop=(l == CMP_LEN - 1))
            ins.then_inc(c_mm, 1)
            for m in range(2):
                for par in range(2):
                    half = slice(par * DH, (par + 1) * DH)
                    for l in range(CMP_LEN):
                        z = ZT[m][half, :, l:l + CMP_STRIDE * (NCMP - 1) + 1:CMP_STRIDE]
                        dst = PB[2 * m + par][0:DH, 0:2 * NCMP].rearrange("p (a b) -> p a b", a=2)
                        ins = pe.matmul(dst, CW[m][half, l, :], z, start=(l == 0), stop=(l == CMP_LEN - 1))
                    ins.then_inc(c_mm, 1)
            pe.wait_ge(c_act, 4)
            pe.matmul(PB[7][0:DH, 0:4 * NCMP], CW2[:, 0, :], HD[:, 0, :, :].rearrange("p a b -> p (a b)"),
                      start=True, stop=True).then_inc(c_mm, 1)
            for q in range(4):
                ins = pe.matmul(PB[6][0:NCMP, q * DH:(q + 1) * DH], HD[:, 1, q, :], CW2[:, 1, :], start=True, stop=True)
            ins.then_inc(c_mm, 1)
            meet(pe, "pe")
            meet(pe, "pe")

            def nsa_products(it, h, i, b, nk):
                q = QST[h][:, i * P:(i + 1) * P]
                if b == 0:
                    return [(q, one_of(keys_, it, NCMP + 1)) for keys_ in (KCH, KCL)]
                return [(q, one_of(keys_, it * 2 + b - 1, nk)) for keys_ in (KGH, KGL)]

            def one_of(v, n, width):
                return v[:, bass.ds(n, 1), 0:width].rearrange("p a b -> p (a b)")

            def nsa_v(it, h, b, j, n):
                if b == 0:
                    return VCS[:, 0, :]
                return VG[b - 1][:, j, bass.ds(it * DH, DH)]

            attention("nsa", nsa_products, nsa_v, lambda it, h: pe.wait_ge(q_ready, it * NSA_R + h + 1))
            meet(pe, "pe")
            heads_T(ND)
            pe.wait_ge(o_ht, 2 * ND + 4)
            for half in range(2):
                split_group(GR["cout"] + half, "cout", 4 * half, "D")
            mlp(1)

        @blk.vector
        def _(dve):
            chain = [0]

            def link(ins):
                ins.then_inc(dve_chain, 1)
                chain[0] += 1
                dve.wait_ge(dve_chain, chain[0])

            V = nc.vector
            for s in (scored, normed, ev[0], ev[1]):
                dve.sem_inc(s, AHEAD)
            for s in (acc_free[0], acc_free[1], act_done):
                dve.sem_inc(s, 1)
            V.memset(ONES[:, :], 1.0)
            dve.wait_ge(loaded, 16 * NFIRST)
            V.tensor_copy(IDB[:, :], IDENT[:, :])
            dve.wait_ge(vec_t, 1)
            V.tensor_copy(COLS[:, :], PB[7][:, 0:NVEC]).then_inc(cols, 1)
            with dve.Fori(0, 3) as it:
                for g in range(4):
                    dve.wait_ge(acc_done, GR["mod"] + g + 1 + it * 4)
                    at_ = bass.ds(it * (4 * W) + g * W, W)
                    V.tensor_tensor(MODR[:, at_], PB[4 * (g % 2)][0:1, :], ADAB[:, at_], ALU.add).then_inc(acc_free[g % 2], 1)
            dve.wait_ge(loaded_rest, 16 * NREST)
            V.tensor_copy(SMB[:, :], TMPB)
            V.tensor_copy(CMB[:, :], BIG[:, 12 * D + 3 * P:12 * D + 4 * P])
            dve.wait_ge(vec_t, 2)
            link(V.tensor_copy(MCOLS[:, :], PB[6][:, 0:48]))
            for k in range(2):
                norm = VEC_AT[f"norm{k + 1}_g"]
                V.scalar_tensor_tensor(out=GS[:, k, :], in0=MCOLS[:, 24 * k + 8:24 * k + 16], scalar=1.0,
                                       in1=COLS[:, norm:norm + 8], op0=ALU.add, op1=ALU.mult)
            meet(dve, "dve")

            def stats():
                k = norm_no["dve"]
                norm_no["dve"] += 1
                dve.wait_ge(n_sq, NT * (k + 1))
                V.tensor_scalar(MS, SS, 1.0 / D, EPS, ALU.mult, ALU.add).then_inc(n_ms, 1)
                dve.wait_ge(n_rms, k + 1)
                V.reciprocal(RSTD, RMS).then_inc(n_rstd, 1)
                dve.wait_ge(n_rstd, k + 1)

            tps = [0]

            def split(stage, q, n, turn, parts_a_turn, chunks_a_turn):
                dve.wait_ge(high_ready, part_no(stage, q, turn, parts_a_turn) + 1)
                ins = V.tensor_tensor(WL[:, q % 2], halves_of(n, q), WH[:, q % 2].bitcast(F32), ALU.subtract)
                if stage in INPUTS:
                    rows = slice(2 * (q % 2), 2 * (q % 2) + 2)
                    ins = V.tensor_tensor(HTL[:, rows, :], INPUTS[stage](q), HTH[:, rows, :].bitcast(F32), ALU.subtract)
                ins.then_inc(low_ready, 1)

            def normed_T(gain, shift, split=True):
                stats()
                for i in range(NT):
                    V.tensor_scalar(NAT[:, i, :], X[:, i, :], RSTD[:, i:i + 1], None, ALU.mult).then_inc(n_xn, 1)
                for d in range(1, ND, 2):
                    dve.wait_ge(n_tp, tps[0] + d + 1)
                    for dst in (EXACT[d], HTH[:, d, :]) if split else (HT[:, d, :],):
                        if shift is None:
                            ins = V.tensor_scalar(dst, PB[d][:, :], gain[:, d:d + 1], None, ALU.mult)
                        else:
                            ins = V.tensor_scalar(dst, PB[d][:, :], gain[:, d:d + 1], shift[:, d:d + 1], ALU.mult, ALU.add)
                    ins.then_inc(norm_high[1] if split else n_ht[1], 1)
                tps[0] += ND

            def evac(g, dst, banks=4, width=T, scale=None):
                dve.wait_ge(acc_done, g + 1)
                for b in range(banks):
                    if scale is None:
                        ins = V.tensor_copy(dst(b), PB[4 + b][:, 0:width])
                    else:
                        ins = V.tensor_scalar(dst(b), PB[4 + b][:, 0:width], scale, None, ALU.mult)
                ins.then_inc(acc_free[1], 1)

            def attention(kind, bias, dst):
                u0, turns, heads, branches = ATT[kind]
                us = units(kind)
                U, lag = len(us), LAG_T[kind]
                with dve.Fori(0, turns) as it:
                    n0 = AHEAD + u0 + it * U
                    per_unit = 2 if kind == "nsa" else 1
                    for s in range(U + lag + 1):
                        if kind != "sb" and lag <= s < U + lag:
                            u, h, i, b = us[s - lag]
                            done = RECIP0[kind] + it * (per_unit * U) + per_unit * u
                            r, s_ = RINV[:, u % 4:u % 4 + 1], GSC[:, u % 4:u % 4 + 1]
                            dve.wait_ge(exped, n0 + u + 1)
                            V.reciprocal(r, RSUM[:, u % 4:u % 4 + 1]).then_inc(recip, 1)
                        if s < U:
                            u, h, i, b = us[s]
                            nk, sc, ps = keys(i, kind, b), SCORE[:, u % 4, :], PB[u % 4]
                            if kind == "sb":
                                dve.wait_ge(sb_beta, it * U + u + 1)
                                rev = QS[:, u % 2, 0:nk][:, ::-1]
                                V.tensor_tensor_scan(rev, rev, ONES[:, 0:nk], 1.0, ALU.mult, ALU.mult).then_inc(sb_scan, 1)
                                dve.wait_ge(sb_scan, it * U + u + 1)
                                V.tensor_tensor(sc[:, 0:nk - 1], sc[:, 0:nk - 1], QS[:, u % 2, 1:nk], ALU.mult).then_inc(scored, 1)
                            else:
                                if kind == "nsa" and u % (U // heads) == 0:
                                    dve.wait_ge(nsa_bias, it * NSA_R + h + 1)
                                if kind == "fox" and u % 8 == 0:
                                    dve.wait_ge(sums_in, it * 2 + h // 2 + 1)
                                dve.wait_ge(qk, n0 + u + 1)
                                wait_apart(dve, tp, n0 + u - 3)
                                V.tensor_tensor_reduce(out=sc[:, 0:nk], in0=ps[:, 0:nk], in1=bias(it, h, i, b, nk), scale=-1.0,
                                                       scalar=BIGNUM, op0=ALU.add, op1=ALU.min,
                                                       accum_out=NM[:, u % 4:u % 4 + 1]).then_inc(scored, 1)
                        if kind == "nsa" and lag <= s < U + lag:
                            u, h, i, b = us[s - lag]
                            dve.wait_ge(recip, done + 1)
                            gate = GATE[:, i, bass.ds(it * NSA_R + (b * NSA_H + h), 1)]
                            V.tensor_tensor(s_, r, gate, ALU.mult).then_inc(recip, 1)
                        if lag <= s < U + lag:
                            u, h, i, b = us[s - lag]
                            if i not in BY_SCALAR[kind]:
                                move_probs(dve, V.tensor_copy, kind, n0, it, U, u, i, b)
                        if s > lag:
                            u, h, i, b = us[s - lag - 1]
                            o = dst(it, h, i)
                            if kind == "sb":
                                dve.wait_ge(pv, n0 + u + 1)
                                V.tensor_copy(o, PB[6 + u % 2][:, 0:DH]).then_inc(normed, 1)
                                continue
                            done = RECIP0[kind] + it * (per_unit * U) + per_unit * (u + 1)
                            dve.wait_ge(recip, done)
                            dve.wait_ge(pv, n0 + u + 1)
                            scale = (GSC if kind == "nsa" else RINV)[:, u % 4:u % 4 + 1]
                            if b == 0:
                                V.tensor_scalar(o, PB[6 + u % 2][:, 0:DH], scale, None, ALU.mult).then_inc(normed, 1)
                            else:
                                dve.wait_ge(normed, n0 + u)
                                V.scalar_tensor_tensor(out=o, in0=PB[6 + u % 2][:, 0:DH], scalar=scale, in1=o,
                                                       op0=ALU.mult, op1=ALU.add).then_inc(normed, 1)

            def heads_T(base, dst, count):
                for d in range(1, count, 2):
                    dve.wait_ge(o_tp, base + d + 1)
                    V.tensor_copy(dst[:, d, :], PB[d][:, :]).then_inc(o_ht, 1)

            normed_T(GS[:, 0, :], MCOLS[:, 0:8])
            g = GR["qkv"]
            upto = splitter(split, "qkv", chunk_list("qkv", 12))
            upto(10)
            evac(g + 1, lambda b: KA[:, b, :])
            upto(18)
            evac(g + 3, lambda b: QB[:, b, :], scale=DH ** -0.5)
            upto(24)
            dve.wait_ge(fw_high, 1)
            V.tensor_tensor(FWL, SW[:, :, SW_FA:SW_FA + NH1], FWH.bitcast(F32), ALU.subtract).then_inc(fw_low, 1)
            evac(g + 5, lambda b: VB[:, b, :])
            meet(dve, "dve")
            dve.wait_ge(fg_mm, 1)
            V.tensor_scalar(FY, PB[0][0:NH1, :], BF[:, 0:1], None, ALU.add).then_inc(fg_dve, 1)
            dve.wait_ge(fg_dve, 1)
            link(V.tensor_scalar(FN, FY, -1.0, 0.0, ALU.mult, ALU.max))
            dve.wait_ge(fg_act, 1)
            link(V.tensor_tensor(FN, FN, FA, ALU.add))
            V.tensor_tensor_scan(FG, ONES[0:NH1, :], FN, 0.0, ALU.mult, ALU.add).then_inc(fg_dve, 1)
            for h in range(1, NH1, 2):
                dve.wait_ge(fg_mm, h + 2)
                V.tensor_copy(GB[:, h, :], PB[h][:, :])
            meet(dve, "dve")

            attention("fox", lambda it, h, i, b, nk: GBS[:, h, 0:nk],
                      lambda it, h, i: NAT[:, i, bass.ds((it * 4 + h) * DH, DH)])
            meet(dve, "dve")
            attention("sb", None, lambda it, h, i: NAT[:, i, bass.ds((it * 4 + h) * DH + 512, DH)])
            meet(dve, "dve")
            heads_T(0, OT, ND)
            meet(dve, "dve")
            g = GR["gates"]
            upto = splitter(split, "gates", GATE_CHUNKS)
            for half in range(2):
                for m in range(2):
                    upto(8 * half + 4 * m + 5)
                    n = g + 4 * half + 2 * m
                    dve.wait_ge(acc_free[0], n // 2 + 1)
                    dve.wait_ge(acc_done, n + 2)
                    for b in range(4):
                        dst = MT[:, 4 * half + b, :]
                        if m == 0:
                            ins = V.tensor_tensor(dst, PB[4 + b][:, :], SIG[:, b, :], ALU.mult)
                        else:
                            ins = V.tensor_tensor(SIG[:, 4 + b, :], PB[4 + b][:, :], SIG[:, 4 + b, :], ALU.mult)
                    ins.then_inc(acc_free[1], 1)
                    if m == 1:
                        dve.wait_ge(acc_free[1], (n + 1) // 2 + 1)
                        for b in range(4):
                            dst = MT[:, 4 * half + b, :]
                            ins = V.tensor_tensor(dst, dst, SIG[:, 4 + b, :], ALU.add)
                        ins.then_inc(half_merged, 1)
            meet(dve, "dve")
            dve.wait_ge(row_in, ROW_NO["gate1"])
            upto = splitter(split, "wout", chunk_list("wout", 4))
            for half in range(2):
                upto(6 + 2 * half)
                g = GR["wout"] + half
                dve.wait_ge(acc_done, g + 1)
                at_ = slice(half * W, (half + 1) * W)
                for b in range(NT):
                    ins = V.tensor_tensor(SCORE[:, b, :], PB[4 * half + b][:, :], ROW[:, at_], ALU.mult)
                ins.then_inc(acc_free[half], 1)
                dve.wait_ge(acc_free[half], g // 2 + 1)
                for b in range(NT):
                    link(V.tensor_tensor(X[:, b, at_], X[:, b, at_], SCORE[:, b, :], ALU.add))
            meet(dve, "dve")

            normed_T(GS[:, 1, :], MCOLS[:, 24:32], split=False)
            dve.wait_ge(aux_in, AUX["router"])
            dve.wait_ge(r_mm, 1)
            V.tensor_copy(RLT, PB[0][0:20, :]).then_inc(r_lt, 1)
            dve.wait_ge(r_mm, 2)
            link(V.tensor_tensor(RL, PB[3][:, 0:NT * 32].rearrange("p (a b) -> p a b", a=NT)[:, :, 0:20],
                                 RBIAS.unsqueeze(1).broadcast_to([P, NT, 20]), ALU.add))

            def on4(v):
                return v.unsqueeze(2).broadcast_to([P, NT, 4])

            def pick(vals, diff, key, top, onehot):
                link(V.tensor_reduce(top[:, :, 0], vals, AX.X, ALU.max))
                link(V.tensor_tensor(diff, vals, on4(top[:, :, 0]), ALU.subtract))
                link(V.tensor_scalar(key, diff, 0.0, None, ALU.is_equal))
                link(V.tensor_tensor(key, key, FIRSTK.unsqueeze(1).broadcast_to([P, NT, 4]), ALU.mult))
                link(V.tensor_reduce(top[:, :, 1], key, AX.X, ALU.max))
                link(V.tensor_tensor(onehot, key, on4(top[:, :, 1]), ALU.is_equal))

            GD, GE, KEY, TOP, OHG, ES, OH1, OH2, D2, P2, ES2, TOP2 = (RG[:, m] for m in range(12))
            pick(RL[:, :, 0:4], GD, KEY, TOP, OHG)
            prod = RP.rearrange("p t (g j) -> p t g j", g=GROUPS)
            link(V.tensor_tensor(prod, RL[:, :, 4:20].rearrange("p t (g j) -> p t g j", g=GROUPS),
                                 OHG.unsqueeze(3).broadcast_to([P, NT, GROUPS, PER_GROUP]), ALU.mult))
            link(V.tensor_reduce(ES, prod.rearrange("p t g j -> p t j g"), AX.X, ALU.add))
            pick(ES, D2, KEY, TOP, OH1)
            link(V.scalar_tensor_tensor(out=ES2, in0=OH1, scalar=MASKED, in1=ES, op0=ALU.mult, op1=ALU.add))
            pick(ES2, D2, KEY, TOP2, OH2)
            V.tensor_tensor(D2[:, :, 0], TOP2[:, :, 0], TOP[:, :, 0], ALU.subtract).then_inc(r_exp_in, 1)
            for m, oh in ((0, OH1), (1, OH2)):
                link(V.tensor_tensor(OH[:, m].rearrange("p t (g j) -> p t g j", g=GROUPS),
                                     OHG.unsqueeze(3).broadcast_to([P, NT, GROUPS, PER_GROUP]),
                                     oh.unsqueeze(2).broadcast_to([P, NT, GROUPS, PER_GROUP]), ALU.mult))
            V.tensor_tensor(OH[:, 2], OH[:, 0], OH[:, 1], ALU.add).then_inc(r_oh, 1)
            dve.wait_ge(r_exp, 1)
            link(V.tensor_reduce(KEY[:, :, 0], GE, AX.X, ALU.add))
            link(V.scalar_tensor_tensor(out=KEY[:, :, 1], in0=P2[:, :, 0], scalar=1.0, in1=KEY[:, :, 0], op0=ALU.add, op1=ALU.mult))
            link(V.reciprocal(MW[:, 0, :], KEY[:, :, 1]))
            link(V.tensor_tensor(MW[:, 1, :], MW[:, 0, :], P2[:, :, 0], ALU.mult))
            dve.wait_ge(r_rank, 1)
            R, TE, CS, SH = (RS[:, m] for m in range(4))
            link(V.tensor_copy(R.rearrange("p t e -> p (t e)"), PB[1][:, 0:NT * EXPERTS]))
            counts = PB[2][:, 0:NT * EXPERTS].rearrange("p (a b) -> p a b", a=NT)
            for m in range(1, NT):
                link(V.tensor_tensor(R[:, m:NT, :], R[:, m:NT, :], counts[:, 0:NT - m, :], ALU.add))
            n_e = RP[:, 0, :]
            link(V.tensor_reduce(n_e, counts.rearrange("p t e -> p e t"), AX.X, ALU.add))
            te, cs, sh = TE[:, 0, :], CS[:, 0, :], SH[:, 0, :]
            link(V.tensor_scalar(te, n_e, float(P), None, ALU.is_gt))
            for m in (2, 3):
                link(V.scalar_tensor_tensor(out=te, in0=n_e, scalar=float(m * P), in1=te, op0=ALU.is_gt, op1=ALU.add))
            link(V.tensor_tensor_scan(cs, ONES[:, 0:EXPERTS], te, 0.0, ALU.mult, ALU.add))
            link(V.tensor_tensor(sh, cs, te, ALU.subtract))
            link(V.tensor_scalar(sh, sh, float(P), float(EXPERTS * P - P), ALU.mult, ALU.add))
            link(V.tensor_tensor(sh, sh, BASE, ALU.subtract))
            on_tiles = lambda v: v.unsqueeze(1).broadcast_to([P, NT, EXPERTS])
            for i in range(NT):
                link(V.scalar_tensor_tensor(out=RP[:, i], in0=R[:, i], scalar=float(P), in1=sh, op0=ALU.is_ge, op1=ALU.mult))
            link(V.tensor_tensor(R, R, RP, ALU.add))
            link(V.tensor_tensor(R, R, on_tiles(BASE), ALU.add))
            for m in range(2):
                link(V.tensor_tensor(OH[:, m], OH[:, m], R, ALU.mult))
                link(V.tensor_reduce(KEY[:, :, m], OH[:, m], AX.X, ALU.add))
                link(V.tensor_copy(IDX[:, m * NT:(m + 1) * NT], KEY[:, :, m]))
            spk = SPK.rearrange("p (g e) -> p g e", e=EXPERTS)
            link(V.tensor_tensor(spk, spk, CS[0:1, 0, :].unsqueeze(1).broadcast_to([1, 8, EXPERTS]), ALU.is_ge))
            link(V.tensor_reduce(TE[0:1, 1, 0:8], spk, AX.X, ALU.add))
            link(V.tensor_scalar(TE[0:1, 1, 0:7], TE[0:1, 1, 0:7], float(EXPERTS - 1), None, ALU.min))
            link(V.tensor_copy(TE[0:1, 1, 7:8], CS[0:1, 0, EXPERTS - 1:EXPERTS]))
            V.tensor_copy(TAB[:, :], TE[0:1, 1, 0:8]).then_inc(routed, 1)
            meet(dve, "dve")

            def rows_T(E, e):
                dve.wait_ge(x_tp, AHEAD + E + 1)
                for d in range(4):
                    ins = V.tensor_scalar(XST[e % 2][:, 4 + d, :], PB[1][:, d * P:(d + 1) * P], GS[:, 1, 4 + d:5 + d],
                                          MCOLS[:, 28 + d:29 + d], ALU.mult, ALU.add)
                ins.then_inc(x_ht, 1)

            def product(E, e):
                dve.wait_ge(silu_done, E + 1)
                V.tensor_tensor(SG[e % 2], SG[e % 2], PB[3][:, :], ALU.mult).then_inc(act_done, 1)

            def product_T(E, e):
                dve.wait_ge(a_tp, E + 1)
                V.tensor_copy(ACTT[e % 2].rearrange("p a b -> p (a b)"), PB[4][:, :]).then_inc(a_ht, 1)

            rows_T(0, 0)
            with dve.Fori(0, EXPERTS // 4) as it:
                for e in range(4):
                    product(it * 4 + e, e)
                    if e == 0:
                        rows_T(it * 4 + 1, 1)
                    for n, d in enumerate(DOWN_AFTER[e]):
                        product_T(it * 4 + d, d)
                        if n == 0:
                            rows_T(it * 4 + e + 1, e + 1)
            n_spare = dve.value_load(TAB[0:1, 7:8], min_val=0, max_val=SPARE)
            with dve.Fori(0, SPARE) as t:
                with dve.If(t < n_spare):
                    E = t + EXPERTS
                    product(E, 0)
                    rows_T(E + 1, 0)
                    product_T(E, 0)
            meet(dve, "dve")
            dve.wait_ge(row_in, ROW_NO["gate2"])
            for i in range(NT):
                dve.wait_ge(gathered[i], 32)
                y1, y2 = YG[:, i, :], YG[:, NT + i, :]
                link(V.tensor_scalar(y1, y1, MW[:, 0, i:i + 1], None, ALU.mult))
                link(V.scalar_tensor_tensor(out=y1, in0=y2, scalar=MW[:, 1, i:i + 1], in1=y1, op0=ALU.mult, op1=ALU.add))
                link(V.tensor_tensor(y1, y1, ROW[:, :], ALU.mult))
                V.tensor_tensor(X[:, i, :], X[:, i, :], y1, ALU.add).then_inc(x_rows, 1)
            stats()
            dve.wait_ge(final_row_in, 16)
            for i in range(NT):
                V.scalar_tensor_tensor(out=X[:, i, :], in0=X[:, i, :], scalar=RSTD[:, i:i + 1], in1=FINAL_ROW,
                                       op0=ALU.mult, op1=ALU.mult).then_inc(x_rows, 1)

            normed_T(COLS[:, VEC_AT["norm_mix_pre_2"]:VEC_AT["norm_mix_pre_2"] + 8], None)
            g = GR["ain"]
            upto = splitter(split, "ain", chunk_list("ain", 10))
            upto(10)
            evac(g + 1, lambda b: GCT[:, b, :])
            upto(18)
            evac(g + 3, lambda b: CQ[:, b, :])
            upto(20)
            evac(g + 5, lambda b: KRN.rearrange("p a b -> p (a b)"), banks=1, width=NT * 32)
            for m, rank in enumerate((Q_RANK, KV_RANK)):
                dve.wait_ge(l_sum, m + 1)
                V.tensor_scalar(RT[:, m, :], PB[m][:, :], 1.0 / rank, EPS, ALU.mult, ALU.add).then_inc(l_ms, 1)
            for m, (v, name, tiles) in enumerate(((CQ, "a_q_norm_2", 6), (CKV, "a_kv_norm_2", 2))):
                dve.wait_ge(l_rms, m + 1)
                link(V.reciprocal(RT[:, m, :], RT[:, m, :]))
                for k in range(tiles):
                    at_ = VEC_AT[name] + k
                    ins = V.scalar_tensor_tensor(out=v[:, k, :], in0=v[:, k, :], scalar=COLS[:, at_:at_ + 1], in1=RT[:, m, :],
                                                 op0=ALU.mult, op1=ALU.mult)
            ins.then_inc(l_c, 1)

            def rope(v, heads, out_):
                shape = [P, NT, heads, 16] if heads else [P, NT, 16]
                wide = (lambda t: t[:, :, :].unsqueeze(2).broadcast_to(shape)) if heads else (lambda t: t[:, :, :])
                n = NT * max(heads, 1) * 16
                tmp = [RT[:, m, 0:n].rearrange("p (a h b) -> p a h b", a=NT, h=heads) if heads
                       else RT[:, m, 0:n].rearrange("p (a b) -> p a b", a=NT) for m in range(3)]
                x1 = v[:, :, :, NOPE:NOPE + 16] if heads else v[:, :, 0:16]
                x2 = v[:, :, :, NOPE + 16:QK_D] if heads else v[:, :, 16:32]
                o1 = x1 if heads else out_[:, :, 0:16]
                o2 = x2 if heads else out_[:, :, 16:32]
                link(V.tensor_tensor(tmp[0], x1, wide(COS), ALU.mult))
                link(V.tensor_tensor(tmp[1], x2, wide(SIN), ALU.mult))
                link(V.tensor_tensor(tmp[0], tmp[0], tmp[1], ALU.subtract))
                link(V.tensor_tensor(tmp[1], x2, wide(COS), ALU.mult))
                link(V.tensor_tensor(tmp[2], x1, wide(SIN), ALU.mult))
                link(V.tensor_copy(o1, tmp[0]))
                return V.tensor_tensor(o2, tmp[1], tmp[2], ALU.add)

            rope(KRN, 0, KR2).then_inc(m_kn, 1)
            dve.wait_ge(m_kn, 1)
            dve.wait_ge(conv_in, 1)
            for k in range(4):
                w = VEC_AT["a_conv_w_2"] + k
                y = RT[:, 0, :]
                link(V.tensor_scalar(y, GCT[:, k, :], COLS[:, w + 8:w + 9], None, ALU.mult))
                for lag in (1, 2):
                    tap = w + 4 * (2 - lag)
                    link(V.scalar_tensor_tensor(out=y[:, lag:T], in0=GCT[:, k, 0:T - lag], scalar=COLS[:, tap:tap + 1],
                                                in1=y[:, lag:T], op0=ALU.mult, op1=ALU.add))
                link(V.tensor_tensor(YC[:, k, :], GBT[:, k, :], y, ALU.mult))
            evac(GR["qup"] + 1, lambda b: QN[:, b, W:768], width=256)
            evac(GR["kvup"] + 1, lambda b: KVN[:, b, W:D])
            dve.wait_ge(acc_free[0], GR["qup"] // 2 + 1)
            rope(QN.rearrange("p t (h d) -> p t h d", h=MLA_H), MLA_H, None).then_inc(m_qn, 1)
            for m in range(2):
                for h in range(1, MLA_H, 2):
                    dve.wait_ge(m_tp, m * MLA_H + h + 1)
                    if m == 0:
                        V.tensor_scalar(QM[0:QK_D, h, :], PB[h][0:QK_D, :], QK_D ** -0.5, None, ALU.mult).then_inc(m_ht, 1)
                    else:
                        V.tensor_copy(KM[0:QK_D, h, :], PB[h][0:QK_D, :]).then_inc(m_ht, 1)
            meet(dve, "dve")
            dve.wait_ge(aux_in, AUX["caus"])
            attention("mla", lambda it, h, i, b, nk: CAUS[:, T - P - i * P:T],
                      lambda it, h, i: NAT[:, i, bass.ds((it * 2 + h) * DH, DH)])
            meet(dve, "dve")
            heads_T(8, OT2, 4)
            upto = splitter(split, "aout", chunk_list("aout", 4))
            upto(8)
            evac(GR["aout"] + 1, lambda b: MN[:, b, W:D])

            def add_normed(row):
                stats()
                dve.wait_ge(row_in, ROW_NO[row])
                for i in range(NT):
                    link(V.scalar_tensor_tensor(out=MN[:, i, :], in0=MN[:, i, :], scalar=RSTD[:, i:i + 1], in1=ROW[:, :],
                                                op0=ALU.mult, op1=ALU.mult))
                    V.tensor_tensor(X[:, i, :], X[:, i, :], MN[:, i, :], ALU.add).then_inc(x_rows, 1)

            def mlp(layer):
                add_normed(f"post{layer}")
                v = VEC_AT["norm_mlp_pre_2"] + 8 * layer
                normed_T(COLS[:, v:v + 8], None)
                g = GR[f"up{layer}"]
                with dve.Fori(0, 2) as it:
                    upto = splitter(split, f"up{layer}", chunk_list(f"up{layer}", 8), it, 16, 8)
                    for m in (1, 3):
                        upto(4 * m + 6)
                        dve.wait_ge(acc_done, g + m + 1 + it * 4)
                        for b in range(4):
                            dst = H1[:, bass.ds(it * 16 + 4 * m + b, 1), :].rearrange("p a b -> p (a b)")
                            ins = V.tensor_scalar(dst, PB[4 + b][:, :], 0.0, None, ALU.max)
                        ins.then_inc(acc_free[1], 1)
                        dve.wait_ge(acc_free[1], (g + m) // 2 + 1 + it * 2)
                        dst = H1[:, bass.ds(it * 16 + 4 * m, 4), :]
                        V.tensor_tensor(dst, dst, dst, ALU.mult)
                meet(dve, "dve")
                upto = splitter(split, f"down{layer}", chunk_list(f"down{layer}", 16))
                upto(32)
                evac(GR[f"down{layer}"] + 1, lambda b: MN[:, b, W:D])
                add_normed(f"mlppost{layer}")

            mlp(0)

            normed_T(COLS[:, VEC_AT["norm_mix_pre_2"] + 8:VEC_AT["norm_mix_pre_2"] + 16], None)
            g = GR["cin"]
            upto = splitter(split, "cin", chunk_list("cin", 10))
            upto(10)
            evac(g + 1, lambda b: Q2[:, 4 + b, :], scale=DH ** -0.5)
            upto(18)
            dve.wait_ge(acc_done, g + 4)
            for j in range(2):
                V.tensor_copy(KG[0][0:DH, 2 * j, :], PB[4 + j][0:DH, :])
                V.tensor_copy(KG[0][DH:P, 2 * j + 1, :], PB[4 + j][DH:P, :])
                ins = V.tensor_copy(VG[0][:, 2 * j:2 * j + 2, :], PB[6 + j][:, :].rearrange("p (a b) -> p a b", a=2))
            ins.then_inc(acc_free[1], 1)
            upto(20)
            evac(g + 5, lambda b: GATE[:, :, :].rearrange("p a b -> p (a b)"), banks=1, width=NT * 48)
            dve.wait_ge(c_mm, 1)
            V.tensor_copy(PET.rearrange("p a b -> p (a b)"), PB[6][0:DH, 0:2 * CMP_LEN]).then_inc(c_dve, 1)
            dve.wait_ge(c_mm, 2)
            V.tensor_copy(BC[:, 0:1], PB[4][0:DH, 0:1])
            V.tensor_copy(BC[:, 1:2], PB[5][0:DH, 0:1]).then_inc(c_dve, 1)
            dve.wait_ge(c_act, 1)
            for i in range(NT):
                V.tensor_scalar(GATE[:, i, 0:NSA_H], GATE[:, i, 0:NSA_H], HAS[:, i:i + 1], None, ALU.mult)
            V.memset(KC[0:DH, :, NCMP:NCMP + 1], 0.0)
            dve.wait_ge(c_mm, 7)
            V.tensor_copy(KC[0:DH, :, 0:NCMP].rearrange("p (b a) n -> p a b n", a=2),
                          PB[7][0:DH, 0:4 * NCMP].rearrange("p (a b n) -> p a b n", a=2, b=2)).then_inc(c_dve, 1)
            dve.wait_ge(c_mm, 8)
            V.tensor_copy(VC[:, :, :].rearrange("p (b a) n -> p a b n", a=2),
                          PB[6][0:NCMP, 0:4 * DH].rearrange("p (a b n) -> p a b n", a=2, b=2)).then_inc(c_dve, 1)
            meet(dve, "dve")
            dve.wait_ge(aux_in, AUX["dist"])
            meet(dve, "dve")

            def nsa_bias_of(it, h, i, b, nk):
                return CBIAS[:, h, i * NCMP:(i + 1) * NCMP] if b == 0 else BIAS[:, h, T - P - i * P:T]

            attention("nsa", nsa_bias_of, lambda it, h, i: NAT[:, i, bass.ds((it * NSA_R + h) * DH, DH)])
            meet(dve, "dve")
            heads_T(12, OT, ND)
            upto = splitter(split, "cout", chunk_list("cout", 4))
            upto(8)
            evac(GR["cout"] + 1, lambda b: MN[:, b, W:D])
            mlp(1)
            dve.drain()
            dve.sem_inc(stored, 1)

        @blk.sync
        def _(sp):
            sp.wait_ge(stored, 1)
            sp.dma_start(out[0].rearrange("(i p) d -> p i d", p=P), X[:, :, :]).then_inc(stored, 16)
            sp.wait_ge(stored, 17)


_INS = ["x", "c", "ada_w", "ada_b", "norm1_g", "w_in", "b_forget", "w_branch_fox", "w_branch_sb", "w_out", "norm2_g",
        "router_group_w", "router_group_b", "router_expert_w", "router_expert_b", "expert_w_gate", "expert_w_up",
        "expert_w_down", "final_g", "norm_mix_pre_2", "norm_mix_post_2", "norm_mlp_pre_2", "norm_mlp_post_2",
        "mlp_w1_2", "mlp_w2_2", "a_w_in_2", "a_conv_w_2", "a_q_norm_2", "a_w_q_up_2", "a_kv_norm_2", "a_w_kv_up_2",
        "a_w_out_2", "c_w_in_2", "c_cmp_pe_k_2", "c_cmp_w1_k_2", "c_cmp_w2_k_2", "c_cmp_pe_v_2", "c_cmp_w1_v_2",
        "c_cmp_w2_v_2", "c_w_out_2"]


def kernel(**inputs):
    import concourse.bacc as bacc
    from concourse.bass_utils import run_bass_kernel_spmd

    nc = bacc.Bacc("TRN2", target_bir_lowering=False, num_devices=1)
    arrays, aps = {}, {}
    given = {name: np.ascontiguousarray(inputs[name]) for name in _INS}
    given.update(constants())
    for name, v in given.items():
        arrays[f"in_{name}"] = v
        aps[name] = nc.dram_tensor(f"in_{name}", v.shape, mybir.dt.from_np(v.dtype), kind="ExternalInput").ap()
    out = nc.dram_tensor("out", (1, T, D), F32, kind="ExternalOutput").ap()
    program(nc, aps, out)
    r = run_bass_kernel_spmd(nc, [arrays], core_ids=[0])
    return r.results[0]["out"]
```
